# Optimizing a Trainium2 kernel written in Bass

```python
import math
import jax, jax.numpy as jnp
from jax import lax
import numpy as np

D_MODEL = 2048
BATCH = 1
SEQ = 256
DEPTH = 1

HEAD_DIM = 64
N_MIXERS = 4
GROUP_WIDTH = D_MODEL // N_MIXERS
N_HEADS = GROUP_WIDTH // HEAD_DIM
NSA_KV_HEADS = 2
NSA_GQA = N_HEADS // NSA_KV_HEADS
CMP_LEN = 32
CMP_STRIDE = 16
SLC_LEN = 64
SLC_TOP = 16
WINDOW = 512
FORCE_BONUS = 1.0e3
N_BUCKETS = 32
MAX_DISTANCE = 1024
CONV_W = 3
CHUNK = 128
Q_BLOCK = 128
D_FF = -(-8 * D_MODEL // (3 * 256)) * 256
NEG_INF = -1.0e30

A_Q_COLS = N_HEADS * HEAD_DIM
A_KV_COLS = 6 * NSA_KV_HEADS * HEAD_DIM
A_GATE_COLS = 3 * N_HEADS
B_COLS = 3 * GROUP_WIDTH
C_COLS = 2 * GROUP_WIDTH
D_COLS = 3 * GROUP_WIDTH
SPLIT_POINTS = (A_Q_COLS, A_Q_COLS + A_KV_COLS, A_Q_COLS + A_KV_COLS + A_GATE_COLS, A_Q_COLS + A_KV_COLS + A_GATE_COLS + B_COLS, A_Q_COLS + A_KV_COLS + A_GATE_COLS + B_COLS + C_COLS)
W_IN_COLS = SPLIT_POINTS[-1] + D_COLS


def rms_norm(x, g, eps=1e-6):
    xf = x.astype(jnp.float32)
    y = xf * lax.rsqrt(jnp.mean(xf * xf, axis=-1, keepdims=True) + eps)
    return (y * g.astype(jnp.float32)).astype(x.dtype)

def layer_norm_noaffine(x, eps=1e-5):
    xf = x.astype(jnp.float32)
    mu = jnp.mean(xf, axis=-1, keepdims=True)
    var = jnp.mean(jnp.square(xf - mu), axis=-1, keepdims=True)
    return ((xf - mu) * lax.rsqrt(var + eps)).astype(x.dtype)

def gelu(x):
    return jax.nn.gelu(x, approximate=True)

def rel_bucket(dist):
    n = jnp.maximum(dist, 0)
    max_exact = N_BUCKETS // 2
    nf = jnp.maximum(n, 1).astype(jnp.float32)
    large = max_exact + (jnp.log(nf / max_exact) / math.log(MAX_DISTANCE / max_exact) * (N_BUCKETS - max_exact)).astype(jnp.int32)
    large = jnp.minimum(large, N_BUCKETS - 1)
    return jnp.where(n < max_exact, n, large)

def rel_bias_heads(dist, table):
    b = table[rel_bucket(dist)].astype(jnp.float32)
    b = jnp.moveaxis(b, -1, 0)
    return b.reshape(NSA_KV_HEADS, NSA_GQA, *dist.shape)

def masked_softmax(s, mask):
    s = jnp.where(mask, s, NEG_INF)
    p = jax.nn.softmax(s, axis=-1)
    return jnp.where(mask, p, 0.0)

def cmp_slc_overlap(n_cmp, n_slc):
    c0 = np.arange(n_cmp)[:, None] * CMP_STRIDE
    s0 = np.arange(n_slc)[None, :] * SLC_LEN
    ov = np.minimum(c0 + CMP_LEN, s0 + SLC_LEN) - np.maximum(c0, s0)
    return (np.maximum(ov, 0) / CMP_LEN).astype(np.float32)

def nsa_attention(q, k_c, v_c, k_s, v_s, k_w, v_w, gates, q_gain, k_gain, cmp_pos, cmp_w1, cmp_w2, rel_table):
    B, T = q.shape[0], q.shape[1]
    G, R, Dh = NSA_KV_HEADS, NSA_GQA, HEAD_DIM
    scale = Dh ** -0.5
    q = rms_norm(q, q_gain).reshape(B, T, G, R, Dh)
    k_s = rms_norm(k_s, k_gain)
    k_w = rms_norm(k_w, k_gain)
    t_pos = jnp.arange(T, dtype=jnp.int32)

    n_cmp = (T - CMP_LEN) // CMP_STRIDE + 1
    blk = np.arange(n_cmp)[:, None] * CMP_STRIDE + np.arange(CMP_LEN)[None, :]

    def compress(z, i):
        zb = z[:, blk] + cmp_pos[i][None, None, :, None, :]
        zb = zb.transpose(0, 1, 3, 2, 4).reshape(B, n_cmp, G, CMP_LEN * Dh)
        return gelu(zb @ cmp_w1[i]) @ cmp_w2[i]

    kc = rms_norm(compress(k_c, 0), k_gain)
    vc = compress(v_c, 1)
    cmp_end = jnp.asarray(blk[:, -1], jnp.int32)
    dist_c = t_pos[:, None] - cmp_end[None, :]
    s_c = jnp.einsum('btgrd,bngd->bgrtn', q, kc).astype(jnp.float32) * scale + rel_bias_heads(dist_c, rel_table)
    p_c = masked_softmax(s_c, dist_c >= 0)
    o_cmp = jnp.einsum('bgrtn,bngd->btgrd', p_c.astype(vc.dtype), vc)

    n_slc = T // SLC_LEN
    top = min(SLC_TOP, n_slc)
    imp = jnp.einsum('bgrtn,nj->bgtj', p_c, jnp.asarray(cmp_slc_overlap(n_cmp, n_slc)))
    j_idx = jnp.arange(n_slc, dtype=jnp.int32)
    cur = t_pos // SLC_LEN
    valid = (j_idx[None, :] * SLC_LEN) <= t_pos[:, None]
    forced = (j_idx[None, :] == 0) | (j_idx[None, :] == cur[:, None]) | (j_idx[None, :] == cur[:, None] - 1)
    score = jnp.where(valid, imp + jnp.where(forced, FORCE_BONUS, 0.0), NEG_INF)
    _, sel = lax.top_k(score, top)

    ks_blk = k_s.reshape(B, n_slc, SLC_LEN, G, Dh).transpose(0, 3, 1, 2, 4)
    vs_blk = v_s.reshape(B, n_slc, SLC_LEN, G, Dh).transpose(0, 3, 1, 2, 4)
    pad = ((0, 0), (WINDOW, 0), (0, 0), (0, 0))
    kw_pad = jnp.pad(k_w, pad)
    vw_pad = jnp.pad(v_w, pad)
    table_g = rel_table.reshape(N_BUCKETS, G, R)
    g_idx = jnp.arange(G)[None, :, None, None, None]
    gather_blocks = jax.vmap(jax.vmap(lambda blocks, ix: blocks[ix]))
    win_len = WINDOW + Q_BLOCK

    def block_fn(qb):
        qs = qb * Q_BLOCK
        qt = qs + jnp.arange(Q_BLOCK, dtype=jnp.int32)
        qblk = lax.dynamic_slice_in_dim(q, qs, Q_BLOCK, axis=1)
        ix = lax.dynamic_slice_in_dim(sel, qs, Q_BLOCK, axis=2)
        ksel = gather_blocks(ks_blk, ix)
        vsel = gather_blocks(vs_blk, ix)
        kpos = ix[..., None] * SLC_LEN + jnp.arange(SLC_LEN, dtype=jnp.int32)
        d_s = qt[None, None, :, None, None] - kpos
        b_s = jnp.moveaxis(table_g[rel_bucket(d_s), g_idx].astype(jnp.float32), -1, 2)
        s_s = jnp.einsum('btgrd,bgtkld->bgrtkl', qblk, ksel).astype(jnp.float32) * scale + b_s
        shp = s_s.shape
        p_s = masked_softmax(s_s.reshape(B, G, R, Q_BLOCK, -1), (d_s >= 0).reshape(B, G, 1, Q_BLOCK, -1)).reshape(shp)
        o_s = jnp.einsum('bgrtkl,bgtkld->btgrd', p_s.astype(vsel.dtype), vsel)
        kw = lax.dynamic_slice_in_dim(kw_pad, qs, win_len, axis=1)
        vw = lax.dynamic_slice_in_dim(vw_pad, qs, win_len, axis=1)
        kp = qs - WINDOW + jnp.arange(win_len, dtype=jnp.int32)
        d_w = qt[:, None] - kp[None, :]
        m_w = (d_w >= 0) & (d_w < WINDOW) & (kp[None, :] >= 0)
        s_w = jnp.einsum('btgrd,bsgd->bgrts', qblk, kw).astype(jnp.float32) * scale + rel_bias_heads(d_w, rel_table)
        p_w = masked_softmax(s_w, m_w)
        o_w = jnp.einsum('bgrts,bsgd->btgrd', p_w.astype(vw.dtype), vw)
        return o_s, o_w

    o_slc, o_win = lax.map(block_fn, jnp.arange(T // Q_BLOCK, dtype=jnp.int32))
    o_slc = jnp.moveaxis(o_slc, 0, 1).reshape(B, T, G, R, Dh)
    o_win = jnp.moveaxis(o_win, 0, 1).reshape(B, T, G, R, Dh)

    g = jax.nn.sigmoid(gates.astype(jnp.float32)).astype(q.dtype).reshape(B, T, G, R, 3)
    o = g[..., 0:1] * o_cmp + g[..., 1:2] * o_slc + g[..., 2:3] * o_win
    return o.reshape(B, T, G * R * Dh)

def short_conv_mixer(cols, conv_w):
    b_gate, c_gate, h = jnp.split(cols, 3, axis=-1)
    z = c_gate * h
    T = z.shape[1]
    zp = jnp.pad(z, ((0, 0), (CONV_W - 1, 0), (0, 0)))
    y = conv_w[0] * zp[:, 0:T]
    for i in range(1, CONV_W):
        y = y + conv_w[i] * zp[:, i:i + T]
    return b_gate * y

def spatial_gating_mixer(cols, sgu_w, sgu_b):
    B, T = cols.shape[0], cols.shape[1]
    u, v = jnp.split(gelu(cols), 2, axis=-1)
    v = layer_norm_noaffine(v).reshape(B, T // CHUNK, CHUNK, N_HEADS, HEAD_DIM)
    w = sgu_w * jnp.asarray(np.tril(np.ones((CHUNK, CHUNK), np.float32)), sgu_w.dtype)
    s = jnp.einsum('hpq,bcqhe->bcphe', w, v) + sgu_b.T[None, None, :, :, None]
    return u * s.reshape(B, T, GROUP_WIDTH)

def stick_breaking_attention(q, k, v):
    B, T, H, Dh = q.shape
    scale = Dh ** -0.5
    outs = []
    for qb in range(T // Q_BLOCK):
        qs, qe = qb * Q_BLOCK, (qb + 1) * Q_BLOCK
        z = jnp.einsum('bthd,bshd->bhts', q[:, qs:qe], k[:, :qe]).astype(jnp.float32) * scale
        mask = jnp.asarray(np.arange(qe)[None, :] < np.arange(qs, qe)[:, None])
        log_beta = jax.nn.log_sigmoid(z)
        log_1m = jnp.where(mask, log_beta - z, 0.0)
        tail = lax.cumsum(log_1m, axis=3, reverse=True) - log_1m
        a = jnp.where(mask, jnp.exp(log_beta + tail), 0.0)
        outs.append(jnp.einsum('bhts,bshd->bthd', a.astype(v.dtype), v[:, :qe]))
    return jnp.concatenate(outs, axis=1).reshape(B, T, H * Dh)

def first_inputs(seed: int = 0) -> dict:
    key = jax.random.key(seed)
    ks = jax.random.split(key, 18)
    f32 = jnp.float32

    def nrm(k, shape, scale):
        return jax.random.normal(k, shape, f32) * scale

    res_scale = (2 * DEPTH) ** -0.5
    return {
        'x': nrm(ks[0], (BATCH, SEQ, D_MODEL), 1.0),
        'w_in': nrm(ks[1], (DEPTH, D_MODEL, W_IN_COLS), D_MODEL ** -0.5),
        'w_out': nrm(ks[2], (DEPTH, D_MODEL, D_MODEL), D_MODEL ** -0.5 * res_scale),
        'norm_mix': 1.0 + nrm(ks[3], (DEPTH, D_MODEL), 0.05),
        'norm_ffn': 1.0 + nrm(ks[4], (DEPTH, D_MODEL), 0.05),
        'q_gain': 1.0 + nrm(ks[5], (DEPTH, HEAD_DIM), 0.05),
        'k_gain': 1.0 + nrm(ks[6], (DEPTH, HEAD_DIM), 0.05),
        'cmp_pos': nrm(ks[7], (DEPTH, 2, CMP_LEN, HEAD_DIM), 0.1),
        'cmp_w1': nrm(ks[8], (DEPTH, 2, CMP_LEN * HEAD_DIM, HEAD_DIM), (CMP_LEN * HEAD_DIM) ** -0.5),
        'cmp_w2': nrm(ks[9], (DEPTH, 2, HEAD_DIM, HEAD_DIM), HEAD_DIM ** -0.5),
        'rel_table': nrm(ks[10], (N_BUCKETS, N_HEADS), 0.5),
        'conv_w': nrm(ks[11], (DEPTH, CONV_W, GROUP_WIDTH), CONV_W ** -0.5),
        'sgu_w': nrm(ks[12], (DEPTH, N_HEADS, CHUNK, CHUNK), CHUNK ** -0.5),
        'sgu_b': 1.0 + nrm(ks[13], (DEPTH, N_HEADS, CHUNK), 0.1),
        'group_gain': 1.0 + nrm(ks[14], (DEPTH, D_MODEL), 0.05),
        'w_ffn_gate': nrm(ks[15], (DEPTH, D_MODEL, D_FF), D_MODEL ** -0.5),
        'w_ffn_up': nrm(ks[16], (DEPTH, D_MODEL, D_FF), D_MODEL ** -0.5),
        'w_ffn_down': nrm(ks[17], (DEPTH, D_FF, D_MODEL), D_FF ** -0.5 * res_scale),
    }

def first_block(x, w_in, w_out, norm_mix, norm_ffn, q_gain, k_gain, cmp_pos, cmp_w1, cmp_w2, rel_table, conv_w, sgu_w, sgu_b, group_gain, w_ffn_gate, w_ffn_up, w_ffn_down):
    B, T = x.shape[0], x.shape[1]
    for l in range(DEPTH):
        h = rms_norm(x, norm_mix[l])
        proj = h @ w_in[l]
        a_q, a_kv, a_g, b_cols, c_cols, d_cols = jnp.split(proj, SPLIT_POINTS, axis=-1)
        kv = a_kv.reshape(B, T, 6, NSA_KV_HEADS, HEAD_DIM)
        o_a = nsa_attention(a_q.reshape(B, T, N_HEADS, HEAD_DIM), kv[:, :, 0], kv[:, :, 1], kv[:, :, 2], kv[:, :, 3], kv[:, :, 4], kv[:, :, 5], a_g.reshape(B, T, N_HEADS, 3), q_gain[l], k_gain[l], cmp_pos[l], cmp_w1[l], cmp_w2[l], rel_table)
        o_b = short_conv_mixer(b_cols, conv_w[l])
        o_c = spatial_gating_mixer(c_cols, sgu_w[l], sgu_b[l])
        dq, dk, dv = jnp.split(d_cols, 3, axis=-1)
        o_d = stick_breaking_attention(dq.reshape(B, T, N_HEADS, HEAD_DIM), dk.reshape(B, T, N_HEADS, HEAD_DIM), dv.reshape(B, T, N_HEADS, HEAD_DIM))
        mixed = jnp.stack([o_a, o_b, o_c, o_d], axis=2)
        mixed = rms_norm(mixed, group_gain[l].reshape(N_MIXERS, GROUP_WIDTH))
        x = x + mixed.reshape(B, T, D_MODEL) @ w_out[l]
        h = rms_norm(x, norm_ffn[l])
        x = x + (jax.nn.silu(h @ w_ffn_gate[l]) * (h @ w_ffn_up[l])) @ w_ffn_down[l]
    return x


CHUNK_2 = 64
D_PLE = 256
EPS = 1e-6

POOL_WIDTH = D_MODEL // 2
POOL_WINDOWS = (2, 4, 8, 16)
POOL_GROUPS = len(POOL_WINDOWS)
POOL_GROUP_WIDTH = POOL_WIDTH // POOL_GROUPS

V_HEAD = 128
MLA_HEADS = (D_MODEL // 2) // V_HEAD
MLA_WIDTH = MLA_HEADS * V_HEAD
QK_NOPE = 128
QK_ROPE = 64
QK_HEAD = QK_NOPE + QK_ROPE
Q_LORA = 512
KV_LORA = 512
ROPE_THETA = 10000.0

MIX_WIDTH = POOL_WIDTH + MLA_WIDTH
IN_COLS = POOL_WIDTH + Q_LORA + KV_LORA + QK_ROPE

PEER_HEADS = 8
PEER_NKEYS = 128
PEER_EXPERTS = PEER_NKEYS * PEER_NKEYS
PEER_DKEY = 256
PEER_HALF = PEER_DKEY // 2
PEER_TOPK = 16
PEER_TOK_BLOCK = 128


def rms_norm_2(x, g):
    xf = x.astype(jnp.float32)
    y = xf * lax.rsqrt(jnp.mean(xf * xf, axis=-1, keepdims=True) + EPS)
    return (y * g.astype(jnp.float32)).astype(x.dtype)

def apply_rope(x, cos, sin):
    half = QK_ROPE // 2
    xf = x.astype(jnp.float32)
    x1, x2 = xf[..., :half], xf[..., half:]
    return jnp.concatenate([x1 * cos - x2 * sin, x2 * cos + x1 * sin], axis=-1).astype(x.dtype)

def pool_mixer(xp, w_pool, pool_scale):
    B, S, _ = xp.shape
    xf = xp.reshape(B, S, POOL_GROUPS, POOL_GROUP_WIDTH).astype(jnp.float32)
    cs = jnp.cumsum(xf, axis=1)
    t = jnp.arange(S)
    outs = []
    for g, w in enumerate(POOL_WINDOWS):
        csg = cs[:, :, g]
        lower = jnp.pad(csg, ((0, 0), (w, 0), (0, 0)))[:, :S]
        cnt = jnp.minimum(t + 1, w).astype(jnp.float32)[None, :, None]
        outs.append((csg - lower) / cnt - xf[:, :, g])
    d = jnp.stack(outs, axis=2).astype(xp.dtype)
    y = jnp.einsum('bsgc,gcd->bsgd', d, w_pool)
    return y.reshape(B, S, POOL_WIDTH) * pool_scale

def mla(c_q, c_kv, k_rope, positions, q_lat_gain, kv_lat_gain, w_uq, w_ukv, q_norm_gain, k_norm_gain):
    B, S, _ = c_q.shape
    q = (rms_norm_2(c_q, q_lat_gain) @ w_uq).reshape(B, S, MLA_HEADS, QK_HEAD)
    kv = (rms_norm_2(c_kv, kv_lat_gain) @ w_ukv).reshape(B, S, MLA_HEADS, QK_NOPE + V_HEAD)
    k_nope, v = kv[..., :QK_NOPE], kv[..., QK_NOPE:]
    k = jnp.concatenate([k_nope, jnp.broadcast_to(k_rope[:, :, None, :], (B, S, MLA_HEADS, QK_ROPE))], axis=-1)
    q = rms_norm_2(q, q_norm_gain)
    k = rms_norm_2(k, k_norm_gain)
    inv_freq = ROPE_THETA ** (-jnp.arange(0, QK_ROPE, 2, dtype=jnp.float32) / QK_ROPE)
    ang = positions.astype(jnp.float32)[:, :, None] * inv_freq
    cos, sin = jnp.cos(ang)[:, :, None, :], jnp.sin(ang)[:, :, None, :]
    q = jnp.concatenate([q[..., :QK_NOPE], apply_rope(q[..., QK_NOPE:], cos, sin)], axis=-1)
    k = jnp.concatenate([k[..., :QK_NOPE], apply_rope(k[..., QK_NOPE:], cos, sin)], axis=-1)

    nb = S // Q_BLOCK
    qb = q.reshape(B, nb, Q_BLOCK, MLA_HEADS, QK_HEAD).transpose(1, 0, 2, 3, 4)
    k_chunk = jnp.arange(S) // CHUNK_2
    scale = QK_HEAD ** -0.5

    def attend(args):
        q_blk, blk = args
        q_chunk = (blk * Q_BLOCK + jnp.arange(Q_BLOCK)) // CHUNK_2
        s = jnp.einsum('bqhd,bkhd->bhqk', q_blk, k, preferred_element_type=jnp.float32) * scale
        s = jnp.where(k_chunk[None, :] <= q_chunk[:, None], s, -jnp.inf)
        pr = jax.nn.softmax(s, axis=-1).astype(v.dtype)
        return jnp.einsum('bhqk,bkhd->bqhd', pr, v)

    o = lax.map(attend, (qb, jnp.arange(nb)))
    return o.transpose(1, 0, 2, 3, 4).reshape(B, S, MLA_WIDTH)

def peer(xn, w_pq, sub_k1, sub_k2, expert_u, expert_v):
    B, S, D = xn.shape
    q = (xn @ w_pq).reshape(B, S, PEER_HEADS, 2, PEER_HALF)
    s1 = jnp.einsum('bshd,hnd->bshn', q[..., 0, :], sub_k1, preferred_element_type=jnp.float32)
    s2 = jnp.einsum('bshd,hnd->bshn', q[..., 1, :], sub_k2, preferred_element_type=jnp.float32)
    v1, i1 = lax.top_k(s1, PEER_TOPK)
    v2, i2 = lax.top_k(s2, PEER_TOPK)
    cand = (v1[..., :, None] + v2[..., None, :]).reshape(B, S, PEER_HEADS, PEER_TOPK * PEER_TOPK)
    vs, ci = lax.top_k(cand, PEER_TOPK)
    e1 = jnp.take_along_axis(i1, ci // PEER_TOPK, axis=-1)
    e2 = jnp.take_along_axis(i2, ci % PEER_TOPK, axis=-1)
    eidx = e1 * PEER_NKEYS + e2
    gates = jax.nn.softmax(vs, axis=-1).astype(xn.dtype)

    T = B * S
    nblk = T // PEER_TOK_BLOCK
    kk = PEER_HEADS * PEER_TOPK
    xt = xn.reshape(nblk, PEER_TOK_BLOCK, D)
    it = eidx.reshape(nblk, PEER_TOK_BLOCK, kk)
    gt = gates.reshape(nblk, PEER_TOK_BLOCK, kk)

    def block(args):
        xb, ib, gb = args
        act = jax.nn.gelu(jnp.einsum('tkd,td->tk', expert_u[ib], xb))
        return jnp.einsum('tk,tkd->td', act * gb, expert_v[ib])

    return lax.map(block, (xt, it, gt)).reshape(B, S, D)

def second_inputs(seed: int = 0) -> dict:
    key = jax.random.key(seed)
    ks = jax.random.split(key, 24)
    f32 = jnp.float32

    def nrm(k, shape, scale):
        return jax.random.normal(k, shape, f32) * scale

    def gain(k, n):
        return 1.0 + 0.02 * jax.random.normal(k, (DEPTH, n), f32)

    x = jax.random.normal(ks[0], (BATCH, SEQ, D_MODEL), f32)
    p = jax.random.normal(ks[1], (DEPTH, BATCH, SEQ, D_PLE), f32)
    offs = jax.random.randint(ks[2], (BATCH, 1), 0, 4096, dtype=jnp.int32)
    positions = offs + jnp.arange(SEQ, dtype=jnp.int32)[None, :]
    return {
        "x": x,
        "p": p,
        "positions": positions,
        "mix_norm_gain": gain(ks[3], D_MODEL),
        "w_in": nrm(ks[4], (DEPTH, D_MODEL, IN_COLS), D_MODEL ** -0.5),
        "w_pool": nrm(ks[5], (DEPTH, POOL_GROUPS, POOL_GROUP_WIDTH, POOL_GROUP_WIDTH), POOL_GROUP_WIDTH ** -0.5),
        "pool_scale": 1.0 + 0.1 * jax.random.normal(ks[6], (DEPTH, POOL_WIDTH), f32),
        "q_lat_gain": gain(ks[7], Q_LORA),
        "kv_lat_gain": gain(ks[8], KV_LORA),
        "w_uq": nrm(ks[9], (DEPTH, Q_LORA, MLA_HEADS * QK_HEAD), Q_LORA ** -0.5),
        "w_ukv": nrm(ks[10], (DEPTH, KV_LORA, MLA_HEADS * (QK_NOPE + V_HEAD)), KV_LORA ** -0.5),
        "q_norm_gain": gain(ks[11], QK_HEAD),
        "k_norm_gain": gain(ks[12], QK_HEAD),
        "w_out": nrm(ks[13], (DEPTH, MIX_WIDTH, D_MODEL), MIX_WIDTH ** -0.5),
        "ffn_norm_gain": gain(ks[14], D_MODEL),
        "w_pq": nrm(ks[15], (DEPTH, D_MODEL, PEER_HEADS * PEER_DKEY), D_MODEL ** -0.5),
        "sub_k1": nrm(ks[16], (DEPTH, PEER_HEADS, PEER_NKEYS, PEER_HALF), PEER_HALF ** -0.5),
        "sub_k2": nrm(ks[17], (DEPTH, PEER_HEADS, PEER_NKEYS, PEER_HALF), PEER_HALF ** -0.5),
        "expert_u": nrm(ks[18], (DEPTH, PEER_EXPERTS, D_MODEL), D_MODEL ** -0.5),
        "expert_v": nrm(ks[19], (DEPTH, PEER_EXPERTS, D_MODEL), PEER_HEADS ** -0.5),
        "ple_norm_gain": gain(ks[20], D_MODEL),
        "w_ple_gate": nrm(ks[21], (DEPTH, D_MODEL, D_MODEL), D_MODEL ** -0.5),
        "w_ple_proj": nrm(ks[22], (DEPTH, D_PLE, D_MODEL), D_PLE ** -0.5),
    }

def second_block(x, p, positions, mix_norm_gain, w_in, w_pool, pool_scale, q_lat_gain, kv_lat_gain,
              w_uq, w_ukv, q_norm_gain, k_norm_gain, w_out, ffn_norm_gain, w_pq, sub_k1, sub_k2,
              expert_u, expert_v, ple_norm_gain, w_ple_gate, w_ple_proj):
    h = x
    c0 = POOL_WIDTH
    c1 = c0 + Q_LORA
    c2 = c1 + KV_LORA
    for i in range(DEPTH):
        z = rms_norm_2(h, mix_norm_gain[i]) @ w_in[i]
        y_pool = pool_mixer(z[..., :c0], w_pool[i], pool_scale[i])
        y_mla = mla(z[..., c0:c1], z[..., c1:c2], z[..., c2:], positions,
                    q_lat_gain[i], kv_lat_gain[i], w_uq[i], w_ukv[i], q_norm_gain[i], k_norm_gain[i])
        h = h + jnp.concatenate([y_pool, y_mla], axis=-1) @ w_out[i]
        h = h + peer(rms_norm_2(h, ffn_norm_gain[i]), w_pq[i], sub_k1[i], sub_k2[i], expert_u[i], expert_v[i])
        gate = jax.nn.sigmoid(rms_norm_2(h, ple_norm_gain[i]) @ w_ple_gate[i])
        h = h + gate * (p[i] @ w_ple_proj[i])
    return h


def setup_inputs(seed=0):
    out = dict(first_inputs(seed))
    for name, value in second_inputs(seed + 1).items():
        if name != "x":
            out[name + "_2"] = value
    return out


def reference(
    x, w_in, w_out, norm_mix, norm_ffn, q_gain, k_gain, cmp_pos, cmp_w1, cmp_w2, rel_table,
    conv_w, sgu_w, sgu_b, group_gain, w_ffn_gate, w_ffn_up, w_ffn_down, p_2, positions_2,
    mix_norm_gain_2, w_in_2, w_pool_2, pool_scale_2, q_lat_gain_2, kv_lat_gain_2, w_uq_2,
    w_ukv_2, q_norm_gain_2, k_norm_gain_2, w_out_2, ffn_norm_gain_2, w_pq_2, sub_k1_2, sub_k2_2,
    expert_u_2, expert_v_2, ple_norm_gain_2, w_ple_gate_2, w_ple_proj_2,
):
    x = first_block(
        x, w_in, w_out, norm_mix, norm_ffn, q_gain, k_gain, cmp_pos, cmp_w1, cmp_w2, rel_table,
        conv_w, sgu_w, sgu_b, group_gain, w_ffn_gate, w_ffn_up, w_ffn_down,
    )
    return second_block(
        x, p_2, positions_2, mix_norm_gain_2, w_in_2, w_pool_2, pool_scale_2, q_lat_gain_2,
        kv_lat_gain_2, w_uq_2, w_ukv_2, q_norm_gain_2, k_norm_gain_2, w_out_2, ffn_norm_gain_2,
        w_pq_2, sub_k1_2, sub_k2_2, expert_u_2, expert_v_2, ple_norm_gain_2, w_ple_gate_2,
        w_ple_proj_2,
    )


_drawn_inputs = setup_inputs


def setup_inputs(seed=0):
    import zlib

    import numpy as np

    out = dict(_drawn_inputs(seed))
    spreads = {}
    factors = {'q_gain': 3.347,
     'k_gain': 3.217,
     'mix_norm_gain_2': 3.833,
     'q_lat_gain_2': 8.0,
     'kv_lat_gain_2': 7.998,
     'q_norm_gain_2': 8.0,
     'k_norm_gain_2': 8.0,
     'ffn_norm_gain_2': 17.016,
     'ple_norm_gain_2': 64.0}
    for name, (base, spread) in spreads.items():
        noise = np.random.default_rng([zlib.crc32(name.encode()), seed]).standard_normal(out[name].shape)
        drawn = base * np.exp(spread * noise) if base else spread * noise
        out[name] = __import__('jax').numpy.asarray(drawn.astype(out[name].dtype))
    for name, factor in factors.items():
        out[name] = (out[name] * factor).astype(out[name].dtype)
    return out
```

```python
import concourse.bass as bass
from concourse import mybir
from contextlib import ExitStack
import math
import numpy as np

F32 = mybir.dt.float32
I32 = mybir.dt.int32
U32 = mybir.dt.uint32
ALU = mybir.AluOpType
ACT = mybir.ActivationFunctionType
AX = mybir.AxisListType

P = 128
T = 256
NT = T // P
D = 2048
KD = D // P
BANK = 512

HD = 64
NH = 8
NG = 2
W_IN_COLS = 5400
A_KV = 512
A_GATE = 1280
B_OFF = 1304
C_OFF = B_OFF + 1536
D_OFF = C_OFF + 1024
D_FF = 5632
KF = D_FF // P
CMP_LEN, CMP_STRIDE = 32, 16
N_CMP = (T - CMP_LEN) // CMP_STRIDE + 1
N_CMP0 = (P - CMP_LEN) // CMP_STRIDE + 1
NEG = -1.0e30

POOL_W = 1024
WINDOWS = (2, 4, 8, 16)
Q_OFF, KV_OFF, ROPE_OFF = 1024, 1536, 2048
IN2_COLS = 2112
QKH = 192
TOPK = 16
NKEYS = 128
SLOTS = NH * TOPK
HALF = 32

G_MIX, G_FFN, G_MIX2, G_FFN2, G_PLE, G_GROUP = 0, 16, 32, 48, 64, 80
G_POOL, G_QLAT, G_KVLAT = 96, 104, 108
G_Q, G_K, G_QN, G_KN, G_SGUB = 112, 113, 114, 115, 116
G_ROWS = 124


def place(h):
    return h % 2 * (NH // 2) + h // 2


def rel_buckets():
    n = np.arange(T)
    nf = np.maximum(n, 1).astype(np.float32)
    large = 16 + (np.log(nf / np.float32(16)) / np.float32(math.log(64)) * np.float32(16)).astype(np.int32)
    return np.where(n < 16, n, np.minimum(large, 31))


class Signal:

    def __init__(self, nc, name):
        self.sem, self.total = nc.alloc_semaphore(name), 0

    def at(self, k):
        return k + self.total

    def close(self, n):
        self.total += n


class Chain:

    def __init__(self, nc, name):
        self.sem, self.n, self.eng = nc.alloc_semaphore(name), 0, None

    def on(self, eng):
        self.eng = eng
        return self

    def __call__(self, ins):
        self.n += 1
        ins.then_inc(self.sem, 1)
        self.eng.wait_ge(self.sem, self.n)


class Stream:

    def __init__(self, source, view, rounds, last=4):
        self.source, self.view, self.rounds, self.last = source, view, rounds, last


class Ring:

    SLOTS = 4
    WORDS = 4096

    def __init__(self, nc):
        self.buf = nc.alloc_sbuf_tensor("weights", [P, self.SLOTS, self.WORDS], F32)
        self.ready = [nc.alloc_semaphore(f"weights_ready{j}") for j in range(self.SLOTS)]
        self.used = nc.alloc_semaphore("weights_used")
        self.fills = 0
        self.base = [0] * self.SLOTS

    def slot(self, j, k, n):
        return self.buf[:, j, 0:k * n].rearrange("p (k n) -> p k n", k=k)

    def fill(self, sp, stream, i, j, fills, wait=True):
        if wait:
            sp.wait_ge(self.used, i * 4 + (fills + j - 3))
        k, n = stream.view
        sp.dma_start(self.slot(j, k, n), stream.source(i, j)).then_inc(self.ready[j], 16)

    def wait(self, pe, i, j):
        pe.wait_ge(self.ready[j], i * 16 + (self.base[j] + 16))

    def rest(self, sp, stream, following):
        if stream.rounds > 2:
            with sp.Fori(1, stream.rounds - (stream.last < 4)) as i:
                for j in range(4):
                    self.fill(sp, stream, i, j, self.fills)
            if stream.last < 4:
                for j in range(stream.last):
                    self.fill(sp, stream, stream.rounds - 1, j, self.fills)
        else:
            for i in range(1, stream.rounds):
                for j in range(4):
                    self.fill(sp, stream, i, j, self.fills)
        if following is not None:
            after = self.fills + 4 * stream.rounds
            for j in range(4 if following.rounds > 1 or following.last == 4 else following.last):
                self.fill(sp, following, 0, j, after)

    def close(self, stream):
        for j in range(4):
            self.base[j] += 16 * (stream.rounds - (j >= stream.last))
        self.fills += 4 * stream.rounds


def wide(w, width, halves=2):
    v = w.rearrange("(k p) n -> p k n", p=P)
    return lambda i, j: v[:, 8 * (j % 2):8 * (j % 2) + 8, bass.ds((i * 2 + j // 2) * width, width)]


class Kernel:
    def __init__(self, nc, a, out):
        self.nc, self.a, self.out = nc, a, out
        sb, ps = nc.alloc_sbuf_tensor, nc.alloc_psum_tensor
        self.X = sb("residual", [P, NT, D], F32)
        self.XN = sb("normed", [P, NT, D], F32)
        self.hT = sb("features_first", [P, KD, T], F32)
        self.ident = sb("identity", [P, P], F32)
        self.gT = sb("gains", [P, G_ROWS], F32)
        self.ring = Ring(nc)
        self.psum = ps("banks", [P, 8 * BANK], F32)
        self.bank_free = [Signal(nc, f"product_bank_free{t}") for t in range(NT)]
        self.turned = Signal(nc, "transposes_done")
        self.turned_read = {e: Signal(nc, f"transposes_read_{e}") for e in ("act", "dve")}
        self.squares = Signal(nc, "squares_summed")
        self.rstd_ready = Signal(nc, "rstd_ready")
        self.scaled = {e: Signal(nc, f"scaled_{e}") for e in ("act", "dve")}
        self.act_chain, self.dve_chain = Chain(nc, "act_chain"), Chain(nc, "dve_chain")
        self.pool_chain, self.sp_chain = Chain(nc, "pool_chain"), Chain(nc, "loads")
        self.loads = 0
        self.minus_half = sb("minus_half", [P, 32], F32)
        self.stat = sb("statistics", [P, 32], F32)
        self.rstd = sb("rstd", [P, 32], F32)
        self.att = sb("attention_statistics", [P, 4, NT, NH], F32)

    def bank(self, b, n=BANK, off=0):
        return self.psum[:, b * BANK + off:b * BANK + off + n]

    def sem(self, name):
        return self.nc.alloc_semaphore(name)

    def block(self):
        return self.nc.Block()

    def rstd_on_pool(self, pool, n, count, extra=1.0, eps=1e-6):
        ch = self.pool_chain.on(pool)
        st, rs = self.stat[:, 0:count], self.rstd[:, 0:count]
        ch(pool.tensor_scalar(st, st, 1.0 / n, eps, ALU.mult, ALU.add))
        ch(pool.tensor_tensor(out=rs, in0=st, in1=self.minus_half[:, 0:count], op=ALU.pow))
        if extra != 1.0:
            ch(pool.tensor_scalar(rs, rs, extra, 0.0, ALU.mult, ALU.add))

    def turn(self, jobs, pe, act, dve, start=None):
        tr, rd = self.turned, self.turned_read
        for j, (ins, dst, gains) in enumerate(jobs):
            b = 4 + j % 4
            reader, k = ("act", "dve")[j % 2], j // 2 + 1
            if pe is not None:
                if j >= 4:
                    pe.wait_ge(rd[reader].sem, rd[reader].at(k - 2))
                off = 0
                for n, i in enumerate(ins):
                    pin, f = i.shape[0], i.shape[1] if len(i.shape) == 2 else int(np.prod(i.shape[1:]))
                    last = pe.transpose(self.psum[0:f, b * BANK + off:b * BANK + off + pin], i,
                                        self.ident[0:pin, 0:pin])
                    off += pin
                last.then_inc(tr.sem, 1)
                continue
            if (act is None) == (reader == "act"):
                continue
            eng = act if act is not None else dve
            eng.wait_ge(tr.sem, tr.at(j + 1))
            rows = dst.shape[0]
            size = int(np.prod(dst.shape[1:]))
            parts = gains or [(size, None)]
            flat = dst if len(dst.shape) == 2 else dst.rearrange("p a b -> p (a b)")
            off = 0
            for n, gain in parts:
                src, to = self.psum[0:rows, b * BANK + off:b * BANK + off + n], flat[:, off:off + n]
                if act is not None:
                    last = eng.activation(to, src, ACT.Copy, scale=1.0 if gain is None else gain)
                elif gain is None:
                    last = eng.tensor_copy(to, src)
                else:
                    last = eng.tensor_scalar(to, src, gain, None, ALU.mult)
                off += n
            last.then_inc(rd[reader].sem, 1)

    def turn_close(self, jobs):
        n = len(jobs)
        self.turned.close(n)
        self.turned_read["act"].close((n + 1) // 2)
        self.turned_read["dve"].close(n // 2)

    def gain(self, row, scale_rows=P):
        return self.gT[0:scale_rows, row:row + 1]

    def turn_stage(self, jobs):
        with self.block() as block:
            @block.tensor
            def _(pe):
                self.turn(jobs, pe, None, None)

            @block.scalar
            def _(act):
                self.turn(jobs, None, act, None)

            @block.vector
            def _(dve):
                self.turn(jobs, None, None, dve)
        self.turn_close(jobs)

    def feature_jobs(self, src, dst, kc, grow):
        jobs = []
        for k in range(0, kc, 2):
            ins = [src(t)[:, kk * P:(kk + 1) * P] for kk in (k, k + 1) for t in range(NT)]
            g = None if grow is None else [(T, self.gain(grow + k)), (T, self.gain(grow + k + 1))]
            jobs.append((ins, dst[:, k:k + 2, :], g))
        return jobs

    def norm_turn(self, src, groups, n, dst, grow):
        sq, rs, sc = self.squares, self.rstd_ready, self.scaled
        width = groups * n
        jobs = self.feature_jobs(lambda t: self.XN[:, t, 0:width], dst, width // P, grow)
        with self.block() as block:
            @block.scalar
            def _(act):
                for t in range(NT):
                    for g in range(groups):
                        c = t * groups + g
                        last = act.activation(self.XN[:, t, g * n:(g + 1) * n], src(t)[:, g * n:(g + 1) * n],
                                              ACT.Square, accum_out=self.stat[:, c:c + 1])
                last.then_inc(sq.sem, 1)
                act.wait_ge(rs.sem, rs.at(1))
                for g in range(groups):
                    last = act.activation(self.XN[:, 0, g * n:(g + 1) * n], src(0)[:, g * n:(g + 1) * n],
                                          ACT.Copy, scale=self.rstd[:, g:g + 1])
                last.then_inc(sc["act"].sem, 1)
                self.turn(jobs, None, act, None)

            @block.gpsimd
            def _(pool):
                pool.wait_ge(sq.sem, sq.at(1))
                self.rstd_on_pool(pool, n, NT * groups)
                pool.sem_inc(rs.sem, 1)

            @block.vector
            def _(dve):
                dve.wait_ge(rs.sem, rs.at(1))
                for g in range(groups):
                    c = groups + g
                    last = dve.tensor_scalar(self.XN[:, 1, g * n:(g + 1) * n], src(1)[:, g * n:(g + 1) * n],
                                             self.rstd[:, c:c + 1], None, ALU.mult)
                last.then_inc(sc["dve"].sem, 1)
                self.turn(jobs, None, None, dve)

            @block.tensor
            def _(pe):
                pe.wait_ge(sc["act"].sem, sc["act"].at(1))
                pe.wait_ge(sc["dve"].sem, sc["dve"].at(1))
                self.turn(jobs, pe, None, None)
        for s in (sq, rs, sc["act"], sc["dve"]):
            s.close(1)
        self.turn_close(jobs)

    def linear(self, stream, following, xT, kc, width, evac, on):
        ring = self.ring
        per = 2 if kc == KD else 4
        fpc = 4 // per
        kf = kc // fpc
        rounds = stream.rounds

        def rounds_of(eng, body):
            if rounds > 2:
                with eng.Fori(0, rounds) as i:
                    body(i)
            else:
                for i in range(rounds):
                    body(i)

        with self.block() as block:
            @block.sync
            def _(sp):
                ring.rest(sp, stream, following)

            @block.tensor
            def _(pe):
                def body(i):
                    for c in range(per):
                        for t in range(NT):
                            pe.wait_ge(self.bank_free[t].sem, i * per + self.bank_free[t].at(c + 1))
                        for f in range(fpc):
                            j = c * fpc + f
                            ring.wait(pe, i, j)
                            w = ring.slot(j, kf, width)
                            for k in range(kf):
                                for t in range(NT):
                                    last = pe.matmul(self.bank(2 * (c % 2) + t, width),
                                                     xT[:, f * kf + k, t * P:(t + 1) * P], w[:, k, :],
                                                     start=(f == 0 and k == 0), stop=(f == fpc - 1 and k == kf - 1))
                            last.then_inc(ring.used, 1)
                rounds_of(pe, body)

            def reader(name):
                def program(eng):
                    def body(i):
                        for c in range(per):
                            eng.wait_ge(ring.used, i * 4 + (ring.fills + (c + 1) * fpc))
                            for t in range(NT):
                                if on[t] == name:
                                    evac(eng, t, i * per + c, self.bank(2 * (c % 2) + t, width))\
                                        .then_inc(self.bank_free[t].sem, 1)
                    rounds_of(eng, body)
                return program

            if "act" in on:
                block.scalar(reader("act"))
            if "dve" in on:
                block.vector(reader("dve"))
        for t in range(NT):
            self.bank_free[t].close(rounds * per)
        ring.close(stream)

    def setup(self, first):
        a, nc = self.a, self.nc
        sb = nc.alloc_sbuf_tensor
        self.tri = sb("later_keys", [P, P], F32)
        self.ones = sb("ones", [P, P], F32)
        self.cosT = sb("cos", [P, NT, HALF], F32)
        self.sinT = sb("sin", [P, NT, HALF], F32)
        self.gbq = sb("rope_gain_q", [P, 64], F32)
        self.gbk = sb("rope_gain_k", [P, 64], F32)
        g = {}
        with ExitStack() as ctx:
            tmp = lambda n, s, d=F32: ctx.enter_context(nc.sbuf_tensor(n, s, d))
            gin = tmp("gains_in", [P, P])
            posi = tmp("positions", [P, NT], I32)
            posf = tmp("positions_f", [P, NT])
            freq = tmp("frequencies", [P, HALF])
            ang = tmp("angles", [P, 2, NT, HALF])
            turns = tmp("whole_turns", [P, 2, NT, HALF])
            loaded, made, cast = self.sem("small_loaded"), self.sem("constants_made"), self.sem("angles_ready")
            turned, kept = self.sem("gains_turned"), self.sem("gains_kept")
            rows = [(a["norm_mix"], G_MIX, 16), (a["norm_ffn"], G_FFN, 16), (a["mix_norm_gain_2"], G_MIX2, 16),
                    (a["ffn_norm_gain_2"], G_FFN2, 16), (a["ple_norm_gain_2"], G_PLE, 16),
                    (a["group_gain"], G_GROUP, 16), (a["pool_scale_2"], G_POOL, 8),
                    (a["q_lat_gain_2"], G_QLAT, 4), (a["kv_lat_gain_2"], G_KVLAT, 4)]
            inv = (np.float32(10000.0) ** (-np.arange(0, 64, 2, dtype=np.float32) / np.float32(64))).astype(np.float32)

            with self.block() as block:
                @block.sync
                def _(sp):
                    xv = a["x"][0].rearrange("(t p) c -> p t c", p=P)
                    sp.dma_start(self.X[:, :, :], xv).then_inc(loaded, 16)
                    for j in range(4):
                        self.ring.fill(sp, first, 0, j, 0, wait=False)

                @block.scalar
                def _(act):
                    n = 0
                    for src, r, k in rows:
                        act.dma_start(gin[r:r + k, :], src[0].rearrange("(k p) -> k p", p=P)).then_inc(loaded, 16)
                    for src, r in ((a["q_gain"], G_Q), (a["k_gain"], G_K)):
                        for h in range(2):
                            act.dma_start(gin[r:r + 1, 64 * h:64 * h + 64], src).then_inc(loaded, 16)
                    for src, r in ((a["q_norm_gain_2"], G_QN), (a["k_norm_gain_2"], G_KN)):
                        act.dma_start(gin[r:r + 1, :], src[:, 0:P]).then_inc(loaded, 16)
                    act.dma_start(gin[G_SGUB:G_SGUB + NH, :], a["sgu_b"][0]).then_inc(loaded, 16)
                    for src, to in ((a["q_norm_gain_2"], self.gbq), (a["k_norm_gain_2"], self.gbk)):
                        act.dma_start(to[:, :], src[:, P:QKH].to_broadcast([P, 64])).then_inc(loaded, 16)
                    act.dma_start(posi[:, :], a["positions_2"].rearrange("o (t p) -> p (o t)", p=P),
                                  allow_slow_non_contiguous=True).then_inc(loaded, 16)
                    act.wait_ge(loaded, 16 * (1 + len(rows) + 4 + 2 + 1 + 2 + 1))
                    act.wait_ge(cast, 1)
                    act.activation(self.sinT[:, :, :], ang[:, 0, :, :], ACT.Sin)
                    act.activation(self.cosT[:, :, :], ang[:, 1, :, :], ACT.Sin)

                @block.gpsimd
                def _(pool):
                    ch = self.pool_chain.on(pool)
                    pool.memset(self.minus_half[:, :], -0.5)
                    pool.memset(self.ones[:, :], 1.0)
                    ch(pool.memset(self.ident[:, :], 0.0))
                    ch(pool.affine_select(out=self.ident[:, :], in_=self.ident[:, :], pattern=[[-1, P]],
                                          compare_op=ALU.not_equal, fill=1.0, base=0, channel_multiplier=1))
                    ch(pool.affine_select(out=self.tri[:, :], in_=self.ones[:, :], pattern=[[-1, P]],
                                          compare_op=ALU.is_gt, fill=0.0, base=0, channel_multiplier=1))
                    for k in range(HALF):
                        last = pool.memset(freq[:, k:k + 1], float(inv[k]))
                    ch(last)
                    pool.sem_inc(made, 1)

                @block.tensor
                def _(pe):
                    pe.wait_ge(loaded, 16 * 20)
                    pe.wait_ge(made, 1)
                    pe.transpose(self.bank(0, G_ROWS), gin[0:G_ROWS, :], self.ident[0:G_ROWS, 0:G_ROWS])\
                        .then_inc(turned, 1)

                @block.vector
                def _(dve):
                    ch = self.dve_chain.on(dve)
                    dve.wait_ge(loaded, 16 * 20)
                    dve.wait_ge(made, 1)
                    ch(dve.tensor_copy(posf[:, :], posi[:, :]))
                    for t in range(NT):
                        last = dve.tensor_scalar(ang[:, 0, t, :], freq[:, :], posf[:, t:t + 1], None, ALU.mult)
                    ch(last)
                    magic = 1.5 * 2.0 ** 23
                    two_pi = 2 * math.pi
                    c1 = 6.28125
                    c2 = float(np.float32(two_pi - c1))
                    c2 = float(np.frombuffer((np.frombuffer(np.float32(c2).tobytes(), np.uint32) & 0xFFFFF000)
                                             .astype(np.uint32).tobytes(), np.float32)[0])
                    c3 = float(np.float32(two_pi - c1 - c2))
                    ch(dve.tensor_scalar(turns[:, 0], ang[:, 0], 1.0 / two_pi, magic, ALU.mult, ALU.add))
                    ch(dve.tensor_scalar(turns[:, 1], ang[:, 0], 1.0 / two_pi, 0.25, ALU.mult, ALU.add))
                    ch(dve.tensor_scalar(turns[:, 1], turns[:, 1], magic, None, ALU.add))
                    ch(dve.tensor_scalar(turns[:, :], turns[:, :], magic, None, ALU.subtract))
                    ch(dve.tensor_copy(ang[:, 1], ang[:, 0]))
                    flat = lambda x: x[:, :, :, :].rearrange("p a t k -> p (a t k)")
                    for c in (c1, c2, c3):
                        ch(dve.scalar_tensor_tensor(out=flat(ang), in0=flat(turns), scalar=-c, in1=flat(ang),
                                                    op0=ALU.mult, op1=ALU.add))
                    ch(dve.tensor_scalar(ang[:, 1], ang[:, 1], math.pi / 2, None, ALU.add))
                    edge = 3.1415925
                    ch(dve.tensor_scalar(ang[:, :], ang[:, :], edge, -edge, ALU.min, ALU.max))
                    dve.sem_inc(cast, 1)
                    dve.wait_ge(turned, 1)
                    ch(dve.tensor_copy(self.gT[:, :], self.bank(0, G_ROWS)))
                    ch(dve.tensor_scalar(self.gT[:, G_Q:G_Q + 1], self.gT[:, G_Q:G_Q + 1], HD ** -0.5, None, ALU.mult))
                    for t in range(NT):
                        dve.sem_inc(self.bank_free[t].sem, 2)

    def conv(self, PR, M):
        nc = self.nc
        with ExitStack() as ctx:
            tmp = lambda n, s: ctx.enter_context(nc.sbuf_tensor(n, s, F32))
            z = tmp("conv_z", [P, 3, NT, BANK])
            cw = tmp("conv_weights", [P, 3, BANK])
            y = tmp("conv_part", [P, NT, BANK])
            gated, zeros, moved = self.sem("conv_gated"), self.sem("conv_zeros"), self.sem("conv_moved")
            out = M[:, :, BANK:2 * BANK]
            with self.block() as block:
                @block.gpsimd
                def _(pool):
                    self.pool_chain.on(pool)(pool.memset(z[0:2, 1:3, 0, :], 0.0))
                    pool.sem_inc(zeros, 1)

                @block.sync
                def _(sp):
                    sp.dma_start(cw[:, :, :], self.a["conv_w"].rearrange("o k c -> o (k c)")
                                 .to_broadcast([P, 3 * BANK]).rearrange("p (k c) -> p k c", k=3)).then_inc(moved, 16)
                    sp.wait_ge(gated, 1)
                    sp.wait_ge(zeros, 1)
                    for s in (1, 2):
                        sp.dma_start(z[s:P, s, :, :], z[0:P - s, 0, :, :]).then_inc(moved, 16)
                        sp.dma_start(z[0:s, s, 1, :], z[P - s:P, 0, 0, :]).then_inc(moved, 16)
                    sp.wait_ge(moved, 16 * 5)

                @block.vector
                def _(dve):
                    ch = self.dve_chain.on(dve)
                    ch(dve.tensor_tensor(z[:, 0], PR[:, :, B_OFF + 512:B_OFF + 1024],
                                         PR[:, :, B_OFF + 1024:B_OFF + 1536], ALU.mult))
                    dve.sem_inc(gated, 1)
                    w = lambda i: cw[:, i:i + 1, :].to_broadcast([P, NT, BANK])
                    dve.wait_ge(moved, 16 * 5)
                    ch(dve.tensor_tensor(out, z[:, 2], w(0), ALU.mult))
                    ch(dve.tensor_tensor(y[:, :, :], z[:, 1], w(1), ALU.mult))
                    ch(dve.tensor_tensor(out, out, y[:, :, :], ALU.add))
                    ch(dve.tensor_tensor(y[:, :, :], z[:, 0], w(2), ALU.mult))
                    ch(dve.tensor_tensor(out, out, y[:, :, :], ALU.add))
                    ch(dve.tensor_tensor(out, out, PR[:, :, B_OFF:B_OFF + 512], ALU.mult))

    def sgu(self, PR, M):
        nc = self.nc
        with ExitStack() as ctx:
            tmp = lambda n, s: ctx.enter_context(nc.sbuf_tensor(n, s, F32))
            w_in = tmp("sgu_w", [P, NH, P])
            wT = tmp("sgu_w_turned", [P, NH, P])
            v = tmp("sgu_v", [P, NT, BANK])
            junk = tmp("sgu_squares", [P, BANK])
            loaded = self.sem("sgu_loaded")
            with self.block() as block:
                @block.sync
                def _(sp):
                    sp.dma_start(w_in[:, :, :], self.a["sgu_w"][0].rearrange("h p q -> p h q")).then_inc(loaded, 16)
                    sp.wait_ge(loaded, 16)
            self.turn_stage([([w_in[:, 4 * b + h, :] for h in range(4)], wT[:, 4 * b:4 * b + 4, :], None)
                             for b in range(2)])
            summed, mean, centred, squared, rs, normed = [self.sem("sgu_" + n) for n in (
                "summed", "mean", "centred", "squared", "rstd", "normed")]
            masked, mixed = self.sem("sgu_masked"), self.sem("sgu_mixed")
            C = PR[:, :, C_OFF:C_OFF + 1024]
            with self.block() as block:
                @block.gpsimd
                def _(pool):
                    ch = self.pool_chain.on(pool)
                    ch(pool.affine_select(out=wT[:, :, :], in_=wT[:, :, :], pattern=[[0, NH], [1, P]],
                                          compare_op=ALU.is_ge, fill=0.0, base=0, channel_multiplier=-1))
                    pool.sem_inc(masked, 1)
                    pool.wait_ge(squared, 1)
                    self.rstd_on_pool(pool, BANK, NT, eps=1e-5)
                    pool.sem_inc(rs, 1)

                @block.scalar
                def _(act):
                    ch = self.act_chain.on(act)
                    ch(act.activation(C[:, :, 0:512], C[:, :, 0:512], ACT.Gelu_apprx_tanh))
                    for t in range(NT):
                        last = act.activation(v[:, t, :], C[:, t, 512:1024], ACT.Gelu_apprx_tanh,
                                              accum_out=self.stat[:, 4 + t:5 + t])
                    ch(last)
                    act.sem_inc(summed, 1)
                    act.wait_ge(centred, 1)
                    for t in range(NT):
                        ch(act.activation(junk[:, :], v[:, t, :], ACT.Square, accum_out=self.stat[:, t:t + 1]))
                    act.sem_inc(squared, 1)

                @block.vector
                def _(dve):
                    ch = self.dve_chain.on(dve)
                    dve.wait_ge(summed, 1)
                    ch(dve.tensor_scalar(self.stat[:, 8:10], self.stat[:, 4:6], 1.0 / BANK, None, ALU.mult))
                    for t in range(NT):
                        last = dve.tensor_scalar(v[:, t, :], v[:, t, :], self.stat[:, 8 + t:9 + t], None, ALU.subtract)
                    ch(last)
                    dve.sem_inc(centred, 1)
                    dve.wait_ge(rs, 1)
                    for t in range(NT):
                        last = dve.tensor_scalar(v[:, t, :], v[:, t, :], self.rstd[:, t:t + 1], None, ALU.mult)
                    ch(last)
                    dve.sem_inc(normed, 1)
                    dve.wait_ge(mixed, 1)
                    bias = self.gT[:, G_SGUB:G_SGUB + NH].unsqueeze(2).to_broadcast([P, NH, HD])
                    for t in range(NT):
                        o = M[:, t, 1024:1536]
                        ch(dve.tensor_tensor(o.rearrange("p (h d) -> p h d", h=NH),
                                             self.bank(t).rearrange("p (h d) -> p h d", h=NH), bias, ALU.add))
                        ch(dve.tensor_tensor(o, o, C[:, t, 0:512], ALU.mult))

                @block.tensor
                def _(pe):
                    pe.wait_ge(masked, 1)
                    pe.wait_ge(normed, 1)
                    for t in range(NT):
                        for h in range(NH):
                            last = pe.matmul(self.bank(t, HD, h * HD), wT[:, h, :], v[:, t, h * HD:(h + 1) * HD],
                                             start=True, stop=True)
                    last.then_inc(mixed, 1)

    def sticks(self, PR, M):
        nc = self.nc
        with ExitStack() as ctx:
            tmp = lambda n, s: ctx.enter_context(nc.sbuf_tensor(n, s, F32))
            qT, kT = tmp("stick_q", [P, 4, T]), tmp("stick_k", [P, 4, T])
            n0, n1 = NH * T, NH * P
            Z, L, W = [self.XN[:, :, :].rearrange("p t c -> p (t c)")[:, 0:n0 + n1],
                       self.hT[:, :, :].rearrange("p k t -> p (k t)")[:, 0:n0 + n1], tmp("stick_w", [P, n0 + n1])[:, :]]
            for c, dst in ((0, qT), (512, kT)):
                self.turn_stage(self.feature_jobs(lambda t: PR[:, t, D_OFF + c:D_OFF + c + 512], dst[:, :, :], 4, None))
            scored, scaled, negd, logd, mask_ready = [self.sem("stick_" + n) for n in (
                "scored", "scaled", "negated", "logs", "masked")]
            sub, tailed, added, exped, amask, mixed = [self.sem("stick_" + n) for n in (
                "log_rest", "tails", "exponents", "weights", "weights_masked", "outputs")]
            allz = self.psum[:, 0:n0 + n1]

            def causal(pool, x):
                for lo, n in ((0, T), (n0, P)):
                    v = x[:, lo:lo + NH * n].rearrange("p (h t) -> p h t", h=NH)
                    last = pool.affine_select(out=v, in_=v, pattern=[[0, NH], [1, n]], compare_op=ALU.is_gt,
                                              fill=0.0, base=0, channel_multiplier=-1)
                return last

            with self.block() as block:
                @block.tensor
                def _(pe):
                    for h in range(NH):
                        r = slice(HD * (h % 2), HD * (h % 2) + HD)
                        s = place(h)
                        pe.matmul(self.psum[:, s * T:(s + 1) * T], kT[r, h // 2, 0:P], qT[r, h // 2, :],
                                  start=True, stop=True)
                        last = pe.matmul(self.psum[:, n0 + s * P:n0 + (s + 1) * P], kT[r, h // 2, P:T],
                                         qT[r, h // 2, P:T], start=True, stop=True)
                    last.then_inc(scored, 1)
                    pe.wait_ge(mask_ready, 1)
                    for h in range(NH):
                        if h % 2 == 0:
                            pe.matmul(self.psum[:, h * T:(h + 2) * T], self.tri[:, :], L[:, h * T:(h + 2) * T],
                                      start=True, stop=False)
                        pe.matmul(self.psum[:, h * T + P:(h + 1) * T], self.ones[:, :],
                                  L[:, n0 + h * P:n0 + (h + 1) * P], start=False, stop=(h % 2 == 1))
                    for b in range(2):
                        last = pe.matmul(self.bank(4 + b), self.tri[:, :], L[:, n0 + b * BANK:n0 + (b + 1) * BANK],
                                         start=True, stop=True)
                    last.then_inc(tailed, 1)
                    pe.wait_ge(amask, 1)
                    v = lambda t, h: PR[:, t, D_OFF + 1024 + h * HD:D_OFF + 1024 + (h + 1) * HD]
                    for h in range(NH):
                        s = place(h)
                        pe.matmul(self.bank(6, HD, h * HD), Z[:, s * T:s * T + P], v(0, h), start=True, stop=True)
                        pe.matmul(self.bank(7, HD, h * HD), Z[:, s * T + P:(s + 1) * T], v(0, h), start=True, stop=False)
                        last = pe.matmul(self.bank(7, HD, h * HD), Z[:, n0 + s * P:n0 + (s + 1) * P], v(1, h),
                                         start=False, stop=True)
                    last.then_inc(mixed, 1)

                @block.scalar
                def _(act):
                    ch = self.act_chain.on(act)
                    act.wait_ge(scored, 1)
                    ch(act.activation(Z, allz, ACT.Copy, scale=HD ** -0.5))
                    act.sem_inc(scaled, 1)
                    act.wait_ge(negd, 1)
                    ch(act.activation(L, L, ACT.Exp))
                    ch(act.activation(L, L, ACT.Ln, bias=1.0))
                    act.sem_inc(logd, 1)
                    act.wait_ge(added, 1)
                    ch(act.activation(Z, W, ACT.Exp))
                    act.sem_inc(exped, 1)

                @block.vector
                def _(dve):
                    ch = self.dve_chain.on(dve)
                    dve.wait_ge(scaled, 1)
                    ch(dve.scalar_tensor_tensor(out=L, in0=Z, scalar=-1.0, in1=Z, op0=ALU.mult, op1=ALU.min))
                    dve.sem_inc(negd, 1)
                    dve.wait_ge(logd, 1)
                    ch(dve.scalar_tensor_tensor(out=W, in0=Z, scalar=0.0, in1=L, op0=ALU.min, op1=ALU.subtract))
                    ch(dve.tensor_tensor(L, W, Z, ALU.subtract))
                    dve.sem_inc(sub, 1)
                    dve.wait_ge(tailed, 1)
                    ch(dve.tensor_tensor(W, allz, W, ALU.add))
                    dve.sem_inc(added, 1)
                    dve.wait_ge(mixed, 1)
                    for t in range(NT):
                        ch(dve.tensor_copy(M[:, t, 1536:2048], self.bank(6 + t)))

                @block.gpsimd
                def _(pool):
                    ch = self.pool_chain.on(pool)
                    pool.wait_ge(sub, 1)
                    ch(causal(pool, L))
                    pool.sem_inc(mask_ready, 1)
                    pool.wait_ge(exped, 1)
                    ch(causal(pool, Z))
                    pool.sem_inc(amask, 1)

    def attention(self, name, nk, qk, bias, val, dv, out, factor, add, work):
        S, PT, wide_tmp = work
        chunks = [[(c, min(P, nk[t] - c)) for c in range(0, nk[t], P)] for t in range(NT)]
        soff, poff = (0, NH * nk[0]), (0, NH * P * len(chunks[0]))
        s_view = lambda t: S[:, soff[t]:soff[t] + NH * nk[t]].rearrange("p (h n) -> p h n", h=NH)
        s_at = lambda h, t: soff[t] + place(h) * nk[t]
        sbank = (0, 2)
        obank = (6, 7) if dv * NH <= BANK else (6, 0)
        scored, shifted, weighed, turned, kept, mixed, out_read = [self.sem(name + n) for n in (
            "_scores", "_maxima", "_weights", "_weights_turned", "_weights_kept", "_outputs", "_outputs_read")]
        st = self.att
        negmax, sums, inv, fac = [st[:, i] for i in range(4)]

        with self.block() as block:
            @block.tensor
            def _(pe):
                for t in range(NT):
                    for h in range(NH):
                        at = (sbank[t] + (h % 2) * (t + 1)) * BANK + h // 2 * nk[t]
                        o = self.psum[:, at:at + nk[t]]
                        for i, (q, k) in enumerate(qk):
                            last = pe.matmul(o, q(h, t), k(h, nk[t]), start=(i == 0), stop=(i == len(qk) - 1))
                    last.then_inc(scored, 1)
                for t in range(NT):
                    pe.wait_ge(weighed, t + 1)
                    for h in range(NH):
                        for c, (k0, kn) in enumerate(chunks[t]):
                            o = sbank[t] * BANK + (h * len(chunks[t]) + c) * P
                            last = pe.transpose(self.psum[0:kn, o:o + P],
                                                S[:, s_at(h, t) + k0:s_at(h, t) + k0 + kn],
                                                self.ident[:, :])
                    last.then_inc(turned, 1)
                for t in range(NT):
                    pe.wait_ge(kept, t + 1)
                    for h in range(NH):
                        for c, (k0, kn) in enumerate(chunks[t]):
                            p0 = poff[t] + (h * len(chunks[t]) + c) * P
                            last = pe.matmul(self.bank(obank[t], dv, h * dv), PT[0:kn, p0:p0 + P], val(h, c, kn),
                                             start=(c == 0), stop=(c == len(chunks[t]) - 1))
                    last.then_inc(mixed, 1)

            @block.vector
            def _(dve):
                ch = self.dve_chain.on(dve)
                for t in range(NT):
                    dve.wait_ge(scored, t + 1)
                    for odd in range(2):
                        ps = self.bank(sbank[t] + odd * (t + 1), 4 * nk[t]).rearrange("p (h n) -> p h n", h=4)
                        h4 = slice(4 * odd, 4 * odd + 4)
                        last = dve.tensor_tensor(s_view(t)[:, h4], ps, bias(t)[:, h4], ALU.add)
                    ch(last)
                    ch(dve.tensor_reduce(negmax[:, t, :], s_view(t), AX.X, ALU.max, negate=True))
                    dve.sem_inc(shifted, 1)
                for t in range(NT):
                    dve.wait_ge(weighed, t + 1)
                    ch(dve.reciprocal(inv[:, t, :], sums[:, t, :]))
                    f = inv
                    if factor is not None:
                        ch(dve.tensor_tensor(fac[:, t, :], inv[:, t, :], factor(t), ALU.mult))
                        f = fac
                    dve.wait_ge(mixed, t + 1)
                    ps = self.bank(obank[t], NH * dv).rearrange("p (h d) -> p h d", h=NH)
                    fb = f[:, t, :].unsqueeze(2).to_broadcast([P, NH, dv])
                    if add:
                        w = wide_tmp[:, 0:NH * dv].rearrange("p (h d) -> p h d", h=NH)
                        ch(dve.tensor_tensor(w, ps, fb, ALU.mult))
                        ch(dve.tensor_tensor(out(t), out(t), w, ALU.add))
                    else:
                        ch(dve.tensor_tensor(out(t), ps, fb, ALU.mult))

            @block.scalar
            def _(act):
                ch = self.act_chain.on(act)
                for t in range(NT):
                    act.wait_ge(shifted, t + 1)
                    for h in range(NH):
                        s = S[:, s_at(h, t):s_at(h, t) + nk[t]]
                        last = act.activation(s, s, ACT.Exp, bias=negmax[:, t, place(h):place(h) + 1],
                                              accum_out=sums[:, t, h:h + 1])
                    ch(last)
                    act.sem_inc(weighed, 1)
                for t in range(NT):
                    act.wait_ge(turned, t + 1)
                    rows = chunks[t][0][1]
                    n = NH * len(chunks[t]) * P
                    ch(act.activation(PT[0:rows, poff[t]:poff[t] + n],
                                      self.psum[0:rows, sbank[t] * BANK:sbank[t] * BANK + n], ACT.Copy))
                    act.sem_inc(kept, 1)

    def nsa(self, PR, M):
        nc, a = self.nc, self.a
        with ExitStack() as ctx:
            tmp = lambda n, s: ctx.enter_context(nc.sbuf_tensor(n, s, F32))
            biasT = tmp("distance_bias", [P, NH, T])
            qT = tmp("nsa_q", [P, 4, T])
            kT = tmp("nsa_k", [P, 4, T])
            kcT = tmp("nsa_kc", [P, NG, N_CMP])
            vc = tmp("nsa_vc", [N_CMP, NG, HD])
            gates = tmp("nsa_gates", [P, NT, 3 * NH])
            S = self.XN[:, :, :].rearrange("p t c -> p (t c)")[:, 0:NH * 3 * P]
            PT = self.hT[:, :, :].rearrange("p k t -> p (k t)")[:, 0:NH * 3 * P]
            wtmp = self.XN[:, 1, 1024:1536]
            vec_dram = nc.dram_tensor("bias_by_distance", [NH, 2 * T], F32, kind="Internal")
            bucket = rel_buckets()

            with ExitStack() as c2:
                tm2 = lambda n, s: c2.enter_context(nc.sbuf_tensor(n, s, F32))
                w1 = self.XN[:, :, :].rearrange("p t (l e) -> p t l e", e=HD)
                w2 = tm2("cmp_w2", [HD, 2, HD])
                pos_in = tm2("cmp_pos", [2 * CMP_LEN, HD])
                posT = tm2("cmp_pos_turned", [HD, 2 * CMP_LEN])
                tab = tm2("table", [32, NH])
                tabT = tm2("table_turned", [NH, 32])
                vec = self.hT[0:NH, 0:2, :].rearrange("p k t -> p (k t)")
                zT = self.hT[:, 2:4, :]
                flipped = self.hT[:, 4:4 + NH, :]
                flip = tm2("flip", [P, P])
                loaded, vecd = self.sem("nsa_loaded"), self.sem("bias_vector_made")
                with self.block() as block:
                    @block.sync
                    def _(sp):
                        for h in range(2):
                            for i in range(2):
                                sp.dma_start(w1[h * HD:(h + 1) * HD, i], a["cmp_w1"][0, i]
                                             .rearrange("(l d) e -> d l e", d=HD)).then_inc(loaded, 16)
                        sp.dma_start(w2[:, :, :], a["cmp_w2"][0].rearrange("i d e -> d i e")).then_inc(loaded, 16)
                        sp.dma_start(pos_in[:, :], a["cmp_pos"][0].rearrange("i l d -> (i l) d")).then_inc(loaded, 16)
                        sp.dma_start(tab[:, :], a["rel_table"]).then_inc(loaded, 16)
                        sp.wait_ge(loaded, 16 * 7)
                self.turn_stage([([tab[:, :]], tabT[:, :], None), ([pos_in[:, :]], posT[:, :], None),
                                 ([PR[:, t, A_KV + P * i:A_KV + P * (i + 1)] for i in range(2) for t in range(NT)],
                                  zT, None)])
                with self.block() as block:
                    @block.vector
                    def _(dve):
                        ch = self.dve_chain.on(dve)
                        last = dve.memset(vec[:, T:2 * T], NEG)
                        for b in range(bucket[-1] + 1):
                            at = np.flatnonzero(bucket == b)
                            if len(at):
                                lo, n = T - 1 - int(at[-1]), len(at)
                                last = dve.tensor_copy(vec[:, lo:lo + n], tabT[:, b:b + 1].to_broadcast([NH, n]))
                        ch(last)
                        dve.sem_inc(vecd, 1)

                    @block.gpsimd
                    def _(pool):
                        ch = self.pool_chain.on(pool)
                        ch(pool.memset(flip[:, :], 0.0))
                        ch(pool.affine_select(out=flip[:, :], in_=flip[:, :], pattern=[[1, P]], compare_op=ALU.not_equal,
                                              fill=1.0, base=1 - P, channel_multiplier=1))

                    @block.sync
                    def _(sp):
                        sp.wait_ge(vecd, 1)
                        sp.dma_start(vec_dram[:, :], vec).then_inc(loaded, 16)
                        sp.wait_ge(loaded, 16 * 8)
                        for odd in range(2):
                            sp.dma_start(flipped[:, 4 * odd:4 * odd + 4, :],
                                         bass.AP(tensor=vec_dram[:, :].tensor, offset=odd * 2 * T,
                                                 ap=[[1, P], [4 * T, 4], [1, T]])).then_inc(loaded, 16)
                        sp.wait_ge(loaded, 16 * 10)

                H1 = tm2("cmp_hidden", [HD, 2, NG, N_CMP])
                posb = tm2("cmp_pos_part", [HD, 2])
                kc = tm2("cmp_k", [N_CMP, NG, 2, HD])
                sq = tm2("cmp_squares", [N_CMP, NG, HD])
                first, hid, second, ssq, rsd, unflipped = [self.sem("cmp_" + n) for n in (
                    "first", "hidden", "second", "squares", "rstd", "bias_unflipped")]
                with self.block() as block:
                    @block.tensor
                    def _(pe):
                        for b in range(4):
                            last = pe.matmul(self.bank(4 + b), flip[:, :],
                                             flipped[:, 2 * b:2 * b + 2, :].rearrange("p h t -> p (h t)"),
                                             start=True, stop=True)
                        last.then_inc(unflipped, 1)
                        for i in range(2):
                            for g in range(NG):
                                r = slice(g * HD, (g + 1) * HD)
                                for l in range(CMP_LEN):
                                    pe.matmul(self.psum[0:HD, g * BANK + i * 16:g * BANK + i * 16 + N_CMP], w1[r, i, l, :],
                                              zT[r, i, l:l + CMP_STRIDE * (N_CMP - 1) + 1:CMP_STRIDE],
                                              start=(l == 0), stop=(l == CMP_LEN - 1))
                            for l in range(CMP_LEN):
                                last = pe.matmul(self.psum[0:HD, 128 + i:129 + i], w1[0:HD, i, l, :],
                                                 posT[:, i * CMP_LEN + l:i * CMP_LEN + l + 1],
                                                 start=(l == 0), stop=(l == CMP_LEN - 1))
                        last.then_inc(first, 1)
                        pe.wait_ge(hid, 1)
                        for i in range(2):
                            for g in range(NG):
                                last = pe.matmul(self.bank(2, HD, (2 * i + g) * HD)[0:N_CMP],
                                                 H1[:, i, g, :], w2[:, i, :], start=True, stop=True)
                        last.then_inc(second, 1)

                    @block.scalar
                    def _(act):
                        ch = self.act_chain.on(act)
                        act.wait_ge(first, 1)
                        ch(act.activation(posb[:, :], self.psum[0:HD, 128:130], ACT.Copy))
                        for i in range(2):
                            for g in range(NG):
                                last = act.activation(H1[:, i, g, :], self.bank(g, N_CMP, i * 16)[0:HD],
                                                      ACT.Gelu_apprx_tanh, bias=posb[:, i:i + 1])
                        ch(last)
                        act.sem_inc(hid, 1)

                    @block.vector
                    def _(dve):
                        ch = self.dve_chain.on(dve)
                        dve.wait_ge(unflipped, 1)
                        ch(dve.tensor_copy(biasT[:, :, :].rearrange("p h t -> p (h t)"), self.psum[:, 4 * BANK:8 * BANK]))
                        dve.wait_ge(second, 1)
                        ps = self.bank(2, 4 * HD)[0:N_CMP].rearrange("p (i g d) -> p i g d", i=2, g=NG)
                        ch(dve.tensor_copy(vc[:, :, :], ps[:, 1]))
                        ch(dve.tensor_copy(kc[:, :, 0, :], ps[:, 0]))
                        ch(dve.tensor_tensor(sq[:, :, :], kc[:, :, 0, :], kc[:, :, 0, :], ALU.mult))
                        ch(dve.tensor_reduce(self.stat[0:N_CMP, 0:NG], sq[:, :, :], AX.X, ALU.add))
                        dve.sem_inc(ssq, 1)
                        dve.wait_ge(rsd, 1)
                        rb = self.rstd[0:N_CMP, 0:NG].unsqueeze(2).to_broadcast([N_CMP, NG, HD])
                        ch(dve.tensor_tensor(kc[:, :, 0, :], kc[:, :, 0, :], rb, ALU.mult))
                        ch(dve.tensor_copy(kc[:, :, 1, :], kc[:, :, 0, :]))

                    @block.gpsimd
                    def _(pool):
                        pool.wait_ge(ssq, 1)
                        ch = self.pool_chain.on(pool)
                        st, rs = self.stat[0:N_CMP, 0:NG], self.rstd[0:N_CMP, 0:NG]
                        ch(pool.tensor_scalar(st, st, 1.0 / HD, 1e-6, ALU.mult, ALU.add))
                        ch(pool.tensor_tensor(out=rs, in0=st, in1=self.minus_half[0:N_CMP, 0:NG], op=ALU.pow))
                        pool.sem_inc(rsd, 1)
                self.turn_stage([([kc[:, g].rearrange("p a d -> p (a d)")], kcT[:, g, :], [(N_CMP, self.gain(G_K))])
                                 for g in range(NG)])

            with ExitStack() as c2:
                tm2 = lambda n, s: c2.enter_context(nc.sbuf_tensor(n, s, F32))
                qn = tm2("nsa_q_normed", [P, NT, 512])
                kn = tm2("nsa_k_normed", [P, NT, 2, NG, 2, HD])
                ks = tm2("nsa_k_squares", [P, NT, 2, NG, HD])
                ssq, rsd = self.sem("nsa_squares"), self.sem("nsa_rstd")
                with self.block() as block:
                    @block.scalar
                    def _(act):
                        act.activation(gates[:, :, :], PR[:, :, A_GATE:A_GATE + 24], ACT.Sigmoid)

                    @block.vector
                    def _(dve):
                        ch = self.dve_chain.on(dve)
                        kv = lambda t: PR[:, t, A_KV + 256:A_KV + 1280 - 512 + 0].rearrange(
                            "p (b s g d) -> p b s g d", b=2, s=2, g=NG)[:, :, 0]
                        q = PR[:, :, 0:512]
                        ch(dve.tensor_tensor(qn[:, :, :], q, q, ALU.mult))
                        for t in range(NT):
                            last = dve.tensor_tensor(ks[:, t], kv(t), kv(t), ALU.mult)
                        ch(last)
                        for t in range(NT):
                            dve.tensor_reduce(self.stat[:, 8 * t:8 * t + 8],
                                              qn[:, t, :].rearrange("p (h d) -> p h d", h=NH), AX.X, ALU.add)
                            last = dve.tensor_reduce(self.stat[:, 16 + 4 * t:20 + 4 * t],
                                                     ks[:, t].rearrange("p b g d -> p (b g) d"), AX.X, ALU.add)
                        ch(last)
                        dve.sem_inc(ssq, 1)
                        dve.wait_ge(rsd, 1)
                        for t in range(NT):
                            dve.tensor_tensor(qn[:, t, :].rearrange("p (h d) -> p h d", h=NH),
                                              q[:, t, :].rearrange("p (h d) -> p h d", h=NH),
                                              self.rstd[:, 8 * t:8 * t + 8].unsqueeze(2).to_broadcast([P, NH, HD]), ALU.mult)
                            for b in range(2):
                                for dup in range(2):
                                    r = self.rstd[:, 16 + 4 * t + 2 * b:18 + 4 * t + 2 * b]
                                    last = dve.tensor_tensor(kn[:, t, b, :, dup, :], kv(t)[:, b],
                                                             r.unsqueeze(2).to_broadcast([P, NG, HD]), ALU.mult)
                        ch(last)

                    @block.gpsimd
                    def _(pool):
                        pool.wait_ge(ssq, 1)
                        self.rstd_on_pool(pool, HD, 24)
                        pool.sem_inc(rsd, 1)
                jobs = []
                for k in range(0, 4, 2):
                    jobs.append(([qn[:, t, kk * P:(kk + 1) * P] for kk in (k, k + 1) for t in range(NT)],
                                 qT[:, k:k + 2, :], [(2 * T, self.gain(G_Q))]))
                for b in range(2):
                    jobs.append(([kn[:, t, b, g].rearrange("p a d -> p (a d)") for g in range(NG) for t in range(NT)],
                                 kT[:, 2 * b:2 * b + 2, :], [(2 * T, self.gain(G_K))]))
                self.turn_stage(jobs)

            q = lambda h, t: qT[HD * (h % 2):HD * (h % 2) + HD, h // 2, t * P:(t + 1) * P]
            g = lambda h: h // (NH // NG)
            out = lambda t: M[:, t, 0:512].rearrange("p (h d) -> p h d", h=NH)
            gate = lambda b: (lambda t: gates[:, t, b:3 * NH:3])
            with self.block() as block:
                @block.gpsimd
                def _(pool):
                    self.pool_chain.on(pool)(pool.affine_select(
                        out=gates[:, 0, 0:3 * NH:3], in_=gates[:, 0, 0:3 * NH:3], pattern=[[0, NH]],
                        compare_op=ALU.is_ge, fill=0.0, base=-(CMP_LEN - 1), channel_multiplier=1))
            first = P + CMP_LEN - 1
            cmp_bias = lambda t: (biasT[:, :, first:T:CMP_STRIDE] if t == 0 else biasT[:, :, CMP_LEN - 1:T:CMP_STRIDE])
            self.attention("cmp", (N_CMP0, N_CMP),
                           [(q, lambda h, n: kcT[HD * (h % 2):HD * (h % 2) + HD, g(h), 0:n])],
                           cmp_bias, lambda h, c, n: vc[0:n, g(h), :], HD, out, gate(0), False, (S, PT, wtmp))
            all_bias = lambda t: biasT[:, :, P:T] if t == 0 else biasT[:, :, :]
            for b, name in ((0, "selected"), (1, "window")):
                self.attention(name, (P, T),
                               [(q, lambda h, n: kT[HD * (h % 2):HD * (h % 2) + HD, 2 * b + g(h), 0:n])],
                               all_bias,
                               lambda h, c, n: PR[0:n, c, A_KV + 384 + 256 * b + g(h) * HD:A_KV + 384 + 256 * b + (g(h) + 1) * HD],
                               HD, out, gate(1 + b), True, (S, PT, wtmp))

    def ffn(self, streams, following):
        nc, ring = self.nc, self.ring
        up, down = streams
        rounds = up.rounds
        with ExitStack() as ctx:
            tmp = lambda n, s: ctx.enter_context(nc.sbuf_tensor(n, s, F32))
            aT = tmp("ffn_turned", [P, KF, T])
            sg = tmp("ffn_silu", [P, NT, BANK])
            pr = tmp("ffn_product", [P, NT, BANK])
            silu, prod, turned, kept = [self.sem("ffn_" + n) for n in ("silu", "product", "turned", "kept")]
            with self.block() as block:
                @block.sync
                def _(sp):
                    ring.rest(sp, up, down)

                @block.tensor
                def _(pe):
                    def half(i, m):
                        for f in range(2):
                            j = 2 * m + f
                            ring.wait(pe, i, j)
                            w = ring.slot(j, 8, BANK)
                            for k in range(8):
                                for t in range(NT):
                                    last = pe.matmul(self.bank(2 * m + t), self.hT[:, 8 * f + k, t * P:(t + 1) * P],
                                                     w[:, k, :], start=(f == 0 and k == 0), stop=(f == 1 and k == 7))
                            last.then_inc(ring.used, 1)

                    def turn(i):
                        pe.wait_ge(prod, i)
                        pe.wait_ge(kept, i)
                        for k in range(4):
                            for t in range(NT):
                                last = pe.transpose(self.bank(4 + k // 2, P, (k % 2) * T + t * P),
                                                    pr[:, t, k * P:(k + 1) * P], self.ident[:, :])
                        last.then_inc(turned, 1)

                    half(0, 0)
                    half(0, 1)
                    with pe.Fori(1, rounds) as i:
                        pe.wait_ge(silu, i)
                        half(i, 0)
                        turn(i)
                        half(i, 1)
                    turn(rounds)

                @block.scalar
                def _(act):
                    def gate(i):
                        act.wait_ge(ring.used, i * 4 + (ring.fills + 2))
                        for t in range(NT):
                            last = act.activation(sg[:, t, :], self.bank(t), ACT.Silu)
                        last.then_inc(silu, 1)

                    def keep(i):
                        act.wait_ge(turned, i)
                        for b in range(2):
                            last = act.activation(aT[:, bass.ds((i - 1) * 4 + 2 * b, 2), :].rearrange("p k t -> p (k t)"),
                                                  self.bank(4 + b), ACT.Copy)
                        last.then_inc(kept, 1)

                    act.sem_inc(kept, 1)
                    gate(0)
                    with act.Fori(1, rounds) as i:
                        act.wait_ge(prod, i)
                        gate(i)
                        keep(i)
                    keep(rounds)

                @block.vector
                def _(dve):
                    def product(i):
                        dve.wait_ge(silu, i + 1)
                        dve.wait_ge(ring.used, i * 4 + (ring.fills + 4))
                        for t in range(NT):
                            last = dve.tensor_tensor(pr[:, t, :], self.bank(2 + t), sg[:, t, :], ALU.mult)
                        last.then_inc(prod, 1)
                    product(0)
                    with dve.Fori(1, rounds) as i:
                        dve.wait_ge(turned, i)
                        product(i)
            ring.close(up)
            with self.block() as block:
                @block.sync
                def _(sp):
                    ring.rest(sp, down, following)

                @block.tensor
                def _(pe):
                    for n in range(KF // 2):
                        i, j = n // 4, n % 4
                        ring.wait(pe, i, j)
                        w = ring.slot(j, 2, D)
                        for k in range(2):
                            kk = 2 * n + k
                            for t in range(NT):
                                for c in range(4):
                                    last = pe.matmul(self.bank(4 * t + c), aT[:, kk, t * P:(t + 1) * P],
                                                     w[:, k, c * BANK:(c + 1) * BANK], start=(kk == 0), stop=(kk == KF - 1))
                        last.then_inc(ring.used, 1 if n < KF // 2 - 1 else 1 + 4 - down.last)

                @block.vector
                def _(dve):
                    dve.wait_ge(ring.used, ring.fills + 4 * down.rounds)
                    for t in range(NT):
                        self.dve_chain.on(dve)(dve.tensor_tensor(self.X[:, t, :], self.psum[:, 4 * t * BANK:4 * (t + 1) * BANK],
                                                                 self.X[:, t, :], ALU.add))
            ring.close(down)

    def pool_mix(self, Z, M):
        nc, a = self.nc, self.a
        with ExitStack() as ctx:
            tmp = lambda n, s: ctx.enter_context(nc.sbuf_tensor(n, s, F32))
            band = tmp("pool_band", [P, 4, T + P])
            wp = tmp("pool_w", [P, 4, 2, T])
            dT = tmp("pool_turned", [P, 4, 2, T])
            made, loaded, diff, kept, done = [self.sem("pool_" + n) for n in ("bands", "loaded", "means", "kept", "done")]
            with self.block() as block:
                @block.sync
                def _(sp):
                    sp.dma_start(wp[:, :, :, :].rearrange("p g k d -> p (g k) d"),
                                 a["w_pool_2"][0].rearrange("g (k p) d -> p (g k) d", p=P)).then_inc(loaded, 16)

                @block.gpsimd
                def _(pool):
                    ch = self.pool_chain.on(pool)
                    for g, w in enumerate(WINDOWS):
                        last = pool.memset(band[:, g, :], 1.0 / w)
                    ch(last)
                    for g, w in enumerate(WINDOWS):
                        for t in range(w - 1):
                            last = pool.memset(band[:, g, t:t + 1], 1.0 / (t + 1))
                    ch(last)
                    for g, w in enumerate(WINDOWS):
                        for lo, n in ((0, T), (T, P)):
                            v = band[:, g, lo:lo + n]
                            ch(pool.affine_select(out=v, in_=v, pattern=[[1, n]], compare_op=ALU.is_ge, fill=0.0,
                                                  base=0, channel_multiplier=-1))
                            ch(pool.affine_select(out=v, in_=v, pattern=[[-1, n]], compare_op=ALU.is_ge, fill=0.0,
                                                  base=w - 1, channel_multiplier=1))
                            ch(pool.tensor_tensor(out=band[:, g, lo:lo + P], in0=band[:, g, lo:lo + P],
                                                  in1=self.ident[:, :], op=ALU.subtract))
                    pool.sem_inc(made, 1)

                @block.tensor
                def _(pe):
                    pe.wait_ge(made, 1)
                    for g in range(4):
                        for c in range(2):
                            o = (2 * g + c) * T
                            col = slice(g * T + c * P, g * T + (c + 1) * P)
                            pe.matmul(self.psum[:, o:o + T], Z[:, 0, col], band[:, g, 0:T], start=True, stop=False)
                            last = pe.matmul(self.psum[:, o + P:o + T], Z[:, 1, col], band[:, g, T:T + P],
                                             start=False, stop=True)
                    last.then_inc(diff, 1)
                    pe.wait_ge(loaded, 16)
                    pe.wait_ge(kept, 1)
                    for t in range(NT):
                        for g in range(4):
                            for c in range(2):
                                last = pe.matmul(self.bank(4 + 2 * t + g // 2, T, (g % 2) * T),
                                                 dT[:, g, c, t * P:(t + 1) * P], wp[:, g, c, :], start=(c == 0), stop=(c == 1))
                    last.then_inc(done, 1)

                @block.scalar
                def _(act):
                    act.wait_ge(diff, 1)
                    self.act_chain.on(act)(act.activation(dT[:, :, :, :].rearrange("p g c t -> p (g c t)"),
                                                          self.psum[:, 0:8 * T], ACT.Copy))
                    act.sem_inc(kept, 1)

                @block.vector
                def _(dve):
                    dve.wait_ge(done, 1)
                    for t in range(NT):
                        dve.tensor_copy(M[:, t, 0:POOL_W], self.psum[:, (4 + 2 * t) * BANK:(6 + 2 * t) * BANK])

    def mla(self, Q, KV, Zr, M):
        nc = self.nc
        with ExitStack() as ctx:
            tmp = lambda n, s: ctx.enter_context(nc.sbuf_tensor(n, s, F32))
            qT, kT = tmp("mla_q", [P, NH, T]), tmp("mla_k", [P, NH, T])
            qrT, krT = tmp("mla_q_rope", [P, 4, T]), tmp("mla_k_rope", [P, 4, T])
            mask = tmp("mla_mask", [P, T + P])
            S = self.XN[:, :, :].rearrange("p t c -> p (t c)")[:, 0:NH * 3 * P]
            PT = self.hT[:, :, :].rearrange("p k t -> p (k t)")[:, 0:NH * 3 * P]
            q4 = Q.rearrange("p t (h d) -> p t h d", h=NH)
            kv4 = KV.rearrange("p t (h d) -> p t h d", h=NH)
            with ExitStack() as c2:
                tm2 = lambda n, s: c2.enter_context(nc.sbuf_tensor(n, s, F32))
                junk = self.XN[:, 0, 0:NH * QKH]
                kg = tm2("rope_k", [P, NT, 64])
                rot = tm2("rope_k_turned", [P, NT, 64])
                rr = tm2("rope_parts", [P, 2, NH, HALF])
                kr = tm2("rope_k_heads", [P, NT, NH, 64])
                qr = tm2("rope_q_heads", [P, NT, NH, 64])
                ssq, rsd, masked = self.sem("mla_squares"), self.sem("mla_rstd"), self.sem("mla_masked")

                def rope(dve, ch, dst, src, heads, t):
                    a1, a2 = src[:, :, 0:HALF], src[:, :, HALF:64]
                    cos = self.cosT[:, t:t + 1, :].to_broadcast([P, heads, HALF])
                    sin = self.sinT[:, t:t + 1, :].to_broadcast([P, heads, HALF])
                    r = rr[:, :, 0:heads, :]
                    ch(dve.tensor_tensor(r[:, 0], a2, sin, ALU.mult))
                    ch(dve.tensor_tensor(dst[:, :, 0:HALF], a1, cos, ALU.mult))
                    ch(dve.tensor_tensor(dst[:, :, 0:HALF], dst[:, :, 0:HALF], r[:, 0], ALU.subtract))
                    ch(dve.tensor_tensor(r[:, 1], a1, sin, ALU.mult))
                    ch(dve.tensor_tensor(dst[:, :, HALF:64], a2, cos, ALU.mult))
                    ch(dve.tensor_tensor(dst[:, :, HALF:64], dst[:, :, HALF:64], r[:, 1], ALU.add))

                with self.block() as block:
                    @block.vector
                    def _(dve):
                        ch = self.dve_chain.on(dve)
                        for t in range(NT):
                            jq = junk.rearrange("p (h d) -> p h d", h=NH)
                            ch(dve.tensor_tensor(jq, q4[:, t], q4[:, t], ALU.mult))
                            ch(dve.tensor_reduce(self.stat[:, 8 * t:8 * t + 8], jq, AX.X, ALU.add))
                            jk = junk[:, 0:NH * P].rearrange("p (h d) -> p h d", h=NH)
                            ch(dve.tensor_tensor(jk, kv4[:, t, :, 0:P], kv4[:, t, :, 0:P], ALU.mult))
                            ch(dve.tensor_reduce(self.stat[:, 16 + 8 * t:24 + 8 * t], jk, AX.X, ALU.add))
                            jr = junk[:, 0:64]
                            ch(dve.tensor_tensor(jr, Zr[:, t, :], Zr[:, t, :], ALU.mult))
                            ch(dve.tensor_reduce(kg[:, t, 0:1], jr, AX.X, ALU.add))
                            ch(dve.tensor_scalar(self.stat[:, 16 + 8 * t:24 + 8 * t], self.stat[:, 16 + 8 * t:24 + 8 * t],
                                                 kg[:, t, 0:1], None, ALU.add))
                        dve.sem_inc(ssq, 1)
                        ch(dve.tensor_tensor(kg[:, :, :], Zr, self.gbk[:, :].unsqueeze(1).to_broadcast([P, NT, 64]), ALU.mult))
                        for t in range(NT):
                            rope(dve, ch, rot[:, t:t + 1, :], kg[:, t:t + 1, :], 1, t)
                        dve.wait_ge(rsd, 1)
                        for t in range(NT):
                            rq = self.rstd[:, 8 * t:8 * t + 8].unsqueeze(2)
                            rk = self.rstd[:, 16 + 8 * t:24 + 8 * t].unsqueeze(2)
                            ch(dve.tensor_tensor(q4[:, t], q4[:, t], rq.to_broadcast([P, NH, QKH]), ALU.mult))
                            ch(dve.tensor_tensor(kv4[:, t, :, 0:P], kv4[:, t, :, 0:P], rk.to_broadcast([P, NH, P]), ALU.mult))
                            ch(dve.tensor_tensor(kr[:, t], rot[:, t:t + 1, :].to_broadcast([P, NH, 64]),
                                                 rk.to_broadcast([P, NH, 64]), ALU.mult))
                            ch(dve.tensor_tensor(q4[:, t, :, P:QKH], q4[:, t, :, P:QKH],
                                                 self.gbq[:, :].unsqueeze(1).to_broadcast([P, NH, 64]), ALU.mult))
                            rope(dve, ch, qr[:, t], q4[:, t, :, P:QKH], NH, t)

                    @block.gpsimd
                    def _(pool):
                        ch = self.pool_chain.on(pool)
                        ch(pool.memset(mask[:, :], 0.0))
                        pool.memset(mask[0:64, 64:P], NEG)
                        ch(pool.memset(mask[0:64, T + 64:T + P], NEG))
                        pool.wait_ge(ssq, 1)
                        self.rstd_on_pool(pool, QKH, 32)
                        ch(pool.tensor_scalar(self.rstd[:, 0:16], self.rstd[:, 0:16], QKH ** -0.5, 0.0, ALU.mult, ALU.add))
                        pool.sem_inc(rsd, 1)
                jobs = []
                for h in range(0, NH, 2):
                    jobs.append(([q4[:, t, hh, 0:P] for hh in (h, h + 1) for t in range(NT)], qT[:, h:h + 2, :],
                                 [(2 * T, self.gain(G_QN))]))
                    jobs.append(([kv4[:, t, hh, 0:P] for hh in (h, h + 1) for t in range(NT)], kT[:, h:h + 2, :],
                                 [(2 * T, self.gain(G_KN))]))
                for k in range(0, 4, 2):
                    for src, dst in ((qr, qrT), (kr, krT)):
                        jobs.append(([src[:, t, 2 * kk:2 * kk + 2, :].rearrange("p a d -> p (a d)")
                                      for kk in (k, k + 1) for t in range(NT)], dst[:, k:k + 2, :], None))
                self.turn_stage(jobs)
            r = lambda h: slice(HD * (h % 2), HD * (h % 2) + HD)
            tok = lambda t: slice(t * P, (t + 1) * P)
            self.attention("mla", (P, T),
                           [(lambda h, t: qT[:, h, tok(t)], lambda h, n: kT[:, h, 0:n]),
                            (lambda h, t: qrT[r(h), h // 2, tok(t)], lambda h, n: krT[r(h), h // 2, 0:n])],
                           lambda t: (mask[:, 0:P] if t == 0 else mask[:, P:P + T]).unsqueeze(1).to_broadcast([P, NH, (P, T)[t]]),
                           lambda h, c, n: KV[0:n, c, h * T + P:(h + 1) * T], P,
                           lambda t: M[:, t, POOL_W:D].rearrange("p (h d) -> p h d", h=NH), None, False, (S, PT, None))

    def peer(self, following, w_pq):
        nc, a = self.nc, self.a
        J = 2 * NH
        with ExitStack() as ctx:
            tmp = lambda n, s, d=F32: ctx.enter_context(nc.sbuf_tensor(n, s, d))
            eidx = tmp("expert_index", [P, NT, SLOTS], U32)
            gts = tmp("expert_gates", [P, NT, NH, TOPK])
            wts = tmp("expert_weights", [P, NT, SLOTS])
            with ExitStack() as c2:
                tm2 = lambda n, s, d=F32: c2.enter_context(nc.sbuf_tensor(n, s, d))
                qp = tm2("peer_q", [P, NT, D])
                sk = tm2("sub_keys", [P, J, P])
                skT = tm2("sub_keys_turned", [P, J, P])
                SC = tm2("peer_scores", [P, NT, D])
                self.linear(w_pq, following, self.hT[:, :, :], KD, BANK,
                            lambda eng, t, c, ps: self.copy_out(eng, qp[:, t, bass.ds(c * BANK, BANK)], ps), ("act", "dve"))
                loaded = self.sem("sub_keys_loaded")
                with self.block() as block:
                    @block.scalar
                    def _(act):
                        for h, name in enumerate(("sub_k1_2", "sub_k2_2")):
                            act.dma_start(sk[:, h:J:2, :], a[name][0].rearrange("h n d -> n h d")).then_inc(loaded, 16)
                        act.wait_ge(loaded, 32)
                self.turn_stage(self.feature_jobs(lambda t: qp[:, t, :], self.hT[:, :, :], KD, None)
                                + [([sk[:, j + i, :] for i in range(4)], skT[:, j:j + 4, :], None) for j in range(0, J, 4)])
                scored, ex, exped = self.sem("peer_scored"), self.sem("peer_shifted"), self.sem("peer_exponentials")
                v, vi = tm2("top_values", [P, NT, J, TOPK]), tm2("top_index", [P, NT, J, TOPK], U32)
                vif = tm2("top_index_f", [P, NT, J, TOPK])
                cv, ci = tm2("pair_values", [P, NT, NH, TOPK]), tm2("pair_index", [P, NT, NH, TOPK], U32)
                cab = tm2("pair_parts", [P, 2, NT, NH, TOPK], U32)
                cf = tm2("pair_parts_f", [P, 2, NT, NH, TOPK])
                io, iof = tm2("count", [P, TOPK], I32), tm2("count_f", [P, TOPK])
                e12 = tm2("pair_experts", [P, 2, NT, NH, TOPK])
                sm = tm2("gate_sums", [P, NT, NH])
                counted = self.sem("counted")
                LOW = -3.0e38
                with self.block() as block:
                    @block.gpsimd
                    def _(pool):
                        ch = self.pool_chain.on(pool)
                        ch(pool.iota(io[:, :], pattern=[[1, TOPK]], base=0, channel_multiplier=0))
                        pool.sem_inc(counted, 1)

                    @block.tensor
                    def _(pe):
                        for t in range(NT):
                            for j in range(J):
                                last = pe.matmul(self.psum[:, (t * J + j) * P:(t * J + j + 1) * P],
                                                 self.hT[:, j, t * P:(t + 1) * P], skT[:, j, :], start=True, stop=True)
                        last.then_inc(scored, 1)

                    @block.vector
                    def _(dve):
                        ch = self.dve_chain.on(dve)
                        dve.wait_ge(scored, 1)
                        ch(dve.tensor_copy(SC[:, :, :].rearrange("p t c -> p (t c)"), self.psum[:, :]))

                        def top16(rows):
                            for s, val, ind in rows:
                                last = dve.max(val[:, 0:8], s)
                            ch(last)
                            for s, val, ind in rows:
                                last = dve.max_index(ind[:, 0:8], val[:, 0:8], s)
                            ch(last)
                            for s, val, ind in rows:
                                last = dve.match_replace(s, val[:, 0:8], s, LOW)
                            ch(last)
                            for s, val, ind in rows:
                                last = dve.max(val[:, 8:16], s)
                            ch(last)
                            for s, val, ind in rows:
                                last = dve.max_index(ind[:, 8:16], val[:, 8:16], s)
                            ch(last)

                        top16([(SC[:, t, j * P:(j + 1) * P], v[:, t, j, :], vi[:, t, j, :]) for t in range(NT) for j in range(J)])
                        ch(dve.tensor_copy(vif[:, :, :, :], vi[:, :, :, :]))
                        for t in range(NT):
                            pair = SC[:, t, :].rearrange("p (h a b) -> p h a b", h=NH, a=TOPK)
                            last = dve.tensor_tensor(pair, v[:, t, 0:J:2, :].unsqueeze(3).to_broadcast([P, NH, TOPK, TOPK]),
                                                     v[:, t, 1:J:2, :].unsqueeze(2).to_broadcast([P, NH, TOPK, TOPK]), ALU.add)
                        ch(last)
                        top16([(SC[:, t, h * 256:(h + 1) * 256], cv[:, t, h, :], ci[:, t, h, :]) for t in range(NT) for h in range(NH)])
                        dve.tensor_scalar(cab[:, 0], ci[:, :, :, :], 4, None, ALU.logical_shift_right)
                        ch(dve.tensor_scalar(cab[:, 1], ci[:, :, :, :], TOPK - 1, None, ALU.bitwise_and))
                        ch(dve.tensor_copy(cf[:, :].rearrange("p a t h k -> p (a t h k)"),
                                           cab[:, :].rearrange("p a t h k -> p (a t h k)")))
                        dve.wait_ge(counted, 1)
                        ch(dve.tensor_copy(iof[:, :], io[:, :]))
                        for half in range(2):
                            for t in range(NT):
                                m = SC[:, t, :].rearrange("p (h k a) -> p h k a", h=NH, k=TOPK)
                                m3 = SC[:, t, :].rearrange("p (hk a) -> p hk a", a=TOPK)
                                ch(dve.tensor_tensor(m3, cf[:, half, t].rearrange("p h k -> p (h k)").unsqueeze(2)
                                                     .to_broadcast([P, SLOTS, TOPK]),
                                                     iof[:, :].unsqueeze(1).to_broadcast([P, SLOTS, TOPK]), ALU.is_equal))
                                ch(dve.tensor_tensor(m, m, vif[:, t, half:J:2, :].unsqueeze(2)
                                                     .to_broadcast([P, NH, TOPK, TOPK]), ALU.mult))
                                ch(dve.tensor_reduce(e12[:, half, t].rearrange("p h k -> p (h k)"), m3, AX.X, ALU.add))
                        ch(dve.scalar_tensor_tensor(out=eidx[:, :, :], in0=e12[:, 0].rearrange("p t h k -> p t (h k)"),
                                                    scalar=float(NKEYS), in1=e12[:, 1].rearrange("p t h k -> p t (h k)"),
                                                    op0=ALU.mult, op1=ALU.add))
                        for t in range(NT):
                            ch(dve.tensor_tensor(gts[:, t], cv[:, t], cv[:, t, :, 0:1].to_broadcast([P, NH, TOPK]), ALU.subtract))
                        dve.sem_inc(ex, 1)
                        dve.wait_ge(exped, 1)
                        for t in range(NT):
                            ch(dve.tensor_reduce(sm[:, t], gts[:, t], AX.X, ALU.add))
                            ch(dve.reciprocal(sm[:, t], sm[:, t]))
                            ch(dve.tensor_tensor(gts[:, t], gts[:, t], sm[:, t].unsqueeze(2).to_broadcast([P, NH, TOPK]), ALU.mult))

                    @block.scalar
                    def _(act):
                        act.wait_ge(ex, 1)
                        self.act_chain.on(act)(act.activation(gts[:, :, :, :], gts[:, :, :, :], ACT.Exp))
                        act.sem_inc(exped, 1)

            NB = 8
            rows = tmp("expert_rows", [P, NB, D])
            cur = tmp("gather_index", [P, NB], U32)
            gb = tmp("ffn_gain", [P, D])
            dots = tmp("expert_products", [P, NB])
            gathered = [self.sem(f"expert_row_gathered{b}") for b in range(NB)]
            used, gained, xready, acted = [self.sem("expert_" + n) for n in ("row_used", "gain_loaded", "input", "activated")]
            kept, started = self.sem("expert_products_kept"), self.sem("gathers_started")
            loops = SLOTS // NB
            with self.block() as block:
                @block.sync
                def _(sp):
                    sp.dma_start(gb[:, :], a["ffn_norm_gain_2"].to_broadcast([P, D])).then_inc(gained, 16)

                @block.gpsimd
                def _(pool):
                    ch_n = self.pool_chain
                    phase = 0
                    pool.sem_inc(used, NB)
                    for t in range(NT):
                        for table in ("expert_u_2", "expert_v_2"):
                            with pool.Fori(0, loops) as i:
                                for b in range(NB):
                                    pool.wait_ge(used, i * NB + (phase * SLOTS + b + 1))
                                    pool.tensor_copy(cur[:, b:b + 1], eidx[:, t, bass.ds(i * NB + b, 1)])\
                                        .then_inc(ch_n.sem, 1)
                                    pool.wait_ge(ch_n.sem, i * NB + (ch_n.n + b + 1))
                                    pool.sem_inc(started, 1)
                                    pool.indirect_dma_start(
                                        out=rows[:, b, :], out_offset=None, in_=a[table][0],
                                        in_offset=bass.IndirectOffsetOnAxis(ap=cur[:, b:b + 1], axis=0))\
                                        .then_inc(gathered[b], 16)
                            ch_n.n += SLOTS
                            phase += 1

                @block.vector
                def _(dve):
                    ch = self.dve_chain.on(dve)
                    phase = 0
                    dve.wait_ge(gained, 16)
                    for t in range(NT):
                        ch(dve.tensor_tensor(self.XN[:, t, :], self.XN[:, t, :], gb[:, :], ALU.mult))
                    for t in range(NT):
                        with dve.Fori(0, loops) as i:
                            for b in range(NB):
                                dve.wait_ge(gathered[b], i * 16 + 16 * (phase * loops + 1))
                                if b == 0:
                                    dve.wait_ge(kept, i + t * loops)
                                dve.tensor_tensor_reduce(rows[:, b, :], rows[:, b, :], self.XN[:, t, :], 1.0, 0.0,
                                                         ALU.mult, ALU.add, dots[:, b:b + 1]).then_inc(used, 1)
                            dve.wait_ge(used, i * NB + (phase * SLOTS + 2 * NB))
                            dve.tensor_copy(wts[:, t, bass.ds(i * NB, NB)], dots[:, :]).then_inc(kept, 1)
                        phase += 1
                        dve.sem_inc(xready, 1)
                        dve.wait_ge(acted, t + 1)
                        ch(dve.tensor_tensor(wts[:, t, :], wts[:, t, :], gts[:, t].rearrange("p h k -> p (h k)"), ALU.mult))
                        with dve.Fori(0, loops) as i:
                            for b in range(NB):
                                dve.wait_ge(gathered[b], i * 16 + 16 * (phase * loops + 1))
                                dve.wait_ge(used, i * NB + (phase * SLOTS + NB + b))
                                dve.scalar_tensor_tensor(out=self.X[:, t, :], in0=rows[:, b, :],
                                                         scalar=wts[:, t, bass.ds(i * NB + b, 1)],
                                                         in1=self.X[:, t, :], op0=ALU.mult, op1=ALU.add).then_inc(used, 1)
                        phase += 1

                @block.scalar
                def _(act):
                    for t in range(NT):
                        act.wait_ge(xready, t + 1)
                        act.wait_ge(kept, loops * (t + 1))
                        self.act_chain.on(act)(act.activation(wts[:, t, :], wts[:, t, :], ACT.Gelu_apprx_tanh))
                        act.sem_inc(acted, 1)

    def copy_out(self, eng, to, src):
        return eng.activation(to, src, ACT.Copy) if eng is self.nc.scalar else eng.tensor_copy(to, src)

    def add_out(self, eng, t, c, ps):
        x = self.X[:, t, bass.ds(c * BANK, BANK)]
        return eng.tensor_tensor(x, ps, x, ALU.add)

    def ple(self, w_gate):
        nc, a = self.nc, self.a
        with ExitStack() as ctx:
            tmp = lambda n, s: ctx.enter_context(nc.sbuf_tensor(n, s, F32))
            gate = tmp("ple_gate", [P, NT, D])
            pin = tmp("ple_in", [P, NT, T])
            pT = tmp("ple_in_turned", [P, 2, T])
            wp = tmp("ple_proj", [P, 2, D])
            loaded, ready, done, stored = [self.sem("ple_" + n) for n in ("loaded", "product", "gated", "stored")]
            self.linear(w_gate, None, self.hT[:, :, :], KD, BANK,
                        lambda eng, t, c, ps: eng.activation(gate[:, t, bass.ds(c * BANK, BANK)], ps, ACT.Sigmoid),
                        ("act", "act"))
            with self.block() as block:
                @block.sync
                def _(sp):
                    sp.dma_start(pin[:, :, :], a["p_2"][0, 0].rearrange("(t p) c -> p t c", p=P)).then_inc(loaded, 16)
                    sp.dma_start(wp[:, :, :], a["w_ple_proj_2"][0].rearrange("(k p) n -> p k n", p=P)).then_inc(loaded, 16)
                    sp.wait_ge(loaded, 32)
            self.turn_stage(self.feature_jobs(lambda t: pin[:, t, :], pT[:, :, :], 2, None))
            with self.block() as block:
                @block.tensor
                def _(pe):
                    for t in range(NT):
                        for c in range(4):
                            for k in range(2):
                                last = pe.matmul(self.bank(4 * t + c), pT[:, k, t * P:(t + 1) * P],
                                                 wp[:, k, c * BANK:(c + 1) * BANK], start=(k == 0), stop=(k == 1))
                        last.then_inc(ready, 1)

                @block.vector
                def _(dve):
                    ch = self.dve_chain.on(dve)
                    for t in range(NT):
                        dve.wait_ge(ready, t + 1)
                        ch(dve.tensor_tensor(gate[:, t, :], self.psum[:, 4 * t * BANK:4 * (t + 1) * BANK], gate[:, t, :], ALU.mult))
                        ch(dve.tensor_tensor(self.X[:, t, :], self.X[:, t, :], gate[:, t, :], ALU.add))
                        dve.sem_inc(done, 1)

                @block.sync
                def _(sp):
                    o = self.out[0].rearrange("(t p) c -> p t c", p=P)
                    for t in range(NT):
                        sp.wait_ge(done, t + 1)
                        sp.dma_start(o[:, t, :], self.X[:, t, :]).then_inc(stored, 16)
                    sp.wait_ge(stored, 16 * NT)

    def run(self):
        nc, a = self.nc, self.a
        w = lambda name: a[name][0]
        kview = lambda name: w(name).rearrange("(k p) n -> p k n", p=P)
        gate, up, down = kview("w_ffn_gate"), kview("w_ffn_up"), kview("w_ffn_down")
        uq, ukv = kview("w_uq_2"), kview("w_ukv_2")
        WI, WI2, WQ = 450, 352, 384
        s_in = Stream(wide(w("w_in"), WI), (8, WI), W_IN_COLS // (2 * WI))
        s_out = Stream(wide(w("w_out"), BANK), (8, BANK), 2)
        s_up = Stream(lambda i, j: (gate if j < 2 else up)[:, 8 * (j % 2):8 * (j % 2) + 8, bass.ds(i * BANK, BANK)],
                      (8, BANK), D_FF // BANK)
        s_down = Stream(lambda i, j: down[:, bass.ds(i * 8 + 2 * j, 2), :], (2, D), 6, last=2)
        s_in2 = Stream(wide(w("w_in_2"), WI2), (8, WI2), IN2_COLS // (2 * WI2))
        s_uq = Stream(lambda i, j: uq[:, :, j * WQ:(j + 1) * WQ], (4, WQ), 1)
        s_ukv = Stream(lambda i, j: ukv[:, :, j * BANK:(j + 1) * BANK], (4, BANK), 1)
        s_out2 = Stream(wide(w("w_out_2"), BANK), (8, BANK), 2)
        s_pq = Stream(wide(w("w_pq_2"), BANK), (8, BANK), 2)
        s_ple = Stream(wide(w("w_ple_gate_2"), BANK), (8, BANK), 2)
        to = lambda dst, width: (lambda eng, t, c, ps: self.copy_out(eng, dst[:, t, bass.ds(c * width, width)], ps))
        X, hT = self.X, self.hT[:, :, :]
        resid = lambda t: X[:, t, :]

        self.setup(s_in)
        self.norm_turn(resid, 1, D, hT, G_MIX)
        with ExitStack() as ctx:
            PR = ctx.enter_context(nc.sbuf_tensor("projections", [P, NT, W_IN_COLS], F32))
            M = ctx.enter_context(nc.sbuf_tensor("mixed", [P, NT, D], F32))
            self.linear(s_in, s_out, hT, KD, WI, to(PR, WI), ("act", "dve"))
            self.nsa(PR, M)
            self.sticks(PR, M)
            self.conv(PR, M)
            self.sgu(PR, M)
            self.norm_turn(lambda t: M[:, t, :], 4, BANK, hT, G_GROUP)
        self.linear(s_out, s_up, hT, KD, BANK, self.add_out, ("dve", "dve"))
        self.norm_turn(resid, 1, D, hT, G_FFN)
        self.ffn((s_up, s_down), s_in2)
        self.norm_turn(resid, 1, D, hT, G_MIX2)
        with ExitStack() as ctx:
            Z = ctx.enter_context(nc.sbuf_tensor("projections2", [P, NT, IN2_COLS], F32))
            Q = ctx.enter_context(nc.sbuf_tensor("queries", [P, NT, NH * QKH], F32))
            self.linear(s_in2, s_uq, hT, KD, WI2, to(Z, WI2), ("act", "dve"))
            self.norm_turn(lambda t: Z[:, t, Q_OFF:KV_OFF], 1, 512, hT[:, 0:4, :], G_QLAT)
            self.linear(s_uq, s_ukv, hT, 4, WQ, to(Q, WQ), ("act", "dve"))
            self.norm_turn(lambda t: Z[:, t, KV_OFF:ROPE_OFF], 1, 512, hT[:, 0:4, :], G_KVLAT)
            with ExitStack() as c2:
                KV = c2.enter_context(nc.sbuf_tensor("keys_values", [P, NT, D], F32))
                self.linear(s_ukv, s_out2, hT, 4, BANK, to(KV, BANK), ("act", "dve"))
                M = Z[:, :, 0:D]
                self.mixers2(Z, Q, KV)
        self.linear(s_out2, s_pq, hT, KD, BANK, self.add_out, ("dve", "dve"))
        self.norm_turn(resid, 1, D, hT, G_FFN2)
        self.peer(s_ple, s_pq)
        self.norm_turn(resid, 1, D, hT, G_PLE)
        self.ple(s_ple)

    def mixers2(self, Z, Q, KV):
        self.mla(Q[:, :, :], KV[:, :, :], Z[:, :, ROPE_OFF:IN2_COLS], Z[:, :, 0:D])
        self.pool_mix(Z, Z[:, :, 0:D])
        src = lambda t: Z[:, t, 0:D]
        self.turn_stage(self.feature_jobs(src, self.hT[:, :, :], 8, G_POOL)
                        + self.feature_jobs(lambda t: Z[:, t, POOL_W:D], self.hT[:, 8:16, :], 8, None))


_INS = ["x", "w_in", "w_out", "norm_mix", "norm_ffn", "q_gain", "k_gain", "cmp_pos", "cmp_w1", "cmp_w2", "rel_table",
        "conv_w", "sgu_w", "sgu_b", "group_gain", "w_ffn_gate", "w_ffn_up", "w_ffn_down", "p_2", "positions_2",
        "mix_norm_gain_2", "w_in_2", "w_pool_2", "pool_scale_2", "q_lat_gain_2", "kv_lat_gain_2", "w_uq_2", "w_ukv_2",
        "q_norm_gain_2", "k_norm_gain_2", "w_out_2", "ffn_norm_gain_2", "w_pq_2", "sub_k1_2", "sub_k2_2",
        "expert_u_2", "expert_v_2", "ple_norm_gain_2", "w_ple_gate_2", "w_ple_proj_2"]


def kernel(**inputs):
    import concourse.bacc as bacc
    from concourse.bass_utils import run_bass_kernel_spmd

    nc = bacc.Bacc("TRN2", target_bir_lowering=False, num_devices=1)
    arrays, args = {}, {}
    for name in _INS:
        v = np.ascontiguousarray(inputs[name])
        arrays["in_" + name] = v
        args[name] = nc.dram_tensor("in_" + name, v.shape, mybir.dt.from_np(v.dtype), kind="ExternalInput").ap()
    out = nc.dram_tensor("out", (1, T, D), F32, kind="ExternalOutput").ap()
    Kernel(nc, args, out).run()
    return run_bass_kernel_spmd(nc, [arrays], core_ids=[0]).results[0]["out"]
```

```python
import concourse.bass as bass
from concourse import mybir
from contextlib import ExitStack
import math
import numpy as np

F32 = mybir.dt.float32
F32R = mybir.dt.float32r
I32 = mybir.dt.int32
U32 = mybir.dt.uint32
ALU = mybir.AluOpType
ACT = mybir.ActivationFunctionType
AX = mybir.AxisListType

P = 128
T = 256
NT = T // P
D = 2048
KD = D // P
BANK = 512

HD = 64
NH = 8
NG = 2
W_IN_COLS = 5400
A_KV = 512
A_GATE = 1280
B_OFF = 1304
C_OFF = B_OFF + 1536
D_OFF = C_OFF + 1024
D_FF = 5632
KF = D_FF // P
CMP_LEN, CMP_STRIDE = 32, 16
N_CMP = (T - CMP_LEN) // CMP_STRIDE + 1
N_CMP0 = (P - CMP_LEN) // CMP_STRIDE + 1
NEG = -1.0e30

POOL_W = 1024
WINDOWS = (2, 4, 8, 16)
Q_OFF, KV_OFF, ROPE_OFF = 1024, 1536, 2048
IN2_COLS = 2112
QKH = 192
TOPK = 16
NKEYS = 128
SLOTS = NH * TOPK
HALF = 32

G_MIX, G_FFN, G_MIX2, G_FFN2, G_PLE, G_GROUP = 0, 16, 32, 48, 64, 80
G_POOL, G_QLAT, G_KVLAT = 96, 104, 108
G_Q, G_K, G_QN, G_KN, G_SGUB = 112, 113, 114, 115, 116
G_ROWS = 124


def place(h):
    return h % 2 * (NH // 2) + h // 2


def rel_buckets():
    n = np.arange(T)
    nf = np.maximum(n, 1).astype(np.float32)
    large = 16 + (np.log(nf / np.float32(16)) / np.float32(math.log(64)) * np.float32(16)).astype(np.int32)
    return np.where(n < 16, n, np.minimum(large, 31))


class Signal:

    def __init__(self, nc, name):
        self.sem, self.total = nc.alloc_semaphore(name), 0

    def at(self, k):
        return k + self.total

    def close(self, n):
        self.total += n


class Chain:

    def __init__(self, nc, name):
        self.sem, self.n, self.eng = nc.alloc_semaphore(name), 0, None

    def on(self, eng):
        self.eng = eng
        return self

    def __call__(self, ins):
        self.n += 1
        ins.then_inc(self.sem, 1)
        self.eng.wait_ge(self.sem, self.n)


class Stream:

    def __init__(self, source, view, rounds, last=4):
        self.source, self.view, self.rounds, self.last = source, view, rounds, last


class Ring:

    SLOTS = 4
    WORDS = 4096
    PIECE = 2048

    def __init__(self, nc):
        self.nc = nc
        self.buf = nc.alloc_sbuf_tensor("weights", [P, self.SLOTS, self.WORDS], F32)
        self.ready = [nc.alloc_semaphore(f"weights_ready{j}") for j in range(self.SLOTS)]
        self.hi_ready = nc.alloc_semaphore("weights_hi_ready")
        self.lo_ready = nc.alloc_semaphore("weights_lo_ready")
        self.used = nc.alloc_semaphore("weights_used")
        self.fills = 0
        self.base = [0] * self.SLOTS
        self.scopes = 0

    def parts(self, ctx):
        self.scopes += 1
        sb = lambda n: ctx.enter_context(self.nc.sbuf_tensor(f"weights_{n}{self.scopes}", [P, 2, self.PIECE], F32R))
        self.hi, self.lo = sb("hi"), sb("lo")

    def raw(self, j, stream):
        k, n = stream.view
        return self.buf[:, j, 0:k * n].rearrange("p (k n) -> p k n", k=k)

    def piece(self, buf, half, stream):
        k, n = stream.view
        return buf[:, half, 0:k // 2 * n].rearrange("p (k n) -> p k n", k=k // 2)

    def fill(self, sp, stream, i, j, fills, wait=True):
        if wait:
            sp.wait_ge(self.lo_ready, i * 8 + 2 * (fills + j - 3))
        sp.dma_start(self.raw(j, stream), stream.source(i, j)).then_inc(self.ready[j], 16)

    def rest(self, sp, stream, following):
        if stream.rounds > 2:
            with sp.Fori(1, stream.rounds - (stream.last < 4)) as i:
                for j in range(4):
                    self.fill(sp, stream, i, j, self.fills)
            if stream.last < 4:
                for j in range(stream.last):
                    self.fill(sp, stream, stream.rounds - 1, j, self.fills)
        else:
            for i in range(1, stream.rounds):
                for j in range(4):
                    self.fill(sp, stream, i, j, self.fills)
        if following is not None:
            after = self.fills + 4 * stream.rounds
            for j in range(4):
                self.fill(sp, following, 0, j, after)

    def split_hi(self, act, stream, i, j, half, skip=0):
        if half == 0:
            act.wait_ge(self.ready[j], i * 16 + (self.base[j] + 16))
        act.wait_ge(self.used, i * 8 + (2 * (self.fills + j) + half + 1))
        k = stream.view[0] // 2
        act.activation(self.piece(self.hi, half, stream), self.raw(j, stream)[:, half * k:half * k + k], ACT.Copy)\
            .then_inc(self.hi_ready, 1 + skip)

    def split_lo(self, dve, stream, i, j, half, skip=0):
        dve.wait_ge(self.hi_ready, i * 8 + (2 * (self.fills + j) + half + 1))
        k = stream.view[0] // 2
        dve.tensor_tensor(self.piece(self.lo, half, stream), self.raw(j, stream)[:, half * k:half * k + k],
                          self.piece(self.hi, half, stream).bitcast(F32), ALU.subtract).then_inc(self.lo_ready, 1 + skip)

    def wait(self, pe, i, j, half):
        pe.wait_ge(self.lo_ready, i * 8 + (2 * (self.fills + j) + half + 1))

    def done(self, i, pieces):
        return i * 8 + (2 * self.fills + pieces + 2)

    def close(self, stream):
        for j in range(4):
            self.base[j] += 16 * (stream.rounds - (j >= stream.last))
        self.fills += 4 * stream.rounds


def wide(w, width, halves=2):
    v = w.rearrange("(k p) n -> p k n", p=P)
    return lambda i, j: v[:, 8 * (j % 2):8 * (j % 2) + 8, bass.ds((i * 2 + j // 2) * width, width)]


class Kernel:
    def __init__(self, nc, a, out):
        self.nc, self.a, self.out = nc, a, out
        sb, ps = nc.alloc_sbuf_tensor, nc.alloc_psum_tensor
        self.X = sb("residual", [P, NT, D], F32)
        self.XN = sb("normed", [P, NT, D], F32)
        self.ident = sb("identity", [P, P], F32)
        self.gT = sb("gains", [P, G_ROWS], F32)
        self.ring = Ring(nc)
        self.psum = ps("banks", [P, 8 * BANK], F32)
        self.bank_free = [Signal(nc, f"product_bank_free{t}") for t in range(NT)]
        self.turned = Signal(nc, "transposes_done")
        self.turned_read = {e: Signal(nc, f"transposes_read_{e}") for e in ("act", "dve")}
        self.squares = Signal(nc, "squares_summed")
        self.rstd_ready = Signal(nc, "rstd_ready")
        self.scaled = {e: Signal(nc, f"scaled_{e}") for e in ("act", "dve")}
        self.act_chain, self.dve_chain = Chain(nc, "act_chain"), Chain(nc, "dve_chain")
        self.pool_chain, self.sp_chain = Chain(nc, "pool_chain"), Chain(nc, "loads")
        self.scopes = 0
        self.minus_half = sb("minus_half", [P, 32], F32)
        self.stat = sb("statistics", [P, 32], F32)
        self.rstd = sb("rstd", [P, 32], F32)
        self.att = sb("attention_statistics", [P, 4, NT, NH], F32)

    def bank(self, b, n=BANK, off=0):
        return self.psum[:, b * BANK + off:b * BANK + off + n]

    def sem(self, name):
        return self.nc.alloc_semaphore(name)

    def block(self):
        return self.nc.Block()

    def rstd_on_pool(self, pool, n, count, extra=1.0, eps=1e-6):
        ch = self.pool_chain.on(pool)
        st, rs = self.stat[:, 0:count], self.rstd[:, 0:count]
        ch(pool.tensor_scalar(st, st, 1.0 / n, eps, ALU.mult, ALU.add))
        ch(pool.tensor_tensor(out=rs, in0=st, in1=self.minus_half[:, 0:count], op=ALU.pow))
        if extra != 1.0:
            ch(pool.tensor_scalar(rs, rs, extra, 0.0, ALU.mult, ALU.add))

    def turn(self, jobs, pe, act, dve, start=None):
        tr, rd = self.turned, self.turned_read
        for j, (ins, dst, gains) in enumerate(jobs):
            b = 4 + j % 4
            reader, k = ("act", "dve")[j % 2], j // 2 + 1
            if pe is not None:
                if j >= 4:
                    pe.wait_ge(rd[reader].sem, rd[reader].at(k - 2))
                off = 0
                for n, i in enumerate(ins):
                    pin, f = i.shape[0], i.shape[1] if len(i.shape) == 2 else int(np.prod(i.shape[1:]))
                    last = pe.transpose(self.psum[0:f, b * BANK + off:b * BANK + off + pin], i,
                                        self.ident[0:pin, 0:pin])
                    off += pin
                last.then_inc(tr.sem, 1)
                continue
            if (act is None) == (reader == "act"):
                continue
            eng = act if act is not None else dve
            eng.wait_ge(tr.sem, tr.at(j + 1))
            rows = dst.shape[0]
            size = int(np.prod(dst.shape[1:]))
            parts = gains or [(size, None)]
            flat = dst if len(dst.shape) == 2 else dst.rearrange("p a b -> p (a b)")
            off = 0
            for n, gain in parts:
                src, to = self.psum[0:rows, b * BANK + off:b * BANK + off + n], flat[:, off:off + n]
                if act is not None:
                    last = eng.activation(to, src, ACT.Copy, scale=1.0 if gain is None else gain)
                elif gain is None:
                    last = eng.tensor_copy(to, src)
                else:
                    last = eng.tensor_scalar(to, src, gain, None, ALU.mult)
                off += n
            last.then_inc(rd[reader].sem, 1)

    def turn_close(self, jobs):
        n = len(jobs)
        self.turned.close(n)
        self.turned_read["act"].close((n + 1) // 2)
        self.turned_read["dve"].close(n // 2)

    def gain(self, row, scale_rows=P):
        return self.gT[0:scale_rows, row:row + 1]

    def turn_stage(self, jobs):
        with self.block() as block:
            @block.tensor
            def _(pe):
                self.turn(jobs, pe, None, None)

            @block.scalar
            def _(act):
                self.turn(jobs, None, act, None)

            @block.vector
            def _(dve):
                self.turn(jobs, None, None, dve)
        self.turn_close(jobs)

    def feature_jobs(self, src, dst, kc):
        jobs = []
        for k in range(0, kc, 2):
            ins = [src(t)[:, kk * P:(kk + 1) * P] for kk in (k, k + 1) for t in range(NT)]
            jobs.append((ins, dst[:, k:k + 2, :], None))
        return jobs

    def features(self, ctx, kc):
        self.scopes += 1
        return [ctx.enter_context(self.nc.sbuf_tensor(f"features_{n}{self.scopes}", [P, kc, T], F32R)) for n in ("hi", "lo")]

    def turn_split(self, src, hT, gains, pe, act, dve):
        tr, rd = self.turned, self.turned_read
        hi, lo = hT
        for j in range(len(gains) // 2):
            b = 4 + j % 4
            if pe is not None:
                if j >= 4:
                    pe.wait_ge(rd["dve"].sem, rd["dve"].at(j - 3))
                for i in range(2):
                    for t in range(NT):
                        last = pe.transpose(self.bank(b, P, i * T + t * P), src(t, 2 * j + i), self.ident[:, :])
                last.then_inc(tr.sem, 1)
                continue
            if act is not None:
                act.wait_ge(tr.sem, tr.at(j + 1))
            else:
                dve.wait_ge(rd["act"].sem, rd["act"].at(j + 1))
            for i in range(2):
                k, g = 2 * j + i, gains[2 * j + i]
                ps = self.bank(b, T, i * T)
                if act is not None:
                    last = act.activation(hi[:, k, :], ps, ACT.Copy, scale=1.0 if g is None else g)
                else:
                    last = dve.scalar_tensor_tensor(out=lo[:, k, :], in0=ps, scalar=1.0 if g is None else g,
                                                    in1=hi[:, k, :].bitcast(F32), op0=ALU.mult, op1=ALU.subtract)
            last.then_inc(rd["act" if act is not None else "dve"].sem, 1)

    def turn_split_close(self, gains):
        for s in (self.turned, self.turned_read["act"], self.turned_read["dve"]):
            s.close(len(gains) // 2)

    def gains_of(self, row, kc):
        return [None if row is None else self.gain(row + k) for k in range(kc)]

    def turn_split_stage(self, src, hT, gains):
        with self.block() as block:
            @block.tensor
            def _(pe):
                self.turn_split(src, hT, gains, pe, None, None)

            @block.scalar
            def _(act):
                self.turn_split(src, hT, gains, None, act, None)

            @block.vector
            def _(dve):
                self.turn_split(src, hT, gains, None, None, dve)
        self.turn_split_close(gains)

    def norm_turn(self, src, groups, n, hT, grow):
        sq, rs, sc = self.squares, self.rstd_ready, self.scaled
        kc = groups * n // P
        gains = self.gains_of(grow, kc)
        turned = lambda t, k: self.XN[:, t, k * P:(k + 1) * P]
        with self.block() as block:
            @block.scalar
            def _(act):
                for g in range(groups):
                    last = act.activation(self.XN[:, 0, g * n:(g + 1) * n], src(0, g), ACT.Square,
                                          accum_out=self.stat[:, g:g + 1])
                last.then_inc(sq.sem, 1)
                act.wait_ge(rs.sem, rs.at(1))
                for g in range(groups):
                    last = act.activation(self.XN[:, 0, g * n:(g + 1) * n], src(0, g), ACT.Copy,
                                          scale=self.rstd[:, g:g + 1])
                last.then_inc(sc["act"].sem, 1)
                self.turn_split(turned, hT, gains, None, act, None)

            @block.gpsimd
            def _(pool):
                pool.wait_ge(sq.sem, sq.at(2))
                self.rstd_on_pool(pool, n, NT * groups)
                pool.sem_inc(rs.sem, 1)

            @block.vector
            def _(dve):
                for g in range(groups):
                    last = dve.tensor_tensor_reduce(self.XN[:, 1, g * n:(g + 1) * n], src(1, g), src(1, g), 1.0, 0.0,
                                                    ALU.mult, ALU.add, self.stat[:, groups + g:groups + g + 1])
                last.then_inc(sq.sem, 1)
                dve.wait_ge(rs.sem, rs.at(1))
                for g in range(groups):
                    c = groups + g
                    last = dve.tensor_scalar(self.XN[:, 1, g * n:(g + 1) * n], src(1, g),
                                             self.rstd[:, c:c + 1], None, ALU.mult)
                last.then_inc(sc["dve"].sem, 1)
                self.turn_split(turned, hT, gains, None, None, dve)

            @block.tensor
            def _(pe):
                pe.wait_ge(sc["act"].sem, sc["act"].at(1))
                pe.wait_ge(sc["dve"].sem, sc["dve"].at(1))
                self.turn_split(turned, hT, gains, pe, None, None)
        sq.close(2)
        for s in (rs, sc["act"], sc["dve"]):
            s.close(1)
        self.turn_split_close(gains)

    def passes(self, pe, out, xh, xl, wh, wl, first, last_one):
        pe.matmul(out, xh, wh, start=first, stop=False)
        pe.matmul(out, xh, wl, start=False, stop=False)
        return pe.matmul(out, xl, wh, start=False, stop=last_one)

    def linear(self, stream, following, hT, kc, width, evac, on):
        ring = self.ring
        per = 2 if kc == KD else 4
        fpc = 4 // per
        kp = kc // fpc // 2
        rounds = stream.rounds
        hi, lo = hT

        def rounds_of(eng, body):
            body(0, True)
            if rounds > 2:
                with eng.Fori(1, rounds) as i:
                    body(i, False)
            else:
                for i in range(1, rounds):
                    body(i, False)

        with ExitStack() as ctx:
            ring.parts(ctx)
            with self.block() as block:
                @block.sync
                def _(sp):
                    ring.rest(sp, stream, following)

                @block.tensor
                def _(pe):
                    def body(i, first):
                        for c in range(per):
                            for t in range(NT):
                                pe.wait_ge(self.bank_free[t].sem, i * per + self.bank_free[t].at(c + 1))
                            for f in range(fpc):
                                for half in range(2):
                                    j, q = c * fpc + f, 2 * f + half
                                    ring.wait(pe, i, j, half)
                                    wh, wl = ring.piece(ring.hi, half, stream), ring.piece(ring.lo, half, stream)
                                    for k in range(kp):
                                        for t in range(NT):
                                            x = (q * kp + k, slice(t * P, (t + 1) * P))
                                            last = self.passes(pe, self.bank(2 * (c % 2) + t, width),
                                                               hi[:, x[0], x[1]], lo[:, x[0], x[1]],
                                                               wh[:, k, :], wl[:, k, :],
                                                               q == 0 and k == 0, q == 2 * fpc - 1 and k == kp - 1)
                                    last.then_inc(ring.used, 1)
                    rounds_of(pe, body)

                def worker(name, split):
                    def program(eng):
                        def leave(i, c):
                            if c < 0:
                                i, c = i - 1, per - 1
                            eng.wait_ge(ring.used, ring.done(i, 2 * fpc * (c + 1)))
                            for t in range(NT):
                                if on[t] == name:
                                    evac(eng, t, i * per + c, self.bank(2 * (c % 2) + t, width))\
                                        .then_inc(self.bank_free[t].sem, 1)

                        def body(i, first):
                            for c in range(per):
                                for f in range(fpc):
                                    for half in range(2):
                                        split(eng, stream, i, c * fpc + f, half)
                                    if f == 0 and not (first and c == 0) and name in on:
                                        leave(i, c - 1)
                        rounds_of(eng, body)
                        if name in on:
                            leave(rounds - 1, per - 1)
                    return program

                block.scalar(worker("act", ring.split_hi))
                block.vector(worker("dve", ring.split_lo))
        for t in range(NT):
            self.bank_free[t].close(rounds * per)
        ring.close(stream)

    def setup(self, first):
        a, nc = self.a, self.nc
        sb = nc.alloc_sbuf_tensor
        self.tri = sb("later_keys", [P, P], F32)
        self.ones = sb("ones", [P, P], F32)
        self.cosT = sb("cos", [P, NT, HALF], F32)
        self.sinT = sb("sin", [P, NT, HALF], F32)
        self.gbq = sb("rope_gain_q", [P, 64], F32)
        self.gbk = sb("rope_gain_k", [P, 64], F32)
        g = {}
        with ExitStack() as ctx:
            tmp = lambda n, s, d=F32: ctx.enter_context(nc.sbuf_tensor(n, s, d))
            gin = tmp("gains_in", [P, P])
            posi = tmp("positions", [P, NT], I32)
            posf = tmp("positions_f", [P, NT])
            freq = tmp("frequencies", [P, HALF])
            ang = tmp("angles", [P, 2, NT, HALF])
            turns = tmp("whole_turns", [P, 2, NT, HALF])
            loaded, made, cast = self.sem("small_loaded"), self.sem("constants_made"), self.sem("angles_ready")
            turned, kept = self.sem("gains_turned"), self.sem("gains_kept")
            rows = [(a["norm_mix"], G_MIX, 16), (a["norm_ffn"], G_FFN, 16), (a["mix_norm_gain_2"], G_MIX2, 16),
                    (a["ffn_norm_gain_2"], G_FFN2, 16), (a["ple_norm_gain_2"], G_PLE, 16),
                    (a["group_gain"], G_GROUP, 16), (a["pool_scale_2"], G_POOL, 8),
                    (a["q_lat_gain_2"], G_QLAT, 4), (a["kv_lat_gain_2"], G_KVLAT, 4)]
            inv = (np.float32(10000.0) ** (-np.arange(0, 64, 2, dtype=np.float32) / np.float32(64))).astype(np.float32)

            with self.block() as block:
                @block.sync
                def _(sp):
                    xv = a["x"][0].rearrange("(t p) c -> p t c", p=P)
                    sp.dma_start(self.X[:, :, :], xv).then_inc(loaded, 16)
                    for j in range(4):
                        self.ring.fill(sp, first, 0, j, 0, wait=False)

                @block.scalar
                def _(act):
                    n = 0
                    for src, r, k in rows:
                        act.dma_start(gin[r:r + k, :], src[0].rearrange("(k p) -> k p", p=P)).then_inc(loaded, 16)
                    for src, r in ((a["q_gain"], G_Q), (a["k_gain"], G_K)):
                        for h in range(2):
                            act.dma_start(gin[r:r + 1, 64 * h:64 * h + 64], src).then_inc(loaded, 16)
                    for src, r in ((a["q_norm_gain_2"], G_QN), (a["k_norm_gain_2"], G_KN)):
                        act.dma_start(gin[r:r + 1, :], src[:, 0:P]).then_inc(loaded, 16)
                    act.dma_start(gin[G_SGUB:G_SGUB + NH, :], a["sgu_b"][0]).then_inc(loaded, 16)
                    for src, to in ((a["q_norm_gain_2"], self.gbq), (a["k_norm_gain_2"], self.gbk)):
                        act.dma_start(to[:, :], src[:, P:QKH].to_broadcast([P, 64])).then_inc(loaded, 16)
                    act.dma_start(posi[:, :], a["positions_2"].rearrange("o (t p) -> p (o t)", p=P),
                                  allow_slow_non_contiguous=True).then_inc(loaded, 16)
                    act.wait_ge(loaded, 16 * (1 + len(rows) + 4 + 2 + 1 + 2 + 1))
                    act.wait_ge(cast, 1)
                    act.activation(self.sinT[:, :, :], ang[:, 0, :, :], ACT.Sin)
                    act.activation(self.cosT[:, :, :], ang[:, 1, :, :], ACT.Sin)

                @block.gpsimd
                def _(pool):
                    ch = self.pool_chain.on(pool)
                    pool.memset(self.minus_half[:, :], -0.5)
                    pool.memset(self.ones[:, :], 1.0)
                    ch(pool.memset(self.ident[:, :], 0.0))
                    ch(pool.affine_select(out=self.ident[:, :], in_=self.ident[:, :], pattern=[[-1, P]],
                                          compare_op=ALU.not_equal, fill=1.0, base=0, channel_multiplier=1))
                    ch(pool.affine_select(out=self.tri[:, :], in_=self.ones[:, :], pattern=[[-1, P]],
                                          compare_op=ALU.is_gt, fill=0.0, base=0, channel_multiplier=1))
                    for k in range(HALF):
                        last = pool.memset(freq[:, k:k + 1], float(inv[k]))
                    ch(last)
                    pool.sem_inc(made, 1)

                @block.tensor
                def _(pe):
                    pe.wait_ge(loaded, 16 * 20)
                    pe.wait_ge(made, 1)
                    pe.transpose(self.bank(0, G_ROWS), gin[0:G_ROWS, :], self.ident[0:G_ROWS, 0:G_ROWS])\
                        .then_inc(turned, 1)

                @block.vector
                def _(dve):
                    ch = self.dve_chain.on(dve)
                    dve.wait_ge(loaded, 16 * 20)
                    dve.wait_ge(made, 1)
                    ch(dve.tensor_copy(posf[:, :], posi[:, :]))
                    for t in range(NT):
                        last = dve.tensor_scalar(ang[:, 0, t, :], freq[:, :], posf[:, t:t + 1], None, ALU.mult)
                    ch(last)
                    magic = 1.5 * 2.0 ** 23
                    two_pi = 2 * math.pi
                    c1 = 6.28125
                    c2 = float(np.float32(two_pi - c1))
                    c2 = float(np.frombuffer((np.frombuffer(np.float32(c2).tobytes(), np.uint32) & 0xFFFFF000)
                                             .astype(np.uint32).tobytes(), np.float32)[0])
                    c3 = float(np.float32(two_pi - c1 - c2))
                    ch(dve.tensor_scalar(turns[:, 0], ang[:, 0], 1.0 / two_pi, magic, ALU.mult, ALU.add))
                    ch(dve.tensor_scalar(turns[:, 1], ang[:, 0], 1.0 / two_pi, 0.25, ALU.mult, ALU.add))
                    ch(dve.tensor_scalar(turns[:, 1], turns[:, 1], magic, None, ALU.add))
                    ch(dve.tensor_scalar(turns[:, :], turns[:, :], magic, None, ALU.subtract))
                    ch(dve.tensor_copy(ang[:, 1], ang[:, 0]))
                    flat = lambda x: x[:, :, :, :].rearrange("p a t k -> p (a t k)")
                    for c in (c1, c2, c3):
                        ch(dve.scalar_tensor_tensor(out=flat(ang), in0=flat(turns), scalar=-c, in1=flat(ang),
                                                    op0=ALU.mult, op1=ALU.add))
                    ch(dve.tensor_scalar(ang[:, 1], ang[:, 1], math.pi / 2, None, ALU.add))
                    edge = 3.1415925
                    ch(dve.tensor_scalar(ang[:, :], ang[:, :], edge, -edge, ALU.min, ALU.max))
                    dve.sem_inc(cast, 1)
                    dve.wait_ge(turned, 1)
                    ch(dve.tensor_copy(self.gT[:, :], self.bank(0, G_ROWS)))
                    ch(dve.tensor_scalar(self.gT[:, G_Q:G_Q + 1], self.gT[:, G_Q:G_Q + 1], HD ** -0.5, None, ALU.mult))
                    for t in range(NT):
                        dve.sem_inc(self.bank_free[t].sem, 2)
                    dve.sem_inc(self.ring.used, 2)

    def conv(self, PR):
        nc = self.nc
        with ExitStack() as ctx:
            tmp = lambda n, s: ctx.enter_context(nc.sbuf_tensor(n, s, F32))
            z = tmp("conv_z", [P, 3, NT, BANK])
            cw = tmp("conv_weights", [P, 3, BANK])
            y = tmp("conv_part", [P, NT, BANK])
            gated, zeros, moved = self.sem("conv_gated"), self.sem("conv_zeros"), self.sem("conv_moved")
            out = z[:, 2]
            with self.block() as block:
                @block.gpsimd
                def _(pool):
                    self.pool_chain.on(pool)(pool.memset(z[0:2, 1:3, 0, :], 0.0))
                    pool.sem_inc(zeros, 1)

                @block.sync
                def _(sp):
                    sp.dma_start(cw[:, :, :], self.a["conv_w"].rearrange("o k c -> o (k c)")
                                 .to_broadcast([P, 3 * BANK]).rearrange("p (k c) -> p k c", k=3)).then_inc(moved, 16)
                    sp.wait_ge(gated, 1)
                    sp.wait_ge(zeros, 1)
                    for s in (1, 2):
                        sp.dma_start(z[s:P, s, :, :], z[0:P - s, 0, :, :]).then_inc(moved, 16)
                        sp.dma_start(z[0:s, s, 1, :], z[P - s:P, 0, 0, :]).then_inc(moved, 16)
                    sp.wait_ge(moved, 16 * 5)

                @block.vector
                def _(dve):
                    ch = self.dve_chain.on(dve)
                    ch(dve.tensor_tensor(z[:, 0], PR[:, :, B_OFF + 512:B_OFF + 1024],
                                         PR[:, :, B_OFF + 1024:B_OFF + 1536], ALU.mult))
                    dve.sem_inc(gated, 1)
                    w = lambda i: cw[:, i:i + 1, :].to_broadcast([P, NT, BANK])
                    dve.wait_ge(moved, 16 * 5)
                    ch(dve.tensor_tensor(out, z[:, 2], w(0), ALU.mult))
                    ch(dve.tensor_tensor(y[:, :, :], z[:, 1], w(1), ALU.mult))
                    ch(dve.tensor_tensor(out, out, y[:, :, :], ALU.add))
                    ch(dve.tensor_tensor(y[:, :, :], z[:, 0], w(2), ALU.mult))
                    ch(dve.tensor_tensor(out, out, y[:, :, :], ALU.add))
                    b = PR[:, :, B_OFF:B_OFF + 512]
                    ch(dve.tensor_tensor(b, out, b, ALU.mult))

    def sgu(self, PR):
        nc = self.nc
        with ExitStack() as ctx:
            tmp = lambda n, s: ctx.enter_context(nc.sbuf_tensor(n, s, F32))
            w_in = tmp("sgu_w", [P, NH, P])
            wT = tmp("sgu_w_turned", [P, NH, P])
            v = tmp("sgu_v", [P, NT, BANK])
            junk = tmp("sgu_squares", [P, BANK])
            loaded = self.sem("sgu_loaded")
            with self.block() as block:
                @block.sync
                def _(sp):
                    sp.dma_start(w_in[:, :, :], self.a["sgu_w"][0].rearrange("h p q -> p h q")).then_inc(loaded, 16)
                    sp.wait_ge(loaded, 16)
            self.turn_stage([([w_in[:, 4 * b + h, :] for h in range(4)], wT[:, 4 * b:4 * b + 4, :], None)
                             for b in range(2)])
            summed, mean, centred, squared, rs, normed = [self.sem("sgu_" + n) for n in (
                "summed", "mean", "centred", "squared", "rstd", "normed")]
            masked, mixed = self.sem("sgu_masked"), self.sem("sgu_mixed")
            C = PR[:, :, C_OFF:C_OFF + 1024]
            with self.block() as block:
                @block.gpsimd
                def _(pool):
                    ch = self.pool_chain.on(pool)
                    ch(pool.affine_select(out=wT[:, :, :], in_=wT[:, :, :], pattern=[[0, NH], [1, P]],
                                          compare_op=ALU.is_ge, fill=0.0, base=0, channel_multiplier=-1))
                    pool.sem_inc(masked, 1)
                    pool.wait_ge(squared, 1)
                    self.rstd_on_pool(pool, BANK, NT, eps=1e-5)
                    pool.sem_inc(rs, 1)

                @block.scalar
                def _(act):
                    ch = self.act_chain.on(act)
                    ch(act.activation(C[:, :, 0:512], C[:, :, 0:512], ACT.Gelu_apprx_tanh))
                    for t in range(NT):
                        last = act.activation(v[:, t, :], C[:, t, 512:1024], ACT.Gelu_apprx_tanh,
                                              accum_out=self.stat[:, 4 + t:5 + t])
                    ch(last)
                    act.sem_inc(summed, 1)
                    act.wait_ge(centred, 1)
                    for t in range(NT):
                        ch(act.activation(junk[:, :], v[:, t, :], ACT.Square, accum_out=self.stat[:, t:t + 1]))
                    act.sem_inc(squared, 1)

                @block.vector
                def _(dve):
                    ch = self.dve_chain.on(dve)
                    dve.wait_ge(summed, 1)
                    ch(dve.tensor_scalar(self.stat[:, 8:10], self.stat[:, 4:6], 1.0 / BANK, None, ALU.mult))
                    for t in range(NT):
                        last = dve.tensor_scalar(v[:, t, :], v[:, t, :], self.stat[:, 8 + t:9 + t], None, ALU.subtract)
                    ch(last)
                    dve.sem_inc(centred, 1)
                    dve.wait_ge(rs, 1)
                    for t in range(NT):
                        last = dve.tensor_scalar(v[:, t, :], v[:, t, :], self.rstd[:, t:t + 1], None, ALU.mult)
                    ch(last)
                    dve.sem_inc(normed, 1)
                    dve.wait_ge(mixed, 1)
                    bias = self.gT[:, G_SGUB:G_SGUB + NH].unsqueeze(2).to_broadcast([P, NH, HD])
                    for t in range(NT):
                        o = v[:, t, :]
                        ch(dve.tensor_tensor(o.rearrange("p (h d) -> p h d", h=NH),
                                             self.bank(t).rearrange("p (h d) -> p h d", h=NH), bias, ALU.add))
                        ch(dve.tensor_tensor(C[:, t, 0:512], o, C[:, t, 0:512], ALU.mult))

                @block.tensor
                def _(pe):
                    pe.wait_ge(masked, 1)
                    pe.wait_ge(normed, 1)
                    for t in range(NT):
                        for h in range(NH):
                            last = pe.matmul(self.bank(t, HD, h * HD), wT[:, h, :], v[:, t, h * HD:(h + 1) * HD],
                                             start=True, stop=True)
                    last.then_inc(mixed, 1)

    def sticks(self, PR):
        nc = self.nc
        with ExitStack() as ctx:
            tmp = lambda n, s: ctx.enter_context(nc.sbuf_tensor(n, s, F32))
            qT, kT = tmp("stick_q", [P, 4, T]), tmp("stick_k", [P, 4, T])
            n0, n1 = NH * T, NH * P
            Z, L, W = [self.XN[:, :, :].rearrange("p t c -> p (t c)")[:, 0:n0 + n1],
                       tmp("stick_l", [P, n0 + n1])[:, :], tmp("stick_w", [P, n0 + n1])[:, :]]
            self.turn_stage([job for c, dst in ((0, qT), (512, kT)) for job in
                             self.feature_jobs(lambda t, c=c: PR[:, t, D_OFF + c:D_OFF + c + 512], dst[:, :, :], 4)])
            scored, scaled, negd, logd, mask_ready = [self.sem("stick_" + n) for n in (
                "scored", "scaled", "negated", "logs", "masked")]
            sub, tailed, added, exped, amask, mixed = [self.sem("stick_" + n) for n in (
                "log_rest", "tails", "exponents", "weights", "weights_masked", "outputs")]
            allz = self.psum[:, 0:n0 + n1]

            def causal(pool, x):
                for lo, n in ((0, T), (n0, P)):
                    v = x[:, lo:lo + NH * n].rearrange("p (h t) -> p h t", h=NH)
                    last = pool.affine_select(out=v, in_=v, pattern=[[0, NH], [1, n]], compare_op=ALU.is_gt,
                                              fill=0.0, base=0, channel_multiplier=-1)
                return last

            with self.block() as block:
                @block.tensor
                def _(pe):
                    for h in range(NH):
                        r = slice(HD * (h % 2), HD * (h % 2) + HD)
                        s = place(h)
                        pe.matmul(self.psum[:, s * T:(s + 1) * T], kT[r, h // 2, 0:P], qT[r, h // 2, :],
                                  start=True, stop=True)
                        last = pe.matmul(self.psum[:, n0 + s * P:n0 + (s + 1) * P], kT[r, h // 2, P:T],
                                         qT[r, h // 2, P:T], start=True, stop=True)
                    last.then_inc(scored, 1)
                    pe.wait_ge(mask_ready, 1)
                    for h in range(NH):
                        if h % 2 == 0:
                            pe.matmul(self.psum[:, h * T:(h + 2) * T], self.tri[:, :], L[:, h * T:(h + 2) * T],
                                      start=True, stop=False)
                        pe.matmul(self.psum[:, h * T + P:(h + 1) * T], self.ones[:, :],
                                  L[:, n0 + h * P:n0 + (h + 1) * P], start=False, stop=(h % 2 == 1))
                    for b in range(2):
                        last = pe.matmul(self.bank(4 + b), self.tri[:, :], L[:, n0 + b * BANK:n0 + (b + 1) * BANK],
                                         start=True, stop=True)
                    last.then_inc(tailed, 1)
                    pe.wait_ge(amask, 1)
                    v = lambda t, h: PR[:, t, D_OFF + 1024 + h * HD:D_OFF + 1024 + (h + 1) * HD]
                    for h in range(NH):
                        s = place(h)
                        pe.matmul(self.bank(6, HD, h * HD), Z[:, s * T:s * T + P], v(0, h), start=True, stop=True)
                        pe.matmul(self.bank(7, HD, h * HD), Z[:, s * T + P:(s + 1) * T], v(0, h), start=True, stop=False)
                        last = pe.matmul(self.bank(7, HD, h * HD), Z[:, n0 + s * P:n0 + (s + 1) * P], v(1, h),
                                         start=False, stop=True)
                    last.then_inc(mixed, 1)

                @block.scalar
                def _(act):
                    ch = self.act_chain.on(act)
                    act.wait_ge(scored, 1)
                    ch(act.activation(Z, allz, ACT.Copy, scale=HD ** -0.5))
                    act.sem_inc(scaled, 1)
                    act.wait_ge(negd, 1)
                    ch(act.activation(L, L, ACT.Exp))
                    ch(act.activation(L, L, ACT.Ln, bias=1.0))
                    act.sem_inc(logd, 1)
                    act.wait_ge(added, 1)
                    ch(act.activation(Z, W, ACT.Exp))
                    act.sem_inc(exped, 1)

                @block.vector
                def _(dve):
                    ch = self.dve_chain.on(dve)
                    dve.wait_ge(scaled, 1)
                    ch(dve.scalar_tensor_tensor(out=L, in0=Z, scalar=-1.0, in1=Z, op0=ALU.mult, op1=ALU.min))
                    dve.sem_inc(negd, 1)
                    dve.wait_ge(logd, 1)
                    ch(dve.scalar_tensor_tensor(out=W, in0=Z, scalar=0.0, in1=L, op0=ALU.min, op1=ALU.subtract))
                    ch(dve.tensor_tensor(L, W, Z, ALU.subtract))
                    dve.sem_inc(sub, 1)
                    dve.wait_ge(tailed, 1)
                    ch(dve.tensor_tensor(W, allz, W, ALU.add))
                    dve.sem_inc(added, 1)
                    dve.wait_ge(mixed, 1)
                    for t in range(NT):
                        ch(dve.tensor_copy(PR[:, t, D_OFF:D_OFF + 512], self.bank(6 + t)))

                @block.gpsimd
                def _(pool):
                    ch = self.pool_chain.on(pool)
                    pool.wait_ge(sub, 1)
                    ch(causal(pool, L))
                    pool.sem_inc(mask_ready, 1)
                    pool.wait_ge(exped, 1)
                    ch(causal(pool, Z))
                    pool.sem_inc(amask, 1)

    def attention(self, name, nk, qk, bias, val, dv, out, factor, add, work):
        S, PT, wide_tmp = work
        chunks = [[(c, min(P, nk[t] - c)) for c in range(0, nk[t], P)] for t in range(NT)]
        soff, poff = (0, NH * nk[0]), (0, NH * P * len(chunks[0]))
        s_view = lambda t: S[:, soff[t]:soff[t] + NH * nk[t]].rearrange("p (h n) -> p h n", h=NH)
        s_at = lambda h, t: soff[t] + place(h) * nk[t]
        sbank = (0, 2)
        obank = (6, 7) if dv * NH <= BANK else (6, 0)
        scored, shifted, weighed, turned, kept, mixed, out_read = [self.sem(name + n) for n in (
            "_scores", "_maxima", "_weights", "_weights_turned", "_weights_kept", "_outputs", "_outputs_read")]
        st = self.att
        negmax, sums, inv, fac = [st[:, i] for i in range(4)]

        with self.block() as block:
            @block.tensor
            def _(pe):
                for t in range(NT):
                    for h in range(NH):
                        at = (sbank[t] + (h % 2) * (t + 1)) * BANK + h // 2 * nk[t]
                        o = self.psum[:, at:at + nk[t]]
                        for i, (q, k) in enumerate(qk):
                            last = pe.matmul(o, q(h, t), k(h, nk[t]), start=(i == 0), stop=(i == len(qk) - 1))
                    last.then_inc(scored, 1)
                for t in range(NT):
                    pe.wait_ge(weighed, t + 1)
                    for h in range(NH):
                        for c, (k0, kn) in enumerate(chunks[t]):
                            o = sbank[t] * BANK + (h * len(chunks[t]) + c) * P
                            last = pe.transpose(self.psum[0:kn, o:o + P],
                                                S[:, s_at(h, t) + k0:s_at(h, t) + k0 + kn],
                                                self.ident[:, :])
                    last.then_inc(turned, 1)
                for t in range(NT):
                    pe.wait_ge(kept, t + 1)
                    for h in range(NH):
                        for c, (k0, kn) in enumerate(chunks[t]):
                            p0 = poff[t] + (h * len(chunks[t]) + c) * P
                            last = pe.matmul(self.bank(obank[t], dv, h * dv), PT[0:kn, p0:p0 + P], val(h, c, kn),
                                             start=(c == 0), stop=(c == len(chunks[t]) - 1))
                    last.then_inc(mixed, 1)

            @block.vector
            def _(dve):
                ch = self.dve_chain.on(dve)
                for t in range(NT):
                    dve.wait_ge(scored, t + 1)
                    for odd in range(2):
                        ps = self.bank(sbank[t] + odd * (t + 1), 4 * nk[t]).rearrange("p (h n) -> p h n", h=4)
                        h4 = slice(4 * odd, 4 * odd + 4)
                        last = dve.tensor_tensor(s_view(t)[:, h4], ps, bias(t)[:, h4], ALU.add)
                    ch(last)
                    ch(dve.tensor_reduce(negmax[:, t, :], s_view(t), AX.X, ALU.max, negate=True))
                    dve.sem_inc(shifted, 1)
                for t in range(NT):
                    dve.wait_ge(weighed, t + 1)
                    ch(dve.reciprocal(inv[:, t, :], sums[:, t, :]))
                    f = inv
                    if factor is not None:
                        ch(dve.tensor_tensor(fac[:, t, :], inv[:, t, :], factor(t), ALU.mult))
                        f = fac
                    dve.wait_ge(mixed, t + 1)
                    ps = self.bank(obank[t], NH * dv).rearrange("p (h d) -> p h d", h=NH)
                    fb = f[:, t, :].unsqueeze(2).to_broadcast([P, NH, dv])
                    if add:
                        w = wide_tmp[:, 0:NH * dv].rearrange("p (h d) -> p h d", h=NH)
                        ch(dve.tensor_tensor(w, ps, fb, ALU.mult))
                        ch(dve.tensor_tensor(out(t), out(t), w, ALU.add))
                    else:
                        ch(dve.tensor_tensor(out(t), ps, fb, ALU.mult))

            @block.scalar
            def _(act):
                ch = self.act_chain.on(act)
                for t in range(NT):
                    act.wait_ge(shifted, t + 1)
                    for h in range(NH):
                        s = S[:, s_at(h, t):s_at(h, t) + nk[t]]
                        last = act.activation(s, s, ACT.Exp, bias=negmax[:, t, place(h):place(h) + 1],
                                              accum_out=sums[:, t, h:h + 1])
                    ch(last)
                    act.sem_inc(weighed, 1)
                for t in range(NT):
                    act.wait_ge(turned, t + 1)
                    rows = chunks[t][0][1]
                    n = NH * len(chunks[t]) * P
                    ch(act.activation(PT[0:rows, poff[t]:poff[t] + n],
                                      self.psum[0:rows, sbank[t] * BANK:sbank[t] * BANK + n], ACT.Copy))
                    act.sem_inc(kept, 1)

    def nsa(self, PR):
        nc, a = self.nc, self.a
        with ExitStack() as ctx:
            tmp = lambda n, s: ctx.enter_context(nc.sbuf_tensor(n, s, F32))
            biasT = tmp("distance_bias", [P, NH, T])
            qT = tmp("nsa_q", [P, 4, T])
            kT = tmp("nsa_k", [P, 4, T])
            kcT = tmp("nsa_kc", [P, NG, N_CMP])
            vc = tmp("nsa_vc", [N_CMP, NG, HD])
            gates = tmp("nsa_gates", [P, NT, 3 * NH])
            S = self.XN[:, :, :].rearrange("p t c -> p (t c)")[:, 0:NH * 3 * P]
            PT = tmp("nsa_weights_turned", [P, NH * 3 * P])
            wtmp = self.XN[:, 1, 1024:1536]
            vec_dram = nc.dram_tensor("bias_by_distance", [NH, 2 * T], F32, kind="Internal")
            bucket = rel_buckets()

            with ExitStack() as c2:
                tm2 = lambda n, s: c2.enter_context(nc.sbuf_tensor(n, s, F32))
                w1 = self.XN[:, :, :].rearrange("p t (l e) -> p t l e", e=HD)
                w2 = tm2("cmp_w2", [HD, 2, HD])
                pos_in = tm2("cmp_pos", [2 * CMP_LEN, HD])
                posT = tm2("cmp_pos_turned", [HD, 2 * CMP_LEN])
                tab = tm2("table", [32, NH])
                tabT = tm2("table_turned", [NH, 32])
                vec = tm2("bias_vector", [NH, 2 * T])
                zT = tm2("cmp_z", [P, 2, T])[:, :, :]
                flipped = tm2("bias_flipped", [P, NH, T])
                flip = tm2("flip", [P, P])
                loaded, vecd = self.sem("nsa_loaded"), self.sem("bias_vector_made")
                with self.block() as block:
                    @block.sync
                    def _(sp):
                        for h in range(2):
                            for i in range(2):
                                sp.dma_start(w1[h * HD:(h + 1) * HD, i], a["cmp_w1"][0, i]
                                             .rearrange("(l d) e -> d l e", d=HD)).then_inc(loaded, 16)
                        sp.dma_start(w2[:, :, :], a["cmp_w2"][0].rearrange("i d e -> d i e")).then_inc(loaded, 16)
                        sp.dma_start(pos_in[:, :], a["cmp_pos"][0].rearrange("i l d -> (i l) d")).then_inc(loaded, 16)
                        sp.dma_start(tab[:, :], a["rel_table"]).then_inc(loaded, 16)
                        sp.wait_ge(loaded, 16 * 7)
                self.turn_stage([([tab[:, :]], tabT[:, :], None), ([pos_in[:, :]], posT[:, :], None),
                                 ([PR[:, t, A_KV + P * i:A_KV + P * (i + 1)] for i in range(2) for t in range(NT)],
                                  zT, None)])
                with self.block() as block:
                    @block.vector
                    def _(dve):
                        ch = self.dve_chain.on(dve)
                        last = dve.memset(vec[:, T:2 * T], NEG)
                        for b in range(bucket[-1] + 1):
                            at = np.flatnonzero(bucket == b)
                            if len(at):
                                lo, n = T - 1 - int(at[-1]), len(at)
                                last = dve.tensor_copy(vec[:, lo:lo + n], tabT[:, b:b + 1].to_broadcast([NH, n]))
                        ch(last)
                        dve.sem_inc(vecd, 1)

                    @block.gpsimd
                    def _(pool):
                        ch = self.pool_chain.on(pool)
                        ch(pool.memset(flip[:, :], 0.0))
                        ch(pool.affine_select(out=flip[:, :], in_=flip[:, :], pattern=[[1, P]], compare_op=ALU.not_equal,
                                              fill=1.0, base=1 - P, channel_multiplier=1))

                    @block.sync
                    def _(sp):
                        sp.wait_ge(vecd, 1)
                        sp.dma_start(vec_dram[:, :], vec[:, :]).then_inc(loaded, 16)
                        sp.wait_ge(loaded, 16 * 8)
                        for odd in range(2):
                            sp.dma_start(flipped[:, 4 * odd:4 * odd + 4, :],
                                         bass.AP(tensor=vec_dram[:, :].tensor, offset=odd * 2 * T,
                                                 ap=[[1, P], [4 * T, 4], [1, T]])).then_inc(loaded, 16)
                        sp.wait_ge(loaded, 16 * 10)

                H1 = tm2("cmp_hidden", [HD, 2, NG, N_CMP])
                posb = tm2("cmp_pos_part", [HD, 2])
                kc = tm2("cmp_k", [N_CMP, NG, 2, HD])
                sq = tm2("cmp_squares", [N_CMP, NG, HD])
                first, hid, second, ssq, rsd, unflipped = [self.sem("cmp_" + n) for n in (
                    "first", "hidden", "second", "squares", "rstd", "bias_unflipped")]
                with self.block() as block:
                    @block.tensor
                    def _(pe):
                        for b in range(4):
                            last = pe.matmul(self.bank(4 + b), flip[:, :],
                                             flipped[:, 2 * b:2 * b + 2, :].rearrange("p h t -> p (h t)"),
                                             start=True, stop=True)
                        last.then_inc(unflipped, 1)
                        for i in range(2):
                            for g in range(NG):
                                r = slice(g * HD, (g + 1) * HD)
                                for l in range(CMP_LEN):
                                    pe.matmul(self.psum[0:HD, g * BANK + i * 16:g * BANK + i * 16 + N_CMP], w1[r, i, l, :],
                                              zT[r, i, l:l + CMP_STRIDE * (N_CMP - 1) + 1:CMP_STRIDE],
                                              start=(l == 0), stop=(l == CMP_LEN - 1))
                            for l in range(CMP_LEN):
                                last = pe.matmul(self.psum[0:HD, 128 + i:129 + i], w1[0:HD, i, l, :],
                                                 posT[:, i * CMP_LEN + l:i * CMP_LEN + l + 1],
                                                 start=(l == 0), stop=(l == CMP_LEN - 1))
                        last.then_inc(first, 1)
                        pe.wait_ge(hid, 1)
                        for i in range(2):
                            for g in range(NG):
                                last = pe.matmul(self.bank(2, HD, (2 * i + g) * HD)[0:N_CMP],
                                                 H1[:, i, g, :], w2[:, i, :], start=True, stop=True)
                        last.then_inc(second, 1)

                    @block.scalar
                    def _(act):
                        ch = self.act_chain.on(act)
                        act.wait_ge(first, 1)
                        ch(act.activation(posb[:, :], self.psum[0:HD, 128:130], ACT.Copy))
                        for i in range(2):
                            for g in range(NG):
                                last = act.activation(H1[:, i, g, :], self.bank(g, N_CMP, i * 16)[0:HD],
                                                      ACT.Gelu_apprx_tanh, bias=posb[:, i:i + 1])
                        ch(last)
                        act.sem_inc(hid, 1)

                    @block.vector
                    def _(dve):
                        ch = self.dve_chain.on(dve)
                        dve.wait_ge(unflipped, 1)
                        ch(dve.tensor_copy(biasT[:, :, :].rearrange("p h t -> p (h t)"), self.psum[:, 4 * BANK:8 * BANK]))
                        dve.wait_ge(second, 1)
                        ps = self.bank(2, 4 * HD)[0:N_CMP].rearrange("p (i g d) -> p i g d", i=2, g=NG)
                        ch(dve.tensor_copy(vc[:, :, :], ps[:, 1]))
                        ch(dve.tensor_copy(kc[:, :, 0, :], ps[:, 0]))
                        ch(dve.tensor_tensor(sq[:, :, :], kc[:, :, 0, :], kc[:, :, 0, :], ALU.mult))
                        ch(dve.tensor_reduce(self.stat[0:N_CMP, 0:NG], sq[:, :, :], AX.X, ALU.add))
                        dve.sem_inc(ssq, 1)
                        dve.wait_ge(rsd, 1)
                        rb = self.rstd[0:N_CMP, 0:NG].unsqueeze(2).to_broadcast([N_CMP, NG, HD])
                        ch(dve.tensor_tensor(kc[:, :, 0, :], kc[:, :, 0, :], rb, ALU.mult))
                        ch(dve.tensor_copy(kc[:, :, 1, :], kc[:, :, 0, :]))

                    @block.gpsimd
                    def _(pool):
                        pool.wait_ge(ssq, 1)
                        ch = self.pool_chain.on(pool)
                        st, rs = self.stat[0:N_CMP, 0:NG], self.rstd[0:N_CMP, 0:NG]
                        ch(pool.tensor_scalar(st, st, 1.0 / HD, 1e-6, ALU.mult, ALU.add))
                        ch(pool.tensor_tensor(out=rs, in0=st, in1=self.minus_half[0:N_CMP, 0:NG], op=ALU.pow))
                        pool.sem_inc(rsd, 1)
                self.turn_stage([([kc[:, g].rearrange("p a d -> p (a d)")], kcT[:, g, :], [(N_CMP, self.gain(G_K))])
                                 for g in range(NG)])

            with ExitStack() as c2:
                tm2 = lambda n, s: c2.enter_context(nc.sbuf_tensor(n, s, F32))
                qn = tm2("nsa_q_normed", [P, NT, 512])
                kn = tm2("nsa_k_normed", [P, NT, 2, NG, 2, HD])
                ks = tm2("nsa_k_squares", [P, NT, 2, NG, HD])
                ssq, rsd = self.sem("nsa_squares"), self.sem("nsa_rstd")
                with self.block() as block:
                    @block.scalar
                    def _(act):
                        act.activation(gates[:, :, :], PR[:, :, A_GATE:A_GATE + 24], ACT.Sigmoid)

                    @block.vector
                    def _(dve):
                        ch = self.dve_chain.on(dve)
                        kv = lambda t: PR[:, t, A_KV + 256:A_KV + 1280 - 512 + 0].rearrange(
                            "p (b s g d) -> p b s g d", b=2, s=2, g=NG)[:, :, 0]
                        q = PR[:, :, 0:512]
                        ch(dve.tensor_tensor(qn[:, :, :], q, q, ALU.mult))
                        for t in range(NT):
                            last = dve.tensor_tensor(ks[:, t], kv(t), kv(t), ALU.mult)
                        ch(last)
                        for t in range(NT):
                            dve.tensor_reduce(self.stat[:, 8 * t:8 * t + 8],
                                              qn[:, t, :].rearrange("p (h d) -> p h d", h=NH), AX.X, ALU.add)
                            last = dve.tensor_reduce(self.stat[:, 16 + 4 * t:20 + 4 * t],
                                                     ks[:, t].rearrange("p b g d -> p (b g) d"), AX.X, ALU.add)
                        ch(last)
                        dve.sem_inc(ssq, 1)
                        dve.wait_ge(rsd, 1)
                        for t in range(NT):
                            dve.tensor_tensor(qn[:, t, :].rearrange("p (h d) -> p h d", h=NH),
                                              q[:, t, :].rearrange("p (h d) -> p h d", h=NH),
                                              self.rstd[:, 8 * t:8 * t + 8].unsqueeze(2).to_broadcast([P, NH, HD]), ALU.mult)
                            for b in range(2):
                                for dup in range(2):
                                    r = self.rstd[:, 16 + 4 * t + 2 * b:18 + 4 * t + 2 * b]
                                    last = dve.tensor_tensor(kn[:, t, b, :, dup, :], kv(t)[:, b],
                                                             r.unsqueeze(2).to_broadcast([P, NG, HD]), ALU.mult)
                        ch(last)

                    @block.gpsimd
                    def _(pool):
                        pool.wait_ge(ssq, 1)
                        self.rstd_on_pool(pool, HD, 24)
                        pool.sem_inc(rsd, 1)
                jobs = []
                for k in range(0, 4, 2):
                    jobs.append(([qn[:, t, kk * P:(kk + 1) * P] for kk in (k, k + 1) for t in range(NT)],
                                 qT[:, k:k + 2, :], [(2 * T, self.gain(G_Q))]))
                for b in range(2):
                    jobs.append(([kn[:, t, b, g].rearrange("p a d -> p (a d)") for g in range(NG) for t in range(NT)],
                                 kT[:, 2 * b:2 * b + 2, :], [(2 * T, self.gain(G_K))]))
                self.turn_stage(jobs)

            q = lambda h, t: qT[HD * (h % 2):HD * (h % 2) + HD, h // 2, t * P:(t + 1) * P]
            g = lambda h: h // (NH // NG)
            out = lambda t: PR[:, t, 0:512].rearrange("p (h d) -> p h d", h=NH)
            gate = lambda b: (lambda t: gates[:, t, b:3 * NH:3])
            with self.block() as block:
                @block.gpsimd
                def _(pool):
                    self.pool_chain.on(pool)(pool.affine_select(
                        out=gates[:, 0, 0:3 * NH:3], in_=gates[:, 0, 0:3 * NH:3], pattern=[[0, NH]],
                        compare_op=ALU.is_ge, fill=0.0, base=-(CMP_LEN - 1), channel_multiplier=1))
            first = P + CMP_LEN - 1
            cmp_bias = lambda t: (biasT[:, :, first:T:CMP_STRIDE] if t == 0 else biasT[:, :, CMP_LEN - 1:T:CMP_STRIDE])
            self.attention("cmp", (N_CMP0, N_CMP),
                           [(q, lambda h, n: kcT[HD * (h % 2):HD * (h % 2) + HD, g(h), 0:n])],
                           cmp_bias, lambda h, c, n: vc[0:n, g(h), :], HD, out, gate(0), False, (S, PT, wtmp))
            all_bias = lambda t: biasT[:, :, P:T] if t == 0 else biasT[:, :, :]
            for b, name in ((0, "selected"), (1, "window")):
                self.attention(name, (P, T),
                               [(q, lambda h, n: kT[HD * (h % 2):HD * (h % 2) + HD, 2 * b + g(h), 0:n])],
                               all_bias,
                               lambda h, c, n: PR[0:n, c, A_KV + 384 + 256 * b + g(h) * HD:A_KV + 384 + 256 * b + (g(h) + 1) * HD],
                               HD, out, gate(1 + b), True, (S, PT, wtmp))

    def ffn(self, streams, following):
        nc, ring = self.nc, self.ring
        up, down = streams
        rounds = up.rounds
        with ExitStack() as ctx:
            aT = ctx.enter_context(nc.sbuf_tensor("ffn_turned", [P, KF, T], F32))
            sg, pr = self.XN[:, :, 0:BANK], self.XN[:, :, BANK:2 * BANK]
            silu, prod, turned, kept = [self.sem("ffn_" + n) for n in ("silu", "product", "turned", "kept")]
            with ExitStack() as c2:
                hT = self.features(c2, KD)
                self.norm_turn(lambda t, g: self.X[:, t, :], 1, D, hT, G_FFN)
                hi, lo = hT
                ring.parts(c2)
                with self.block() as block:
                    @block.sync
                    def _(sp):
                        ring.rest(sp, up, down)

                    @block.tensor
                    def _(pe):
                        def half_round(i, m):
                            for q in range(4):
                                j, half = 2 * m + q // 2, q % 2
                                ring.wait(pe, i, j, half)
                                wh, wl = ring.piece(ring.hi, half, up), ring.piece(ring.lo, half, up)
                                for k in range(4):
                                    for t in range(NT):
                                        kk, tok = 4 * q + k, slice(t * P, (t + 1) * P)
                                        last = self.passes(pe, self.bank(2 * m + t), hi[:, kk, tok], lo[:, kk, tok],
                                                           wh[:, k, :], wl[:, k, :], kk == 0, kk == KD - 1)
                                last.then_inc(ring.used, 1)

                        def turn(i):
                            pe.wait_ge(prod, i)
                            pe.wait_ge(kept, i)
                            for k in range(4):
                                for t in range(NT):
                                    last = pe.transpose(self.bank(4 + k // 2, P, (k % 2) * T + t * P),
                                                        pr[:, t, k * P:(k + 1) * P], self.ident[:, :])
                            last.then_inc(turned, 1)

                        pe.sem_inc(turned, 1)
                        half_round(0, 0)
                        half_round(0, 1)
                        with pe.Fori(1, rounds) as i:
                            pe.wait_ge(silu, i)
                            half_round(i, 0)
                            turn(i)
                            half_round(i, 1)
                        turn(rounds)

                    @block.scalar
                    def _(act):
                        def gate(i):
                            act.wait_ge(ring.used, ring.done(i, 4))
                            for t in range(NT):
                                last = act.activation(sg[:, t, :], self.bank(t), ACT.Silu)
                            last.then_inc(silu, 1)

                        def keep(i):
                            act.wait_ge(turned, i + 1)
                            for b in range(2):
                                last = act.activation(aT[:, bass.ds((i - 1) * 4 + 2 * b, 2), :].rearrange("p k t -> p (k t)"),
                                                      self.bank(4 + b), ACT.Copy)
                            last.then_inc(kept, 1)

                        def split(i, pieces):
                            for q in pieces:
                                ring.split_hi(act, up, i, q // 2, q % 2)

                        act.sem_inc(kept, 1)
                        split(0, range(6))
                        gate(0)
                        split(0, range(6, 8))
                        with act.Fori(1, rounds) as i:
                            split(i, range(6))
                            act.wait_ge(prod, i)
                            gate(i)
                            keep(i)
                            split(i, range(6, 8))
                        keep(rounds)

                    @block.vector
                    def _(dve):
                        def product(i):
                            dve.wait_ge(silu, i)
                            dve.wait_ge(ring.used, ring.done(i - 1, 8))
                            dve.wait_ge(turned, i)
                            for t in range(NT):
                                last = dve.tensor_tensor(pr[:, t, :], self.bank(2 + t), sg[:, t, :], ALU.mult)
                            last.then_inc(prod, 1)

                        def split(i, pieces):
                            for q in pieces:
                                ring.split_lo(dve, up, i, q // 2, q % 2)

                        split(0, range(8))
                        with dve.Fori(1, rounds) as i:
                            split(i, range(2))
                            product(i)
                            split(i, range(2, 8))
                        product(rounds)
            ring.close(up)
            ring.parts(ctx)
            ahi, alo = [ctx.enter_context(nc.sbuf_tensor("ffn_turned_" + n, [P, 2, T], F32R)) for n in ("hi", "lo")]
            a_hi = self.sem("ffn_hidden_hi")
            pieces = [(n // 8, n % 8 // 2, n % 2) for n in range(KF)]
            skip = lambda n: 2 * (4 - down.last) if n == KF - 1 else 0
            with self.block() as block:
                @block.sync
                def _(sp):
                    ring.rest(sp, down, following)

                @block.scalar
                def _(act):
                    for n, (i, j, half) in enumerate(pieces):
                        ring.split_hi(act, down, i, j, half, skip(n))
                        act.activation(ahi[:, n % 2, :], aT[:, n, :], ACT.Copy).then_inc(a_hi, 1)

                @block.vector
                def _(dve):
                    for n, (i, j, half) in enumerate(pieces):
                        dve.wait_ge(a_hi, n + 1)
                        dve.tensor_tensor(alo[:, n % 2, :], aT[:, n, :], ahi[:, n % 2, :].bitcast(F32), ALU.subtract)
                        ring.split_lo(dve, down, i, j, half, skip(n))
                    dve.wait_ge(ring.used, ring.done(down.rounds, 0))
                    for t in range(NT):
                        self.dve_chain.on(dve)(dve.tensor_tensor(self.X[:, t, :], self.psum[:, 4 * t * BANK:4 * (t + 1) * BANK],
                                                                 self.X[:, t, :], ALU.add))

                @block.tensor
                def _(pe):
                    for n, (i, j, half) in enumerate(pieces):
                        ring.wait(pe, i, j, half)
                        wh, wl = ring.piece(ring.hi, half, down), ring.piece(ring.lo, half, down)
                        for t in range(NT):
                            tok = slice(t * P, (t + 1) * P)
                            for c in range(4):
                                col = slice(c * BANK, (c + 1) * BANK)
                                last = self.passes(pe, self.bank(4 * t + c), ahi[:, n % 2, tok], alo[:, n % 2, tok],
                                                   wh[:, 0, col], wl[:, 0, col], n == 0, n == KF - 1)
                        last.then_inc(ring.used, 1 + skip(n))
            ring.close(down)

    def pool_mix(self, Z):
        nc, a = self.nc, self.a
        with ExitStack() as ctx:
            tmp = lambda n, s: ctx.enter_context(nc.sbuf_tensor(n, s, F32))
            band = tmp("pool_band", [P, 4, T + P])
            wp = tmp("pool_w", [P, 4, 2, T])
            dT = tmp("pool_turned", [P, 4, 2, T])
            made, loaded, diff, kept, done = [self.sem("pool_" + n) for n in ("bands", "loaded", "means", "kept", "done")]
            with self.block() as block:
                @block.sync
                def _(sp):
                    sp.dma_start(wp[:, :, :, :].rearrange("p g k d -> p (g k) d"),
                                 a["w_pool_2"][0].rearrange("g (k p) d -> p (g k) d", p=P)).then_inc(loaded, 16)

                @block.gpsimd
                def _(pool):
                    ch = self.pool_chain.on(pool)
                    for g, w in enumerate(WINDOWS):
                        last = pool.memset(band[:, g, :], 1.0 / w)
                    ch(last)
                    for g, w in enumerate(WINDOWS):
                        for t in range(w - 1):
                            last = pool.memset(band[:, g, t:t + 1], 1.0 / (t + 1))
                    ch(last)
                    for g, w in enumerate(WINDOWS):
                        for lo, n in ((0, T), (T, P)):
                            v = band[:, g, lo:lo + n]
                            ch(pool.affine_select(out=v, in_=v, pattern=[[1, n]], compare_op=ALU.is_ge, fill=0.0,
                                                  base=0, channel_multiplier=-1))
                            ch(pool.affine_select(out=v, in_=v, pattern=[[-1, n]], compare_op=ALU.is_ge, fill=0.0,
                                                  base=w - 1, channel_multiplier=1))
                            ch(pool.tensor_tensor(out=band[:, g, lo:lo + P], in0=band[:, g, lo:lo + P],
                                                  in1=self.ident[:, :], op=ALU.subtract))
                    pool.sem_inc(made, 1)

                @block.tensor
                def _(pe):
                    pe.wait_ge(made, 1)
                    for g in range(4):
                        for c in range(2):
                            o = (2 * g + c) * T
                            col = slice(g * T + c * P, g * T + (c + 1) * P)
                            pe.matmul(self.psum[:, o:o + T], Z[:, 0, col], band[:, g, 0:T], start=True, stop=False)
                            last = pe.matmul(self.psum[:, o + P:o + T], Z[:, 1, col], band[:, g, T:T + P],
                                             start=False, stop=True)
                    last.then_inc(diff, 1)
                    pe.wait_ge(loaded, 16)
                    pe.wait_ge(kept, 1)
                    for t in range(NT):
                        for g in range(4):
                            for c in range(2):
                                last = pe.matmul(self.bank(4 + 2 * t + g // 2, T, (g % 2) * T),
                                                 dT[:, g, c, t * P:(t + 1) * P], wp[:, g, c, :], start=(c == 0), stop=(c == 1))
                    last.then_inc(done, 1)

                @block.scalar
                def _(act):
                    act.wait_ge(diff, 1)
                    self.act_chain.on(act)(act.activation(dT[:, :, :, :].rearrange("p g c t -> p (g c t)"),
                                                          self.psum[:, 0:8 * T], ACT.Copy))
                    act.sem_inc(kept, 1)

                @block.vector
                def _(dve):
                    dve.wait_ge(done, 1)
                    for t in range(NT):
                        dve.tensor_copy(Z[:, t, 0:POOL_W], self.psum[:, (4 + 2 * t) * BANK:(6 + 2 * t) * BANK])

    def mla(self, Q, KV, Zr, M):
        nc = self.nc
        with ExitStack() as ctx:
            tmp = lambda n, s: ctx.enter_context(nc.sbuf_tensor(n, s, F32))
            qT, kT = tmp("mla_q", [P, NH, T]), tmp("mla_k", [P, NH, T])
            qrT, krT = tmp("mla_q_rope", [P, 4, T]), tmp("mla_k_rope", [P, 4, T])
            mask = tmp("mla_mask", [P, T + P])
            S = self.XN[:, :, :].rearrange("p t c -> p (t c)")[:, 0:NH * 3 * P]
            PT = tmp("mla_weights_turned", [P, NH * 3 * P])
            q4 = Q.rearrange("p t (h d) -> p t h d", h=NH)
            kv4 = KV.rearrange("p t (h d) -> p t h d", h=NH)
            with ExitStack() as c2:
                tm2 = lambda n, s: c2.enter_context(nc.sbuf_tensor(n, s, F32))
                junk = self.XN[:, 0, 0:NH * QKH]
                kg = tm2("rope_k", [P, NT, 64])
                rot = tm2("rope_k_turned", [P, NT, 64])
                rr = tm2("rope_parts", [P, 2, NH, HALF])
                kr = tm2("rope_k_heads", [P, NT, NH, 64])
                qr = tm2("rope_q_heads", [P, NT, NH, 64])
                ssq, rsd, masked = self.sem("mla_squares"), self.sem("mla_rstd"), self.sem("mla_masked")

                def rope(dve, ch, dst, src, heads, t):
                    a1, a2 = src[:, :, 0:HALF], src[:, :, HALF:64]
                    cos = self.cosT[:, t:t + 1, :].to_broadcast([P, heads, HALF])
                    sin = self.sinT[:, t:t + 1, :].to_broadcast([P, heads, HALF])
                    r = rr[:, :, 0:heads, :]
                    ch(dve.tensor_tensor(r[:, 0], a2, sin, ALU.mult))
                    ch(dve.tensor_tensor(dst[:, :, 0:HALF], a1, cos, ALU.mult))
                    ch(dve.tensor_tensor(dst[:, :, 0:HALF], dst[:, :, 0:HALF], r[:, 0], ALU.subtract))
                    ch(dve.tensor_tensor(r[:, 1], a1, sin, ALU.mult))
                    ch(dve.tensor_tensor(dst[:, :, HALF:64], a2, cos, ALU.mult))
                    ch(dve.tensor_tensor(dst[:, :, HALF:64], dst[:, :, HALF:64], r[:, 1], ALU.add))

                with self.block() as block:
                    @block.vector
                    def _(dve):
                        ch = self.dve_chain.on(dve)
                        for t in range(NT):
                            jq = junk.rearrange("p (h d) -> p h d", h=NH)
                            ch(dve.tensor_tensor(jq, q4[:, t], q4[:, t], ALU.mult))
                            ch(dve.tensor_reduce(self.stat[:, 8 * t:8 * t + 8], jq, AX.X, ALU.add))
                            jk = junk[:, 0:NH * P].rearrange("p (h d) -> p h d", h=NH)
                            ch(dve.tensor_tensor(jk, kv4[:, t, :, 0:P], kv4[:, t, :, 0:P], ALU.mult))
                            ch(dve.tensor_reduce(self.stat[:, 16 + 8 * t:24 + 8 * t], jk, AX.X, ALU.add))
                            jr = junk[:, 0:64]
                            ch(dve.tensor_tensor(jr, Zr[:, t, :], Zr[:, t, :], ALU.mult))
                            ch(dve.tensor_reduce(kg[:, t, 0:1], jr, AX.X, ALU.add))
                            ch(dve.tensor_scalar(self.stat[:, 16 + 8 * t:24 + 8 * t], self.stat[:, 16 + 8 * t:24 + 8 * t],
                                                 kg[:, t, 0:1], None, ALU.add))
                        dve.sem_inc(ssq, 1)
                        ch(dve.tensor_tensor(kg[:, :, :], Zr, self.gbk[:, :].unsqueeze(1).to_broadcast([P, NT, 64]), ALU.mult))
                        for t in range(NT):
                            rope(dve, ch, rot[:, t:t + 1, :], kg[:, t:t + 1, :], 1, t)
                        dve.wait_ge(rsd, 1)
                        for t in range(NT):
                            rq = self.rstd[:, 8 * t:8 * t + 8].unsqueeze(2)
                            rk = self.rstd[:, 16 + 8 * t:24 + 8 * t].unsqueeze(2)
                            ch(dve.tensor_tensor(q4[:, t], q4[:, t], rq.to_broadcast([P, NH, QKH]), ALU.mult))
                            ch(dve.tensor_tensor(kv4[:, t, :, 0:P], kv4[:, t, :, 0:P], rk.to_broadcast([P, NH, P]), ALU.mult))
                            ch(dve.tensor_tensor(kr[:, t], rot[:, t:t + 1, :].to_broadcast([P, NH, 64]),
                                                 rk.to_broadcast([P, NH, 64]), ALU.mult))
                            ch(dve.tensor_tensor(q4[:, t, :, P:QKH], q4[:, t, :, P:QKH],
                                                 self.gbq[:, :].unsqueeze(1).to_broadcast([P, NH, 64]), ALU.mult))
                            rope(dve, ch, qr[:, t], q4[:, t, :, P:QKH], NH, t)

                    @block.gpsimd
                    def _(pool):
                        ch = self.pool_chain.on(pool)
                        ch(pool.memset(mask[:, :], 0.0))
                        pool.memset(mask[0:64, 64:P], NEG)
                        ch(pool.memset(mask[0:64, T + 64:T + P], NEG))
                        pool.wait_ge(ssq, 1)
                        self.rstd_on_pool(pool, QKH, 32)
                        ch(pool.tensor_scalar(self.rstd[:, 0:16], self.rstd[:, 0:16], QKH ** -0.5, 0.0, ALU.mult, ALU.add))
                        pool.sem_inc(rsd, 1)
                jobs = []
                for h in range(0, NH, 2):
                    jobs.append(([q4[:, t, hh, 0:P] for hh in (h, h + 1) for t in range(NT)], qT[:, h:h + 2, :],
                                 [(2 * T, self.gain(G_QN))]))
                    jobs.append(([kv4[:, t, hh, 0:P] for hh in (h, h + 1) for t in range(NT)], kT[:, h:h + 2, :],
                                 [(2 * T, self.gain(G_KN))]))
                for k in range(0, 4, 2):
                    for src, dst in ((qr, qrT), (kr, krT)):
                        jobs.append(([src[:, t, 2 * kk:2 * kk + 2, :].rearrange("p a d -> p (a d)")
                                      for kk in (k, k + 1) for t in range(NT)], dst[:, k:k + 2, :], None))
                self.turn_stage(jobs)
            r = lambda h: slice(HD * (h % 2), HD * (h % 2) + HD)
            tok = lambda t: slice(t * P, (t + 1) * P)
            self.attention("mla", (P, T),
                           [(lambda h, t: qT[:, h, tok(t)], lambda h, n: kT[:, h, 0:n]),
                            (lambda h, t: qrT[r(h), h // 2, tok(t)], lambda h, n: krT[r(h), h // 2, 0:n])],
                           lambda t: (mask[:, 0:P] if t == 0 else mask[:, P:P + T]).unsqueeze(1).to_broadcast([P, NH, (P, T)[t]]),
                           lambda h, c, n: KV[0:n, c, h * T + P:(h + 1) * T], P,
                           lambda t: M[:, t, POOL_W:D].rearrange("p (h d) -> p h d", h=NH), None, False, (S, PT, None))

    def peer(self, following, w_pq):
        nc, a = self.nc, self.a
        J = 2 * NH
        with ExitStack() as ctx:
            tmp = lambda n, s, d=F32: ctx.enter_context(nc.sbuf_tensor(n, s, d))
            eidx = tmp("expert_index", [P, NT, SLOTS], U32)
            gts = tmp("expert_gates", [P, NT, NH, TOPK])
            wts = tmp("expert_weights", [P, NT, SLOTS])
            with ExitStack() as c2:
                tm2 = lambda n, s, d=F32: c2.enter_context(nc.sbuf_tensor(n, s, d))
                qp = tm2("peer_q", [P, NT, D])
                with ExitStack() as c3:
                    hT = self.features(c3, KD)
                    self.norm_turn(lambda t, g: self.X[:, t, :], 1, D, hT, G_FFN2)
                    self.linear(w_pq, following, hT, KD, BANK,
                                lambda eng, t, c, ps: self.copy_out(eng, qp[:, t, bass.ds(c * BANK, BANK)], ps), ("act", "dve"))
                sk = tm2("sub_keys", [P, J, P])
                skT = tm2("sub_keys_turned", [P, J, P])
                SC = tm2("peer_scores", [P, NT, D])
                qpT = tm2("peer_q_turned", [P, J, T])
                loaded = self.sem("sub_keys_loaded")
                with self.block() as block:
                    @block.scalar
                    def _(act):
                        for h, name in enumerate(("sub_k1_2", "sub_k2_2")):
                            act.dma_start(sk[:, h:J:2, :], a[name][0].rearrange("h n d -> n h d")).then_inc(loaded, 16)
                        act.wait_ge(loaded, 32)
                self.turn_stage(self.feature_jobs(lambda t: qp[:, t, :], qpT[:, :, :], KD)
                                + [([sk[:, j + i, :] for i in range(4)], skT[:, j:j + 4, :], None) for j in range(0, J, 4)])
                scored, ex, exped = self.sem("peer_scored"), self.sem("peer_shifted"), self.sem("peer_exponentials")
                v, vi = tm2("top_values", [P, NT, J, TOPK]), tm2("top_index", [P, NT, J, TOPK], U32)
                vif = tm2("top_index_f", [P, NT, J, TOPK])
                cv, ci = tm2("pair_values", [P, NT, NH, TOPK]), tm2("pair_index", [P, NT, NH, TOPK], U32)
                cab = tm2("pair_parts", [P, 2, NT, NH, TOPK], U32)
                cf = tm2("pair_parts_f", [P, 2, NT, NH, TOPK])
                io, iof = tm2("count", [P, TOPK], I32), tm2("count_f", [P, TOPK])
                e12 = tm2("pair_experts", [P, 2, NT, NH, TOPK])
                sm = tm2("gate_sums", [P, NT, NH])
                counted = self.sem("counted")
                LOW = -3.0e38
                with self.block() as block:
                    @block.gpsimd
                    def _(pool):
                        ch = self.pool_chain.on(pool)
                        ch(pool.iota(io[:, :], pattern=[[1, TOPK]], base=0, channel_multiplier=0))
                        pool.sem_inc(counted, 1)

                    @block.tensor
                    def _(pe):
                        for t in range(NT):
                            for j in range(J):
                                last = pe.matmul(self.psum[:, (t * J + j) * P:(t * J + j + 1) * P],
                                                 qpT[:, j, t * P:(t + 1) * P], skT[:, j, :], start=True, stop=True)
                        last.then_inc(scored, 1)

                    @block.vector
                    def _(dve):
                        ch = self.dve_chain.on(dve)
                        dve.wait_ge(scored, 1)
                        ch(dve.tensor_copy(SC[:, :, :].rearrange("p t c -> p (t c)"), self.psum[:, :]))

                        def top16(rows):
                            for s, val, ind in rows:
                                last = dve.max(val[:, 0:8], s)
                            ch(last)
                            for s, val, ind in rows:
                                last = dve.max_index(ind[:, 0:8], val[:, 0:8], s)
                            ch(last)
                            for s, val, ind in rows:
                                last = dve.match_replace(s, val[:, 0:8], s, LOW)
                            ch(last)
                            for s, val, ind in rows:
                                last = dve.max(val[:, 8:16], s)
                            ch(last)
                            for s, val, ind in rows:
                                last = dve.max_index(ind[:, 8:16], val[:, 8:16], s)
                            ch(last)

                        top16([(SC[:, t, j * P:(j + 1) * P], v[:, t, j, :], vi[:, t, j, :]) for t in range(NT) for j in range(J)])
                        ch(dve.tensor_copy(vif[:, :, :, :], vi[:, :, :, :]))
                        for t in range(NT):
                            pair = SC[:, t, :].rearrange("p (h a b) -> p h a b", h=NH, a=TOPK)
                            last = dve.tensor_tensor(pair, v[:, t, 0:J:2, :].unsqueeze(3).to_broadcast([P, NH, TOPK, TOPK]),
                                                     v[:, t, 1:J:2, :].unsqueeze(2).to_broadcast([P, NH, TOPK, TOPK]), ALU.add)
                        ch(last)
                        top16([(SC[:, t, h * 256:(h + 1) * 256], cv[:, t, h, :], ci[:, t, h, :]) for t in range(NT) for h in range(NH)])
                        dve.tensor_scalar(cab[:, 0], ci[:, :, :, :], 4, None, ALU.logical_shift_right)
                        ch(dve.tensor_scalar(cab[:, 1], ci[:, :, :, :], TOPK - 1, None, ALU.bitwise_and))
                        ch(dve.tensor_copy(cf[:, :].rearrange("p a t h k -> p (a t h k)"),
                                           cab[:, :].rearrange("p a t h k -> p (a t h k)")))
                        dve.wait_ge(counted, 1)
                        ch(dve.tensor_copy(iof[:, :], io[:, :]))
                        for half in range(2):
                            for t in range(NT):
                                m = SC[:, t, :].rearrange("p (h k a) -> p h k a", h=NH, k=TOPK)
                                m3 = SC[:, t, :].rearrange("p (hk a) -> p hk a", a=TOPK)
                                ch(dve.tensor_tensor(m3, cf[:, half, t].rearrange("p h k -> p (h k)").unsqueeze(2)
                                                     .to_broadcast([P, SLOTS, TOPK]),
                                                     iof[:, :].unsqueeze(1).to_broadcast([P, SLOTS, TOPK]), ALU.is_equal))
                                ch(dve.tensor_tensor(m, m, vif[:, t, half:J:2, :].unsqueeze(2)
                                                     .to_broadcast([P, NH, TOPK, TOPK]), ALU.mult))
                                ch(dve.tensor_reduce(e12[:, half, t].rearrange("p h k -> p (h k)"), m3, AX.X, ALU.add))
                        ch(dve.scalar_tensor_tensor(out=eidx[:, :, :], in0=e12[:, 0].rearrange("p t h k -> p t (h k)"),
                                                    scalar=float(NKEYS), in1=e12[:, 1].rearrange("p t h k -> p t (h k)"),
                                                    op0=ALU.mult, op1=ALU.add))
                        for t in range(NT):
                            ch(dve.tensor_tensor(gts[:, t], cv[:, t], cv[:, t, :, 0:1].to_broadcast([P, NH, TOPK]), ALU.subtract))
                        dve.sem_inc(ex, 1)
                        dve.wait_ge(exped, 1)
                        for t in range(NT):
                            ch(dve.tensor_reduce(sm[:, t], gts[:, t], AX.X, ALU.add))
                            ch(dve.reciprocal(sm[:, t], sm[:, t]))
                            ch(dve.tensor_tensor(gts[:, t], gts[:, t], sm[:, t].unsqueeze(2).to_broadcast([P, NH, TOPK]), ALU.mult))

                    @block.scalar
                    def _(act):
                        act.wait_ge(ex, 1)
                        self.act_chain.on(act)(act.activation(gts[:, :, :, :], gts[:, :, :, :], ACT.Exp))
                        act.sem_inc(exped, 1)

            NB = 8
            rows = tmp("expert_rows", [P, NB, D])
            cur = tmp("gather_index", [P, NB], U32)
            gb = tmp("ffn_gain", [P, D])
            dots = tmp("expert_products", [P, NB])
            gathered = [self.sem(f"expert_row_gathered{b}") for b in range(NB)]
            used, gained, xready, acted = [self.sem("expert_" + n) for n in ("row_used", "gain_loaded", "input", "activated")]
            kept, started = self.sem("expert_products_kept"), self.sem("gathers_started")
            loops = SLOTS // NB
            with self.block() as block:
                @block.sync
                def _(sp):
                    sp.dma_start(gb[:, :], a["ffn_norm_gain_2"].to_broadcast([P, D])).then_inc(gained, 16)

                @block.gpsimd
                def _(pool):
                    ch_n = self.pool_chain
                    phase = 0
                    pool.sem_inc(used, NB)
                    for t in range(NT):
                        for table in ("expert_u_2", "expert_v_2"):
                            with pool.Fori(0, loops) as i:
                                for b in range(NB):
                                    pool.wait_ge(used, i * NB + (phase * SLOTS + b + 1))
                                    pool.tensor_copy(cur[:, b:b + 1], eidx[:, t, bass.ds(i * NB + b, 1)])\
                                        .then_inc(ch_n.sem, 1)
                                    pool.wait_ge(ch_n.sem, i * NB + (ch_n.n + b + 1))
                                    pool.sem_inc(started, 1)
                                    pool.indirect_dma_start(
                                        out=rows[:, b, :], out_offset=None, in_=a[table][0],
                                        in_offset=bass.IndirectOffsetOnAxis(ap=cur[:, b:b + 1], axis=0))\
                                        .then_inc(gathered[b], 16)
                            ch_n.n += SLOTS
                            phase += 1

                @block.vector
                def _(dve):
                    ch = self.dve_chain.on(dve)
                    phase = 0
                    dve.wait_ge(gained, 16)
                    for t in range(NT):
                        ch(dve.tensor_tensor(self.XN[:, t, :], self.XN[:, t, :], gb[:, :], ALU.mult))
                    for t in range(NT):
                        with dve.Fori(0, loops) as i:
                            for b in range(NB):
                                dve.wait_ge(gathered[b], i * 16 + 16 * (phase * loops + 1))
                                if b == 0:
                                    dve.wait_ge(kept, i + t * loops)
                                dve.tensor_tensor_reduce(rows[:, b, :], rows[:, b, :], self.XN[:, t, :], 1.0, 0.0,
                                                         ALU.mult, ALU.add, dots[:, b:b + 1]).then_inc(used, 1)
                            dve.wait_ge(used, i * NB + (phase * SLOTS + 2 * NB))
                            dve.tensor_copy(wts[:, t, bass.ds(i * NB, NB)], dots[:, :]).then_inc(kept, 1)
                        phase += 1
                        dve.sem_inc(xready, 1)
                        dve.wait_ge(acted, t + 1)
                        ch(dve.tensor_tensor(wts[:, t, :], wts[:, t, :], gts[:, t].rearrange("p h k -> p (h k)"), ALU.mult))
                        with dve.Fori(0, loops) as i:
                            for b in range(NB):
                                dve.wait_ge(gathered[b], i * 16 + 16 * (phase * loops + 1))
                                dve.wait_ge(used, i * NB + (phase * SLOTS + NB + b))
                                dve.scalar_tensor_tensor(out=self.X[:, t, :], in0=rows[:, b, :],
                                                         scalar=wts[:, t, bass.ds(i * NB + b, 1)],
                                                         in1=self.X[:, t, :], op0=ALU.mult, op1=ALU.add).then_inc(used, 1)
                        phase += 1

                @block.scalar
                def _(act):
                    for t in range(NT):
                        act.wait_ge(xready, t + 1)
                        act.wait_ge(kept, loops * (t + 1))
                        self.act_chain.on(act)(act.activation(wts[:, t, :], wts[:, t, :], ACT.Gelu_apprx_tanh))
                        act.sem_inc(acted, 1)

    def copy_out(self, eng, to, src):
        return eng.activation(to, src, ACT.Copy) if eng is self.nc.scalar else eng.tensor_copy(to, src)

    def add_out(self, eng, t, c, ps):
        x = self.X[:, t, bass.ds(c * BANK, BANK)]
        return eng.tensor_tensor(x, ps, x, ALU.add)

    def ple(self, w_gate):
        nc, a = self.nc, self.a
        with ExitStack() as ctx:
            tmp = lambda n, s: ctx.enter_context(nc.sbuf_tensor(n, s, F32))
            gate = tmp("ple_gate", [P, NT, D])
            pin = tmp("ple_in", [P, NT, T])
            pT = tmp("ple_in_turned", [P, 2, T])
            wp = tmp("ple_proj", [P, 2, D])
            loaded, ready, done, stored = [self.sem("ple_" + n) for n in ("loaded", "product", "gated", "stored")]
            with ExitStack() as c2:
                hT = self.features(c2, KD)
                self.norm_turn(lambda t, g: self.X[:, t, :], 1, D, hT, G_PLE)
                self.linear(w_gate, None, hT, KD, BANK,
                            lambda eng, t, c, ps: eng.activation(gate[:, t, bass.ds(c * BANK, BANK)], ps, ACT.Sigmoid),
                            ("act", "act"))
            with self.block() as block:
                @block.sync
                def _(sp):
                    sp.dma_start(pin[:, :, :], a["p_2"][0, 0].rearrange("(t p) c -> p t c", p=P)).then_inc(loaded, 16)
                    sp.dma_start(wp[:, :, :], a["w_ple_proj_2"][0].rearrange("(k p) n -> p k n", p=P)).then_inc(loaded, 16)
                    sp.wait_ge(loaded, 32)
            self.turn_stage(self.feature_jobs(lambda t: pin[:, t, :], pT[:, :, :], 2))
            with self.block() as block:
                @block.tensor
                def _(pe):
                    for t in range(NT):
                        for c in range(4):
                            for k in range(2):
                                last = pe.matmul(self.bank(4 * t + c), pT[:, k, t * P:(t + 1) * P],
                                                 wp[:, k, c * BANK:(c + 1) * BANK], start=(k == 0), stop=(k == 1))
                        last.then_inc(ready, 1)

                @block.vector
                def _(dve):
                    ch = self.dve_chain.on(dve)
                    for t in range(NT):
                        dve.wait_ge(ready, t + 1)
                        ch(dve.tensor_tensor(gate[:, t, :], self.psum[:, 4 * t * BANK:4 * (t + 1) * BANK], gate[:, t, :], ALU.mult))
                        ch(dve.tensor_tensor(self.X[:, t, :], self.X[:, t, :], gate[:, t, :], ALU.add))
                        dve.sem_inc(done, 1)

                @block.sync
                def _(sp):
                    o = self.out[0].rearrange("(t p) c -> p t c", p=P)
                    for t in range(NT):
                        sp.wait_ge(done, t + 1)
                        sp.dma_start(o[:, t, :], self.X[:, t, :]).then_inc(stored, 16)
                    sp.wait_ge(stored, 16 * NT)

    def run(self):
        nc, a = self.nc, self.a
        w = lambda name: a[name][0]
        kview = lambda name: w(name).rearrange("(k p) n -> p k n", p=P)
        gate, up, down = kview("w_ffn_gate"), kview("w_ffn_up"), kview("w_ffn_down")
        uq, ukv = kview("w_uq_2"), kview("w_ukv_2")
        WI, WI2, WQ = 450, 352, 384
        s_in = Stream(wide(w("w_in"), WI), (8, WI), W_IN_COLS // (2 * WI))
        s_out = Stream(wide(w("w_out"), BANK), (8, BANK), 2)
        s_up = Stream(lambda i, j: (gate if j < 2 else up)[:, 8 * (j % 2):8 * (j % 2) + 8, bass.ds(i * BANK, BANK)],
                      (8, BANK), D_FF // BANK)
        s_down = Stream(lambda i, j: down[:, bass.ds(i * 8 + 2 * j, 2), :], (2, D), 6, last=2)
        s_in2 = Stream(wide(w("w_in_2"), WI2), (8, WI2), IN2_COLS // (2 * WI2))
        s_uq = Stream(lambda i, j: uq[:, :, j * WQ:(j + 1) * WQ], (4, WQ), 1)
        s_ukv = Stream(lambda i, j: ukv[:, :, j * BANK:(j + 1) * BANK], (4, BANK), 1)
        s_out2 = Stream(wide(w("w_out_2"), BANK), (8, BANK), 2)
        s_pq = Stream(wide(w("w_pq_2"), BANK), (8, BANK), 2)
        s_ple = Stream(wide(w("w_ple_gate_2"), BANK), (8, BANK), 2)
        to = lambda dst, width: (lambda eng, t, c, ps: self.copy_out(eng, dst[:, t, bass.ds(c * width, width)], ps))
        X = self.X

        self.setup(s_in)
        with ExitStack() as ctx:
            PR = ctx.enter_context(nc.sbuf_tensor("projections", [P, NT, W_IN_COLS], F32))
            with ExitStack() as c2:
                hT = self.features(c2, KD)
                self.norm_turn(lambda t, g: X[:, t, :], 1, D, hT, G_MIX)
                self.linear(s_in, s_out, hT, KD, WI, to(PR, WI), ("act", "dve"))
            self.nsa(PR)
            self.sticks(PR)
            self.conv(PR)
            self.sgu(PR)
            hT = self.features(ctx, KD)
            offs = (0, B_OFF, C_OFF, D_OFF)
            self.norm_turn(lambda t, g: PR[:, t, offs[g]:offs[g] + BANK], 4, BANK, hT, G_GROUP)
            self.linear(s_out, s_up, hT, KD, BANK, self.add_out, ("dve", "dve"))
        self.ffn((s_up, s_down), s_in2)
        with ExitStack() as ctx:
            Z = ctx.enter_context(nc.sbuf_tensor("projections2", [P, NT, IN2_COLS], F32))
            with ExitStack() as c2:
                hT = self.features(c2, KD)
                self.norm_turn(lambda t, g: X[:, t, :], 1, D, hT, G_MIX2)
                self.linear(s_in2, s_uq, hT, KD, WI2, to(Z, WI2), ("act", "dve"))
            with ExitStack() as c2:
                Q = c2.enter_context(nc.sbuf_tensor("queries", [P, NT, NH * QKH], F32))
                KV = c2.enter_context(nc.sbuf_tensor("keys_values", [P, NT, D], F32))
                with ExitStack() as c3:
                    hT = self.features(c3, 4)
                    self.norm_turn(lambda t, g: Z[:, t, Q_OFF:KV_OFF], 1, 512, hT, G_QLAT)
                    self.linear(s_uq, s_ukv, hT, 4, WQ, to(Q, WQ), ("act", "dve"))
                    self.norm_turn(lambda t, g: Z[:, t, KV_OFF:ROPE_OFF], 1, 512, hT, G_KVLAT)
                    self.linear(s_ukv, s_out2, hT, 4, BANK, to(KV, BANK), ("act", "dve"))
                self.mla(Q[:, :, :], KV[:, :, :], Z[:, :, ROPE_OFF:IN2_COLS], Z)
            self.pool_mix(Z)
            hT = self.features(ctx, KD)
            self.turn_split_stage(lambda t, k: Z[:, t, k * P:(k + 1) * P], hT,
                                  self.gains_of(G_POOL, 8) + self.gains_of(None, 8))
            self.linear(s_out2, s_pq, hT, KD, BANK, self.add_out, ("dve", "dve"))
        self.peer(s_ple, s_pq)
        self.ple(s_ple)


_INS = ["x", "w_in", "w_out", "norm_mix", "norm_ffn", "q_gain", "k_gain", "cmp_pos", "cmp_w1", "cmp_w2", "rel_table",
        "conv_w", "sgu_w", "sgu_b", "group_gain", "w_ffn_gate", "w_ffn_up", "w_ffn_down", "p_2", "positions_2",
        "mix_norm_gain_2", "w_in_2", "w_pool_2", "pool_scale_2", "q_lat_gain_2", "kv_lat_gain_2", "w_uq_2", "w_ukv_2",
        "q_norm_gain_2", "k_norm_gain_2", "w_out_2", "ffn_norm_gain_2", "w_pq_2", "sub_k1_2", "sub_k2_2",
        "expert_u_2", "expert_v_2", "ple_norm_gain_2", "w_ple_gate_2", "w_ple_proj_2"]


def kernel(**inputs):
    import concourse.bacc as bacc
    from concourse.bass_utils import run_bass_kernel_spmd

    nc = bacc.Bacc("TRN2", target_bir_lowering=False, num_devices=1)
    arrays, args = {}, {}
    for name in _INS:
        v = np.ascontiguousarray(inputs[name])
        arrays["in_" + name] = v
        args[name] = nc.dram_tensor("in_" + name, v.shape, mybir.dt.from_np(v.dtype), kind="ExternalInput").ap()
    out = nc.dram_tensor("out", (1, T, D), F32, kind="ExternalOutput").ap()
    Kernel(nc, args, out).run()
    return run_bass_kernel_spmd(nc, [arrays], core_ids=[0]).results[0]["out"]
```

```python
import concourse.bass as bass
from concourse import mybir
from contextlib import ExitStack
import math
import numpy as np

F32 = mybir.dt.float32
F32R = mybir.dt.float32r
I32 = mybir.dt.int32
U32 = mybir.dt.uint32
ALU = mybir.AluOpType
ACT = mybir.ActivationFunctionType
AX = mybir.AxisListType

P = 128
T = 256
NT = T // P
D = 2048
KD = D // P
BANK = 512

HD = 64
NH = 8
NG = 2
W_IN_COLS = 5400
A_KV = 512
A_GATE = 1280
B_OFF = 1304
C_OFF = B_OFF + 1536
D_OFF = C_OFF + 1024
D_FF = 5632
KF = D_FF // P
CMP_LEN, CMP_STRIDE = 32, 16
N_CMP = (T - CMP_LEN) // CMP_STRIDE + 1
N_CMP0 = (P - CMP_LEN) // CMP_STRIDE + 1
NEG = -1.0e30

POOL_W = 1024
WINDOWS = (2, 4, 8, 16)
Q_OFF, KV_OFF, ROPE_OFF = 1024, 1536, 2048
IN2_COLS = 2112
QKH = 192
TOPK = 16
NKEYS = 128
SLOTS = NH * TOPK
HALF = 32

G_MIX, G_FFN, G_MIX2, G_FFN2, G_PLE, G_GROUP = 0, 16, 32, 48, 64, 80
G_POOL, G_QLAT, G_KVLAT = 96, 104, 108
G_Q, G_K, G_QN, G_KN, G_SGUB = 112, 113, 114, 115, 116
G_ROWS = 124


def place(h):
    return h % 2 * (NH // 2) + h // 2


def rel_buckets():
    n = np.arange(T)
    nf = np.maximum(n, 1).astype(np.float32)
    large = 16 + (np.log(nf / np.float32(16)) / np.float32(math.log(64)) * np.float32(16)).astype(np.int32)
    return np.where(n < 16, n, np.minimum(large, 31))


class Signal:

    def __init__(self, nc, name):
        self.sem, self.total = nc.alloc_semaphore(name), 0

    def at(self, k):
        return k + self.total

    def close(self, n):
        self.total += n


class Chain:

    def __init__(self, nc, name):
        self.sem, self.n, self.eng = nc.alloc_semaphore(name), 0, None

    def on(self, eng):
        self.eng = eng
        return self

    def __call__(self, ins):
        self.n += 1
        ins.then_inc(self.sem, 1)
        self.eng.wait_ge(self.sem, self.n)


class Stream:

    def __init__(self, source, view, rounds, last=4):
        self.source, self.view, self.rounds, self.last = source, view, rounds, last


class Ring:

    SLOTS = 4
    WORDS = 4096
    PIECE = 2048

    def __init__(self, nc):
        self.nc = nc
        self.buf = nc.alloc_sbuf_tensor("weights", [P, self.SLOTS, self.WORDS], F32)
        self.ready = [nc.alloc_semaphore(f"weights_ready{j}") for j in range(self.SLOTS)]
        self.hi_ready = nc.alloc_semaphore("weights_hi_ready")
        self.lo_ready = nc.alloc_semaphore("weights_lo_ready")
        self.used = nc.alloc_semaphore("weights_used")
        self.fills = 0
        self.base = [0] * self.SLOTS
        self.scopes = 0

    def parts(self, ctx):
        self.scopes += 1
        sb = lambda n: ctx.enter_context(self.nc.sbuf_tensor(f"weights_{n}{self.scopes}", [P, 2, self.PIECE], F32R))
        self.hi, self.lo = sb("hi"), sb("lo")

    def raw(self, j, stream):
        k, n = stream.view
        return self.buf[:, j, 0:k * n].rearrange("p (k n) -> p k n", k=k)

    def piece(self, buf, half, stream):
        k, n = stream.view
        return buf[:, half, 0:k // 2 * n].rearrange("p (k n) -> p k n", k=k // 2)

    def fill(self, sp, stream, i, j, fills, wait=True):
        if wait:
            sp.wait_ge(self.lo_ready, i * 8 + 2 * (fills + j - 3))
        sp.dma_start(self.raw(j, stream), stream.source(i, j)).then_inc(self.ready[j], 16)

    def rest(self, sp, stream, following):
        if stream.rounds > 2:
            with sp.Fori(1, stream.rounds - (stream.last < 4)) as i:
                for j in range(4):
                    self.fill(sp, stream, i, j, self.fills)
            if stream.last < 4:
                for j in range(stream.last):
                    self.fill(sp, stream, stream.rounds - 1, j, self.fills)
        else:
            for i in range(1, stream.rounds):
                for j in range(4):
                    self.fill(sp, stream, i, j, self.fills)
        if following is not None:
            after = self.fills + 4 * stream.rounds
            for j in range(4):
                self.fill(sp, following, 0, j, after)

    def split_hi(self, act, stream, i, j, half, skip=0):
        if half == 0:
            act.wait_ge(self.ready[j], i * 16 + (self.base[j] + 16))
        act.wait_ge(self.used, i * 8 + (2 * (self.fills + j) + half + 1))
        k = stream.view[0] // 2
        act.activation(self.piece(self.hi, half, stream), self.raw(j, stream)[:, half * k:half * k + k], ACT.Copy)\
            .then_inc(self.hi_ready, 1 + skip)

    def split_lo(self, dve, stream, i, j, half, skip=0):
        dve.wait_ge(self.hi_ready, i * 8 + (2 * (self.fills + j) + half + 1))
        k = stream.view[0] // 2
        dve.tensor_tensor(self.piece(self.lo, half, stream), self.raw(j, stream)[:, half * k:half * k + k],
                          self.piece(self.hi, half, stream).bitcast(F32), ALU.subtract).then_inc(self.lo_ready, 1 + skip)

    def wait(self, pe, i, j, half):
        pe.wait_ge(self.lo_ready, i * 8 + (2 * (self.fills + j) + half + 1))

    def done(self, i, pieces):
        return i * 8 + (2 * self.fills + pieces + 2)

    def close(self, stream):
        for j in range(4):
            self.base[j] += 16 * (stream.rounds - (j >= stream.last))
        self.fills += 4 * stream.rounds


def wide(w, width, halves=2):
    v = w.rearrange("(k p) n -> p k n", p=P)
    return lambda i, j: v[:, 8 * (j % 2):8 * (j % 2) + 8, bass.ds((i * 2 + j // 2) * width, width)]


class Kernel:
    def __init__(self, nc, a, out):
        self.nc, self.a, self.out = nc, a, out
        sb, ps = nc.alloc_sbuf_tensor, nc.alloc_psum_tensor
        self.X = sb("residual", [P, NT, D], F32)
        self.XN = sb("normed", [P, NT, D], F32)
        self.ident = sb("identity", [P, P], F32)
        self.gT = sb("gains", [P, G_ROWS], F32)
        self.ring = Ring(nc)
        self.psum = ps("banks", [P, 8 * BANK], F32)
        self.bank_free = [Signal(nc, f"product_bank_free{t}") for t in range(NT)]
        self.turned = Signal(nc, "transposes_done")
        self.turned_read = {e: Signal(nc, f"transposes_read_{e}") for e in ("act", "dve")}
        self.squares = Signal(nc, "squares_summed")
        self.rstd_ready = Signal(nc, "rstd_ready")
        self.act_chain, self.dve_chain = Chain(nc, "act_chain"), Chain(nc, "dve_chain")
        self.pool_chain, self.sp_chain = Chain(nc, "pool_chain"), Chain(nc, "loads")
        self.scopes = 0
        self.minus_half = sb("minus_half", [P, 32], F32)
        self.stat = sb("statistics", [P, 32], F32)
        self.rstd = sb("rstd", [P, 32], F32)
        self.att = sb("attention_statistics", [P, 4, NT, NH], F32)

    def bank(self, b, n=BANK, off=0):
        return self.psum[:, b * BANK + off:b * BANK + off + n]

    def sem(self, name):
        return self.nc.alloc_semaphore(name)

    def block(self):
        return self.nc.Block()

    def rstd_on_pool(self, pool, n, count, extra=1.0, eps=1e-6, at=0):
        ch = self.pool_chain.on(pool)
        st, rs = self.stat[:, at:at + count], self.rstd[:, at:at + count]
        ch(pool.tensor_scalar(st, st, 1.0 / n, eps, ALU.mult, ALU.add))
        ch(pool.tensor_tensor(out=rs, in0=st, in1=self.minus_half[:, 0:count], op=ALU.pow))
        if extra != 1.0:
            ch(pool.tensor_scalar(rs, rs, extra, 0.0, ALU.mult, ALU.add))

    def turn(self, jobs, pe, act, dve, start=None):
        tr, rd = self.turned, self.turned_read
        for j, (ins, dst, gains) in enumerate(jobs):
            b = 4 + j % 4
            reader, k = ("act", "dve")[j % 2], j // 2 + 1
            if pe is not None:
                if j >= 4:
                    pe.wait_ge(rd[reader].sem, rd[reader].at(k - 2))
                off = 0
                for n, i in enumerate(ins):
                    pin, f = i.shape[0], i.shape[1] if len(i.shape) == 2 else int(np.prod(i.shape[1:]))
                    last = pe.transpose(self.psum[0:f, b * BANK + off:b * BANK + off + pin], i,
                                        self.ident[0:pin, 0:pin])
                    off += pin
                last.then_inc(tr.sem, 1)
                continue
            if (act is None) == (reader == "act"):
                continue
            eng = act if act is not None else dve
            eng.wait_ge(tr.sem, tr.at(j + 1))
            rows = dst.shape[0]
            size = int(np.prod(dst.shape[1:]))
            parts = gains or [(size, None)]
            flat = dst if len(dst.shape) == 2 else dst.rearrange("p a b -> p (a b)")
            off = 0
            for n, gain in parts:
                src, to = self.psum[0:rows, b * BANK + off:b * BANK + off + n], flat[:, off:off + n]
                if act is not None:
                    last = eng.activation(to, src, ACT.Copy, scale=1.0 if gain is None else gain)
                elif gain is None:
                    last = eng.tensor_copy(to, src)
                else:
                    last = eng.tensor_scalar(to, src, gain, None, ALU.mult)
                off += n
            last.then_inc(rd[reader].sem, 1)

    def turn_close(self, jobs):
        n = len(jobs)
        self.turned.close(n)
        self.turned_read["act"].close((n + 1) // 2)
        self.turned_read["dve"].close(n // 2)

    def gain(self, row, scale_rows=P):
        return self.gT[0:scale_rows, row:row + 1]

    def turn_stage(self, jobs):
        with self.block() as block:
            @block.tensor
            def _(pe):
                self.turn(jobs, pe, None, None)

            @block.scalar
            def _(act):
                self.turn(jobs, None, act, None)

            @block.vector
            def _(dve):
                self.turn(jobs, None, None, dve)
        self.turn_close(jobs)

    def feature_jobs(self, src, dst, kc):
        jobs = []
        for k in range(0, kc, 2):
            ins = [src(t)[:, kk * P:(kk + 1) * P] for kk in (k, k + 1) for t in range(NT)]
            jobs.append((ins, dst[:, k:k + 2, :], None))
        return jobs

    def features(self, ctx, kc):
        self.scopes += 1
        return [ctx.enter_context(self.nc.sbuf_tensor(f"features_{n}{self.scopes}", [P, kc, T], F32R)) for n in ("hi", "lo")]

    def turn_split(self, src, hT, gains, pe, act, dve, part=None):
        tr, rd = self.turned, self.turned_read
        hi, lo = hT
        jobs = len(gains) // 2
        for j in range(jobs) if part is None else range(part * jobs // 2, (part + 1) * jobs // 2):
            b = 4 + j % 4
            if pe is not None:
                if j >= 4:
                    pe.wait_ge(rd["dve"].sem, rd["dve"].at(j - 3))
                for i in range(2):
                    for t in range(NT):
                        last = pe.transpose(self.bank(b, P, i * T + t * P), src(t, 2 * j + i), self.ident[:, :])
                last.then_inc(tr.sem, 1)
                continue
            if act is not None:
                act.wait_ge(tr.sem, tr.at(j + 1))
            else:
                dve.wait_ge(rd["act"].sem, rd["act"].at(j + 1))
            for i in range(2):
                k, g = 2 * j + i, gains[2 * j + i]
                ps = self.bank(b, T, i * T)
                if act is not None:
                    last = act.activation(hi[:, k, :], ps, ACT.Copy, scale=1.0 if g is None else g)
                else:
                    last = dve.scalar_tensor_tensor(out=lo[:, k, :], in0=ps, scalar=1.0 if g is None else g,
                                                    in1=hi[:, k, :].bitcast(F32), op0=ALU.mult, op1=ALU.subtract)
            last.then_inc(rd["act" if act is not None else "dve"].sem, 1)

    def turn_split_close(self, gains):
        for s in (self.turned, self.turned_read["act"], self.turned_read["dve"]):
            s.close(len(gains) // 2)

    def gains_of(self, row, kc):
        return [None if row is None else self.gain(row + k) for k in range(kc)]

    def norm_groups(self, src, groups, n):
        sq, rs = self.squares, self.rstd_ready
        with self.block() as block:
            @block.scalar
            def _(act):
                for g in range(groups):
                    last = act.activation(self.XN[:, 0, g * n:(g + 1) * n], src(0, g), ACT.Square,
                                          accum_out=self.stat[:, g:g + 1])
                last.then_inc(sq.sem, 1)
                act.wait_ge(rs.sem, rs.at(1))
                for g in range(groups):
                    act.activation(self.XN[:, 0, g * n:(g + 1) * n], src(0, g), ACT.Copy,
                                   scale=self.rstd[:, g:g + 1])

            @block.gpsimd
            def _(pool):
                pool.wait_ge(sq.sem, sq.at(2))
                self.rstd_on_pool(pool, n, NT * groups)
                pool.sem_inc(rs.sem, 1)

            @block.vector
            def _(dve):
                for g in range(groups):
                    last = dve.tensor_tensor_reduce(self.XN[:, 1, g * n:(g + 1) * n], src(1, g), src(1, g), 1.0, 0.0,
                                                    ALU.mult, ALU.add, self.stat[:, groups + g:groups + g + 1])
                last.then_inc(sq.sem, 1)
                dve.wait_ge(rs.sem, rs.at(1))
                for g in range(groups):
                    c = groups + g
                    dve.tensor_scalar(self.XN[:, 1, g * n:(g + 1) * n], src(1, g), self.rstd[:, c:c + 1], None, ALU.mult)
        sq.close(2)
        rs.close(1)

    def sum_squares(self, x, act, dve):
        n = x(0).shape[1]
        if act is not None:
            ins = act.activation(self.XN[:, 0, 0:n], x(0), ACT.Square, accum_out=self.stat[:, 0:1])
        else:
            ins = dve.tensor_tensor_reduce(self.XN[:, 1, 0:n], x(1), x(1), 1.0, 0.0, ALU.mult, ALU.add, self.stat[:, 1:2])
        ins.then_inc(self.squares.sem, 1)

    def rstd_of_tiles(self, pool, n):
        pool.wait_ge(self.squares.sem, self.squares.at(2))
        self.rstd_on_pool(pool, n, NT)
        pool.sem_inc(self.rstd_ready.sem, 1)

    def rstd_wait(self, eng):
        eng.wait_ge(self.rstd_ready.sem, self.rstd_ready.at(1))

    def norm_close(self):
        self.squares.close(2)
        self.rstd_ready.close(1)

    def turn_split_wait(self, pe, gains, part):
        rd = self.turned_read["dve"]
        pe.wait_ge(rd.sem, rd.at((part + 1) * len(gains) // 4))

    def passes(self, pe, out, xh, xl, wh, wl, first, last_one):
        pe.matmul(out, xh, wh, start=first, stop=False)
        pe.matmul(out, xh, wl, start=False, stop=False)
        return pe.matmul(out, xl, wh, start=False, stop=last_one)

    def linear(self, stream, following, hT, src, gains, width, evac, on, norm=None, meanwhile=None):
        ring, kc = self.ring, len(gains)
        per = 2 if kc == KD else 4
        fpc = 4 // per
        kp = kc // fpc // 2
        rounds = stream.rounds
        hi, lo = hT

        def rounds_of(eng, body):
            body(0, True)
            if rounds > 2:
                with eng.Fori(1, rounds) as i:
                    body(i, False)
            else:
                for i in range(1, rounds):
                    body(i, False)

        with ExitStack() as ctx:
            ring.parts(ctx)
            with self.block() as block:
                @block.sync
                def _(sp):
                    ring.rest(sp, stream, following)

                @block.tensor
                def _(pe):
                    def body(i, first):
                        for c in range(per):
                            for t in range(NT):
                                pe.wait_ge(self.bank_free[t].sem, i * per + self.bank_free[t].at(c + 1))
                            for f in range(fpc):
                                for half in range(2):
                                    j, q = c * fpc + f, 2 * f + half
                                    if first and c == 0 and q % fpc == 0:
                                        self.turn_split_wait(pe, gains, q // fpc)
                                    ring.wait(pe, i, j, half)
                                    wh, wl = ring.piece(ring.hi, half, stream), ring.piece(ring.lo, half, stream)
                                    for k in range(kp):
                                        for t in range(NT):
                                            x = (q * kp + k, slice(t * P, (t + 1) * P))
                                            last = self.passes(pe, self.bank(2 * (c % 2) + t, width),
                                                               hi[:, x[0], x[1]], lo[:, x[0], x[1]],
                                                               wh[:, k, :], wl[:, k, :],
                                                               q == 0 and k == 0, q == 2 * fpc - 1 and k == kp - 1)
                                    last.then_inc(ring.used, 1)
                    self.turn_split(src, hT, gains, pe, None, None)
                    rounds_of(pe, body)

                if norm is not None:
                    @block.gpsimd
                    def _(pool):
                        self.rstd_of_tiles(pool, norm(0).shape[1])
                        if meanwhile is not None:
                            meanwhile(pool)

                def worker(name, split):
                    def program(eng):
                        def leave(i, c):
                            if c < 0:
                                i, c = i - 1, per - 1
                            eng.wait_ge(ring.used, ring.done(i, 2 * fpc * (c + 1)))
                            for t in range(NT):
                                if on[t] == name:
                                    evac(eng, t, i * per + c, self.bank(2 * (c % 2) + t, width))\
                                        .then_inc(self.bank_free[t].sem, 1)

                        def body(i, first):
                            for c in range(per):
                                for f in range(fpc):
                                    if first and c == f == 0:
                                        if norm is not None:
                                            self.sum_squares(norm, *sides)
                                        continue
                                    for half in range(2):
                                        split(eng, stream, i, c * fpc + f, half)
                                    if f == 0 and name in on:
                                        if first and c == 1 and norm is not None:
                                            self.rstd_wait(eng)
                                        leave(i, c - 1)
                        sides = (eng, None) if name == "act" else (None, eng)
                        for half in range(2):
                            self.turn_split(src, hT, gains, None, *sides, part=half)
                            split(eng, stream, 0, 0, half)
                        rounds_of(eng, body)
                        if name in on:
                            leave(rounds - 1, per - 1)
                    return program

                block.scalar(worker("act", ring.split_hi))
                block.vector(worker("dve", ring.split_lo))
        for t in range(NT):
            self.bank_free[t].close(rounds * per)
        self.turn_split_close(gains)
        if norm is not None:
            self.norm_close()
        ring.close(stream)

    def setup(self, first):
        a, nc = self.a, self.nc
        sb = nc.alloc_sbuf_tensor
        self.tri = sb("later_keys", [P, P], F32)
        self.ones = sb("ones", [P, P], F32)
        self.cosT = sb("cos", [P, NT, HALF], F32)
        self.sinT = sb("sin", [P, NT, HALF], F32)
        self.gbq = sb("rope_gain_q", [P, 64], F32)
        self.gbk = sb("rope_gain_k", [P, 64], F32)
        with ExitStack() as ctx:
            gin = ctx.enter_context(nc.sbuf_tensor("gains_in", [P, P], F32))
            gains, tokens, made, turned = [self.sem(n) for n in ("gains_loaded", "tokens_loaded", "constants_made", "gains_turned")]
            rows = [(a["norm_mix"], G_MIX, 16), (a["norm_ffn"], G_FFN, 16), (a["mix_norm_gain_2"], G_MIX2, 16),
                    (a["ffn_norm_gain_2"], G_FFN2, 16), (a["ple_norm_gain_2"], G_PLE, 16),
                    (a["group_gain"], G_GROUP, 16), (a["pool_scale_2"], G_POOL, 8),
                    (a["q_lat_gain_2"], G_QLAT, 4), (a["kv_lat_gain_2"], G_KVLAT, 4)]
            loads = [(gin[r:r + k, :], src[0].rearrange("(k p) -> k p", p=P)) for src, r, k in rows]
            loads += [(gin[r:r + 1, 64 * h:64 * h + 64], src) for src, r in ((a["q_gain"], G_Q), (a["k_gain"], G_K))
                      for h in range(2)]
            loads += [(gin[r:r + 1, :], src[:, 0:P]) for src, r in ((a["q_norm_gain_2"], G_QN), (a["k_norm_gain_2"], G_KN))]
            loads += [(gin[G_SGUB:G_SGUB + NH, :], a["sgu_b"][0])]

            with self.block() as block:
                @block.sync
                def _(sp):
                    for to, src in loads[0::2]:
                        sp.dma_start(to, src).then_inc(gains, 16)
                    sp.dma_start(self.X[:, :, :], a["x"][0].rearrange("(t p) c -> p t c", p=P)).then_inc(tokens, 16)
                    for j in range(4):
                        self.ring.fill(sp, first, 0, j, 0, wait=False)
                    sp.wait_ge(tokens, 16)

                @block.scalar
                def _(act):
                    for to, src in loads[1::2]:
                        act.dma_start(to, src).then_inc(gains, 16)

                @block.gpsimd
                def _(pool):
                    ch = self.pool_chain.on(pool)
                    pool.memset(self.minus_half[:, :], -0.5)
                    pool.memset(self.ones[:, :], 1.0)
                    ch(pool.memset(self.ident[:, :], 0.0))
                    ch(pool.affine_select(out=self.ident[:, :], in_=self.ident[:, :], pattern=[[-1, P]],
                                          compare_op=ALU.not_equal, fill=1.0, base=0, channel_multiplier=1))
                    pool.sem_inc(made, 1)
                    pool.affine_select(out=self.tri[:, :], in_=self.ones[:, :], pattern=[[-1, P]],
                                       compare_op=ALU.is_gt, fill=0.0, base=0, channel_multiplier=1)

                @block.tensor
                def _(pe):
                    pe.wait_ge(gains, 16 * len(loads))
                    pe.wait_ge(made, 1)
                    pe.transpose(self.bank(0, G_ROWS), gin[0:G_ROWS, :], self.ident[0:G_ROWS, 0:G_ROWS])\
                        .then_inc(turned, 1)

                @block.vector
                def _(dve):
                    ch = self.dve_chain.on(dve)
                    for t in range(NT):
                        dve.sem_inc(self.bank_free[t].sem, 2)
                    dve.sem_inc(self.ring.used, 2)
                    dve.wait_ge(turned, 1)
                    ch(dve.tensor_copy(self.gT[:, :], self.bank(0, G_ROWS)))
                    dve.tensor_scalar(self.gT[:, G_Q:G_Q + 1], self.gT[:, G_Q:G_Q + 1], HD ** -0.5, None, ALU.mult)

    def rope_inputs(self, ctx):
        nc, a = self.nc, self.a
        tmp = lambda n, s, d=F32: ctx.enter_context(nc.sbuf_tensor(n, s, d))
        ang, turns, part = [self.XN[:, 1, 1024 + i * 4 * HALF:1024 + (i + 1) * 4 * HALF]
                            .rearrange("p (s t k) -> p s t k", s=2, t=NT) for i in range(3)]
        self.angles = ang
        posi, posf = tmp("positions", [P, NT], I32), tmp("positions_f", [P, NT])
        freq = tmp("frequencies", [P, HALF])
        loaded = self.sem("rope_loaded")
        inv = (np.float32(10000.0) ** (-np.arange(0, 64, 2, dtype=np.float32) / np.float32(64))).astype(np.float32)

        def gpsimd(pool):
            for src, to in ((a["q_norm_gain_2"], self.gbq), (a["k_norm_gain_2"], self.gbk)):
                pool.dma_start(to[:, :], src[:, P:QKH].to_broadcast([P, 64])).then_inc(loaded, 16)
            pool.dma_start(posi[:, :], a["positions_2"].rearrange("o (t p) -> p (o t)", p=P),
                           allow_slow_non_contiguous=True).then_inc(loaded, 16)
            ch = self.pool_chain.on(pool)
            for k in range(HALF):
                last = pool.memset(freq[:, k:k + 1], float(inv[k]))
            ch(last)
            pool.wait_ge(loaded, 16 * 3)
            ch(pool.tensor_copy(posf[:, :], posi[:, :]))
            for t in range(NT):
                last = pool.tensor_scalar(ang[:, 0, t, :], freq[:, :], posf[:, t:t + 1], 0.0, ALU.mult, ALU.add)
            ch(last)
            magic = 1.5 * 2.0 ** 23
            two_pi = 2 * math.pi
            c1 = 6.28125
            c2 = float(np.float32(two_pi - c1))
            c2 = float(np.frombuffer((np.frombuffer(np.float32(c2).tobytes(), np.uint32) & 0xFFFFF000)
                                     .astype(np.uint32).tobytes(), np.float32)[0])
            c3 = float(np.float32(two_pi - c1 - c2))
            flat = lambda x: x.rearrange("p t k -> p (t k)")
            ch(pool.tensor_scalar(flat(turns[:, 0]), flat(ang[:, 0]), 1.0 / two_pi, magic, ALU.mult, ALU.add))
            ch(pool.tensor_scalar(flat(turns[:, 1]), flat(ang[:, 0]), 1.0 / two_pi, 0.25, ALU.mult, ALU.add))
            ch(pool.tensor_scalar(flat(turns[:, 1]), flat(turns[:, 1]), magic, 0.0, ALU.add, ALU.add))
            ch(pool.tensor_scalar(flat(turns[:, 0]), flat(turns[:, 0]), magic, 0.0, ALU.subtract, ALU.add))
            ch(pool.tensor_scalar(flat(turns[:, 1]), flat(turns[:, 1]), magic, 0.0, ALU.subtract, ALU.add))
            ch(pool.tensor_copy(flat(ang[:, 1]), flat(ang[:, 0])))
            for c in (c1, c2, c3):
                for s in range(2):
                    ch(pool.tensor_scalar(flat(part[:, s]), flat(turns[:, s]), -c, 0.0, ALU.mult, ALU.add))
                    ch(pool.tensor_tensor(out=flat(ang[:, s]), in0=flat(ang[:, s]), in1=flat(part[:, s]), op=ALU.add))
            ch(pool.tensor_scalar(flat(ang[:, 1]), flat(ang[:, 1]), math.pi / 2, 0.0, ALU.add, ALU.add))
            edge = 3.1415925
            for s in range(2):
                pool.tensor_scalar(flat(ang[:, s]), flat(ang[:, s]), edge, -edge, ALU.min, ALU.max)

        return gpsimd

    def conv(self, ctx, PR):
        tmp = lambda n, s: ctx.enter_context(self.nc.sbuf_tensor(n, s, F32))
        z = tmp("conv_z", [P, 3, NT, BANK])
        cw = tmp("conv_weights", [P, 3, BANK])
        y = tmp("conv_part", [P, NT, BANK])
        gated, zeros, moved = self.sem("conv_gated"), self.sem("conv_zeros"), self.sem("conv_moved")
        out = z[:, 2]

        def sync(sp):
            sp.dma_start(cw[:, :, :], self.a["conv_w"].rearrange("o k c -> o (k c)")
                         .to_broadcast([P, 3 * BANK]).rearrange("p (k c) -> p k c", k=3)).then_inc(moved, 16)
            sp.wait_ge(gated, 1)
            sp.wait_ge(zeros, 1)
            for s in (1, 2):
                sp.dma_start(z[s:P, s, :, :], z[0:P - s, 0, :, :]).then_inc(moved, 16)
                sp.dma_start(z[0:s, s, 1, :], z[P - s:P, 0, 0, :]).then_inc(moved, 16)

        def gpsimd(pool):
            ch = self.pool_chain.on(pool)
            ch(pool.memset(z[0:2, 1:3, 0, :], 0.0))
            pool.sem_inc(zeros, 1)
            ch(pool.tensor_tensor(z[:, 0], PR[:, :, B_OFF + 512:B_OFF + 1024],
                                  PR[:, :, B_OFF + 1024:B_OFF + 1536], ALU.mult))
            pool.sem_inc(gated, 1)
            w = lambda i: cw[:, i:i + 1, :].to_broadcast([P, NT, BANK])
            pool.wait_ge(moved, 16 * 5)
            ch(pool.tensor_tensor(out, z[:, 2], w(0), ALU.mult))
            ch(pool.tensor_tensor(y[:, :, :], z[:, 1], w(1), ALU.mult))
            ch(pool.tensor_tensor(out, out, y[:, :, :], ALU.add))
            ch(pool.tensor_tensor(y[:, :, :], z[:, 0], w(2), ALU.mult))
            ch(pool.tensor_tensor(out, out, y[:, :, :], ALU.add))
            b = PR[:, :, B_OFF:B_OFF + 512]
            ch(pool.tensor_tensor(b, out, b, ALU.mult))

        return {"gpsimd": gpsimd, "sync": sync}

    def load_sgu(self, sp):
        loaded = self.sem("sgu_loaded")
        sp.dma_start(self.sgu_w[:, :, :], self.a["sgu_w"][0].rearrange("h p q -> p h q")).then_inc(loaded, 16)
        sp.wait_ge(loaded, 16)

    def sticks_sgu(self, PR):
        nc = self.nc
        with ExitStack() as ctx:
            tmp = lambda n, s: ctx.enter_context(nc.sbuf_tensor(n, s, F32))
            qT, kT = tmp("stick_q", [P, 4, T]), tmp("stick_k", [P, 4, T])
            G0, G1 = 4 * T, 4 * P
            GW = G0 + G1
            Z, L, W = [self.XN[:, :, :].rearrange("p t c -> p (t c)")[:, 0:2 * GW],
                       tmp("stick_l", [P, 2 * GW])[:, :], tmp("stick_w", [P, 2 * GW])[:, :]]
            junk = self.XN[:, 1, D - NT * BANK:D].rearrange("p (t c) -> p t c", t=NT)
            of = lambda x, g: x[:, g * GW:(g + 1) * GW]
            wT = tmp("sgu_w_turned", [P, NH, P])
            v = tmp("sgu_v", [P, NT, BANK])
            C = PR[:, :, C_OFF:C_OFF + 1024]
            self.turn_stage([([self.sgu_w[:, 4 * b + h, :] for h in range(4)], wT[:, 4 * b:4 * b + 4, :], None)
                             for b in range(2)]
                            + [job for c, dst in ((0, qT), (512, kT)) for job in
                               self.feature_jobs(lambda t, c=c: PR[:, t, D_OFF + c:D_OFF + c + 512], dst[:, :, :], 4)])
            scored, scaled, negd, logd, mask_ready = [self.sem("stick_" + n) for n in (
                "scored", "scaled", "negated", "logs", "masked")]
            sub, tailed, added, exped, amask, mixed = [self.sem("stick_" + n) for n in (
                "log_rest", "tails", "exponents", "weights", "weights_masked", "outputs")]
            summed, centred, squared, rs, normed, wmasked, gmixed, gread = [self.sem("sgu_" + n) for n in (
                "summed", "centred", "squared", "rstd", "normed", "weights_masked", "mixed", "mixed_read")]

            def causal(pool, x, g):
                for lo, n in ((0, T), (G0, P)):
                    y = of(x, g)[:, lo:lo + 4 * n].rearrange("p (h t) -> p h t", h=4)
                    last = pool.affine_select(out=y, in_=y, pattern=[[0, 4], [1, n]], compare_op=ALU.is_gt,
                                              fill=0.0, base=0, channel_multiplier=-1)
                return last

            with self.block() as block:
                @block.tensor
                def _(pe):
                    for g in range(2):
                        ps = of(self.psum, g)
                        r = slice(HD * g, HD * g + HD)
                        for i in range(4):
                            pe.matmul(ps[:, i * T:(i + 1) * T], kT[r, i, 0:P], qT[r, i, :], start=True, stop=True)
                            last = pe.matmul(ps[:, G0 + i * P:G0 + (i + 1) * P], kT[r, i, P:T], qT[r, i, P:T],
                                             start=True, stop=True)
                        last.then_inc(scored, 1)
                    for g in range(2):
                        ps = of(self.psum, g)
                        pe.wait_ge(mask_ready, g + 1)
                        for i in range(4):
                            if i % 2 == 0:
                                pe.matmul(ps[:, i * T:(i + 2) * T], self.tri[:, :], of(L, g)[:, i * T:(i + 2) * T],
                                          start=True, stop=False)
                            pe.matmul(ps[:, i * T + P:(i + 1) * T], self.ones[:, :],
                                      of(L, g)[:, G0 + i * P:G0 + (i + 1) * P], start=False, stop=(i % 2 == 1))
                        pe.matmul(ps[:, G0:GW], self.tri[:, :], of(L, g)[:, G0:GW], start=True, stop=True)\
                            .then_inc(tailed, 1)
                        if g == 0:
                            pe.wait_ge(wmasked, 1)
                            pe.wait_ge(normed, 1)
                            for t in range(NT):
                                for h in range(NH):
                                    last = pe.matmul(self.bank(6 + t, HD, h * HD), wT[:, h, :], v[:, t, h * HD:(h + 1) * HD],
                                                     start=True, stop=True)
                            last.then_inc(gmixed, 1)
                    pe.wait_ge(gread, 1)
                    vD = lambda t, h: PR[:, t, D_OFF + 1024 + h * HD:D_OFF + 1024 + (h + 1) * HD]
                    for g in range(2):
                        pe.wait_ge(amask, g + 1)
                        for i in range(4):
                            h = 2 * i + g
                            z0, z1 = of(Z, g)[:, i * T:(i + 1) * T], of(Z, g)[:, G0 + i * P:G0 + (i + 1) * P]
                            pe.matmul(self.bank(6, HD, h * HD), z0[:, 0:P], vD(0, h), start=True, stop=True)
                            pe.matmul(self.bank(7, HD, h * HD), z0[:, P:T], vD(0, h), start=True, stop=False)
                            last = pe.matmul(self.bank(7, HD, h * HD), z1, vD(1, h), start=False, stop=True)
                    last.then_inc(mixed, 1)

                @block.scalar
                def _(act):
                    ch = self.act_chain.on(act)
                    for t in range(NT):
                        last = act.activation(v[:, t, :], C[:, t, 512:1024], ACT.Gelu_apprx_tanh,
                                              accum_out=self.stat[:, 4 + t:5 + t])
                    ch(last)
                    act.sem_inc(summed, 1)
                    act.activation(C[:, :, 0:512], C[:, :, 0:512], ACT.Gelu_apprx_tanh)
                    for g in range(2):
                        act.wait_ge(scored, g + 1)
                        ch(act.activation(of(Z, g), of(self.psum, g), ACT.Copy, scale=HD ** -0.5))
                        act.sem_inc(scaled, 1)
                    act.wait_ge(centred, 1)
                    for t in range(NT):
                        last = act.activation(junk[:, t, :], v[:, t, :], ACT.Square, accum_out=self.stat[:, t:t + 1])
                    ch(last)
                    act.sem_inc(squared, 1)
                    for g in range(2):
                        act.wait_ge(negd, g + 1)
                        ch(act.activation(of(L, g), of(L, g), ACT.Exp))
                        ch(act.activation(of(L, g), of(L, g), ACT.Ln, bias=1.0))
                        act.sem_inc(logd, 1)
                    for g in range(2):
                        act.wait_ge(added, g + 1)
                        ch(act.activation(of(Z, g), of(W, g), ACT.Exp))
                        act.sem_inc(exped, 1)

                @block.vector
                def _(dve):
                    ch = self.dve_chain.on(dve)
                    dve.wait_ge(summed, 1)
                    ch(dve.tensor_scalar(self.stat[:, 8:10], self.stat[:, 4:6], 1.0 / BANK, None, ALU.mult))
                    for t in range(NT):
                        last = dve.tensor_scalar(v[:, t, :], v[:, t, :], self.stat[:, 8 + t:9 + t], None, ALU.subtract)
                    ch(last)
                    dve.sem_inc(centred, 1)
                    for g in range(2):
                        dve.wait_ge(scaled, g + 1)
                        ch(dve.scalar_tensor_tensor(out=of(L, g), in0=of(Z, g), scalar=-1.0, in1=of(Z, g),
                                                    op0=ALU.mult, op1=ALU.min))
                        dve.sem_inc(negd, 1)
                    dve.wait_ge(rs, 1)
                    for t in range(NT):
                        last = dve.tensor_scalar(v[:, t, :], v[:, t, :], self.rstd[:, t:t + 1], None, ALU.mult)
                    ch(last)
                    dve.sem_inc(normed, 1)
                    for g in range(2):
                        dve.wait_ge(logd, g + 1)
                        ch(dve.scalar_tensor_tensor(out=of(W, g), in0=of(Z, g), scalar=0.0, in1=of(L, g),
                                                    op0=ALU.min, op1=ALU.subtract))
                        ch(dve.tensor_tensor(of(L, g), of(W, g), of(Z, g), ALU.subtract))
                        dve.sem_inc(sub, 1)
                    for g in range(2):
                        dve.wait_ge(tailed, g + 1)
                        ch(dve.tensor_tensor(of(W, g), of(self.psum, g), of(W, g), ALU.add))
                        dve.sem_inc(added, 1)
                    dve.wait_ge(gmixed, 1)
                    bias = self.gT[:, G_SGUB:G_SGUB + NH].unsqueeze(2).to_broadcast([P, NH, HD])
                    for t in range(NT):
                        last = dve.tensor_tensor(v[:, t, :].rearrange("p (h d) -> p h d", h=NH),
                                                 self.bank(6 + t).rearrange("p (h d) -> p h d", h=NH), bias, ALU.add)
                    ch(last)
                    dve.sem_inc(gread, 1)
                    ch(dve.tensor_tensor(C[:, :, 0:512], v[:, :, :], C[:, :, 0:512], ALU.mult))
                    dve.wait_ge(mixed, 1)
                    for t in range(NT):
                        dve.tensor_copy(PR[:, t, D_OFF:D_OFF + 512], self.bank(6 + t))

                @block.gpsimd
                def _(pool):
                    ch = self.pool_chain.on(pool)
                    ch(pool.affine_select(out=wT[:, :, :], in_=wT[:, :, :], pattern=[[0, NH], [1, P]],
                                          compare_op=ALU.is_ge, fill=0.0, base=0, channel_multiplier=-1))
                    pool.sem_inc(wmasked, 1)
                    pool.wait_ge(squared, 1)
                    self.rstd_on_pool(pool, BANK, NT, eps=1e-5)
                    pool.sem_inc(rs, 1)
                    for g in range(2):
                        pool.wait_ge(sub, g + 1)
                        ch(causal(pool, L, g))
                        pool.sem_inc(mask_ready, 1)
                    for g in range(2):
                        pool.wait_ge(exped, g + 1)
                        ch(causal(pool, Z, g))
                        pool.sem_inc(amask, 1)

    def attention(self, name, branches, dv, out, work, beside):
        S, PT, wide_tmp = work
        units = [(b, t) for b in range(len(branches)) for t in range(NT)]
        nk = lambda u: branches[units[u][0]][0][units[u][1]]
        chunks = lambda u: [(c, min(P, nk(u) - c)) for c in range(0, nk(u), P)]
        off = (0, NH * P)
        s_view = lambda u: S[:, off[units[u][1]]:off[units[u][1]] + NH * nk(u)].rearrange("p (h n) -> p h n", h=NH)
        s_at = lambda h, u: off[units[u][1]] + place(h) * nk(u)
        sbank = (0, 2)
        obank = (6, 7) if dv * NH <= BANK else (6, 0)
        scored, shifted, weighed, turned, kept, mixed, out_read = [self.sem(name + n) for n in (
            "_scores", "_maxima", "_weights", "_weights_turned", "_weights_kept", "_outputs", "_outputs_read")]
        st = self.att
        negmax, sums, inv, fac = [st[:, i] for i in range(4)]

        with self.block() as block:
            block.gpsimd(beside["gpsimd"])
            block.sync(beside["sync"])

            @block.tensor
            def _(pe):
                def scores(u):
                    b, t = units[u]
                    qk = branches[b][1]
                    for h in range(NH):
                        at = (sbank[t] + (h % 2) * (t + 1)) * BANK + h // 2 * nk(u)
                        o = self.psum[:, at:at + nk(u)]
                        for i, (q, k) in enumerate(qk):
                            last = pe.matmul(o, q(h, t), k(h, nk(u)), start=(i == 0), stop=(i == len(qk) - 1))
                    last.then_inc(scored, 1)

                scores(0)
                scores(1)
                for u, (b, t) in enumerate(units):
                    pe.wait_ge(weighed, u + 1)
                    for h in range(NH):
                        for c, (k0, kn) in enumerate(chunks(u)):
                            o = sbank[t] * BANK + (h * len(chunks(u)) + c) * P
                            last = pe.transpose(self.psum[0:kn, o:o + P],
                                                S[:, s_at(h, u) + k0:s_at(h, u) + k0 + kn],
                                                self.ident[:, :])
                    last.then_inc(turned, 1)
                    pe.wait_ge(kept, u + 1)
                    if u + 2 < len(units):
                        scores(u + 2)
                    if u >= 2:
                        pe.wait_ge(out_read, u - 1)
                    for h in range(NH):
                        for c, (k0, kn) in enumerate(chunks(u)):
                            p0 = off[t] + (h * len(chunks(u)) + c) * P
                            last = pe.matmul(self.bank(obank[t], dv, h * dv), PT[0:kn, p0:p0 + P], branches[b][3](h, c, kn),
                                             start=(c == 0), stop=(c == len(chunks(u)) - 1))
                    last.then_inc(mixed, 1)

            @block.vector
            def _(dve):
                ch = self.dve_chain.on(dve)

                def shift(u):
                    b, t = units[u]
                    dve.wait_ge(scored, u + 1)
                    for odd in range(2):
                        ps = self.bank(sbank[t] + odd * (t + 1), 4 * nk(u)).rearrange("p (h n) -> p h n", h=4)
                        h4 = slice(4 * odd, 4 * odd + 4)
                        last = dve.tensor_tensor(s_view(u)[:, h4], ps, branches[b][2](t)[:, h4], ALU.add)
                    ch(last)
                    ch(dve.tensor_reduce(negmax[:, t, :], s_view(u), AX.X, ALU.max, negate=True))
                    dve.sem_inc(shifted, 1)

                shift(0)
                shift(1)
                for u, (b, t) in enumerate(units):
                    factor = branches[b][4]
                    dve.wait_ge(weighed, u + 1)
                    ch(dve.reciprocal(inv[:, t, :], sums[:, t, :]))
                    f = inv
                    if factor is not None:
                        ch(dve.tensor_tensor(fac[:, t, :], inv[:, t, :], factor(t), ALU.mult))
                        f = fac
                    if u + 2 < len(units):
                        shift(u + 2)
                    dve.wait_ge(mixed, u + 1)
                    ps = self.bank(obank[t], NH * dv).rearrange("p (h d) -> p h d", h=NH)
                    fb = f[:, t, :].unsqueeze(2).to_broadcast([P, NH, dv])
                    if b > 0:
                        w = wide_tmp[:, 0:NH * dv].rearrange("p (h d) -> p h d", h=NH)
                        ch(dve.tensor_tensor(w, ps, fb, ALU.mult))
                        dve.sem_inc(out_read, 1)
                        ch(dve.tensor_tensor(out(t), out(t), w, ALU.add))
                    else:
                        ch(dve.tensor_tensor(out(t), ps, fb, ALU.mult))
                        dve.sem_inc(out_read, 1)

            @block.scalar
            def _(act):
                ch = self.act_chain.on(act)

                def exponentials(u):
                    t = units[u][1]
                    act.wait_ge(shifted, u + 1)
                    for h in range(NH):
                        s = S[:, s_at(h, u):s_at(h, u) + nk(u)]
                        last = act.activation(s, s, ACT.Exp, bias=negmax[:, t, place(h):place(h) + 1],
                                              accum_out=sums[:, t, h:h + 1])
                    ch(last)
                    act.sem_inc(weighed, 1)

                def keep(u):
                    t = units[u][1]
                    act.wait_ge(turned, u + 1)
                    rows = chunks(u)[0][1]
                    n = NH * len(chunks(u)) * P
                    ch(act.activation(PT[0:rows, off[t]:off[t] + n],
                                      self.psum[0:rows, sbank[t] * BANK:sbank[t] * BANK + n], ACT.Copy))
                    act.sem_inc(kept, 1)

                for u in range(len(units)):
                    exponentials(u)
                    keep(u)

    def nsa_views(self):
        w1 = self.XN[:, 0, :].rearrange("p (i k e) -> p i k e", i=2, e=HD)
        flipped = self.XN[:, 1, :].rearrange("p (h t) -> p h t", h=NH)
        vec = self.XN[0:NH, 1, 0:2 * T]
        tabT = self.XN[0:NH, 1, 2 * T:2 * T + 32]
        return w1, flipped, vec, tabT

    def nsa_inputs(self, pool):
        a = self.a
        w1, flipped, vec, tabT = self.nsa_views()
        vec_dram = self.nc.dram_tensor("bias_by_distance", [NH, 2 * T], F32, kind="Internal")
        table, vec_stored, loaded = self.sem("bias_table_loaded"), self.sem("bias_vector_stored"), self.sem("nsa_loaded")
        bucket = rel_buckets()
        ch = self.pool_chain.on(pool)
        pool.dma_start(tabT, a["rel_table"].rearrange("b h -> h b"), allow_slow_non_contiguous=True).then_inc(table, 16)
        for i in range(2):
            pool.dma_start(w1[:, i], a["cmp_w1"][0, i].rearrange("(k p) e -> p k e", p=P)).then_inc(loaded, 16)
            pool.dma_start(self.cmp_pos[:, i, :], a["cmp_pos"][0].rearrange("i l d -> (i l) d")).then_inc(loaded, 16)
        pool.dma_start(self.cmp_w2[:, :, :], a["cmp_w2"][0].rearrange("i d e -> d i e")).then_inc(loaded, 16)
        pool.wait_ge(table, 16)
        last = pool.memset(vec[:, T:2 * T], NEG)
        for b in range(bucket[-1] + 1):
            at = np.flatnonzero(bucket == b)
            if len(at):
                lo, n = T - 1 - int(at[-1]), len(at)
                last = pool.tensor_copy(vec[:, lo:lo + n], tabT[:, b:b + 1].to_broadcast([NH, n]))
        ch(last)
        pool.dma_start(vec_dram[:, :], vec).then_inc(vec_stored, 16)
        pool.wait_ge(vec_stored, 16)
        for odd in range(2):
            pool.dma_start(flipped[:, 4 * odd:4 * odd + 4, :],
                           bass.AP(tensor=vec_dram[:, :].tensor, offset=odd * 2 * T,
                                   ap=[[1, P], [4 * T, 4], [1, T]])).then_inc(loaded, 16)
        pool.wait_ge(loaded, 16 * 7)

    def nsa(self, PR):
        nc, a = self.nc, self.a
        with ExitStack() as ctx:
            tmp = lambda n, s: ctx.enter_context(nc.sbuf_tensor(n, s, F32))
            biasT = tmp("distance_bias", [P, NH, T])
            qT = tmp("nsa_q", [P, 4, T])
            kT = tmp("nsa_k", [P, 4, T])
            kcT = tmp("nsa_kc", [P, NG, N_CMP])
            vc = tmp("nsa_vc", [N_CMP, NG, HD])
            gates = tmp("nsa_gates", [P, NT, 3 * NH])
            S = self.XN[:, :, :].rearrange("p t c -> p (t c)")[:, 0:NH * 3 * P]
            PT = tmp("nsa_weights_turned", [P, NH * 3 * P])
            wtmp = self.XN[:, 1, D - 512:D]

            with ExitStack() as c2:
                tm2 = lambda n, s: c2.enter_context(nc.sbuf_tensor(n, s, F32))
                w1, flipped, _, _ = self.nsa_views()
                w2 = self.cmp_w2
                posT = tm2("cmp_pos_turned", [P, 2, CMP_LEN])
                zT = tm2("cmp_z", [P, 2, T])[:, :, :]
                Zc = tm2("cmp_windows", [P, 2, CMP_LEN // 2, NG, N_CMP])
                flip = tm2("flip", [P, P])
                H1 = tm2("cmp_hidden", [HD, 2, NG, N_CMP])
                kc = tm2("cmp_k", [N_CMP, NG, 2, HD])
                sq = tm2("cmp_squares", [N_CMP, NG, HD])
                first, hid, second, ssq, rsd, unflipped, flip_made, windows = [self.sem("cmp_" + n) for n in (
                    "first", "hidden", "second", "squares", "rstd", "bias_unflipped", "flip_made", "windows")]
                self.turn_stage([([self.cmp_pos[:, :, :].rearrange("l a d -> l (a d)")],
                                  posT[:, :, :].rearrange("p i l -> p (i l)"), None),
                                 ([PR[:, t, A_KV + P * i:A_KV + P * (i + 1)] for i in range(2) for t in range(NT)],
                                  zT, None)])
                qn = tm2("nsa_q_normed", [P, NT, 512])
                kn = tm2("nsa_k_normed", [P, NT, 2, NG, 2, HD])
                ks = tm2("nsa_k_squares", [P, NT, 2, NG, HD])
                qk_ssq, qk_rsd = self.sem("nsa_squares"), self.sem("nsa_rstd")
                kv = lambda t: PR[:, t, A_KV + 256:A_KV + 768].rearrange("p (b s g d) -> p b s g d", b=2, s=2, g=NG)[:, :, 0]
                q = PR[:, :, 0:512]
                with self.block() as block:
                    @block.tensor
                    def _(pe):
                        pe.wait_ge(flip_made, 1)
                        for b in range(4):
                            last = pe.matmul(self.bank(4 + b), flip[:, :],
                                             flipped[:, 2 * b:2 * b + 2, :].rearrange("p h t -> p (h t)"),
                                             start=True, stop=True)
                        last.then_inc(unflipped, 1)
                        pe.wait_ge(windows, 1)
                        for i in range(2):
                            for k in range(CMP_LEN // 2):
                                last = pe.matmul(self.bank(0, NG * N_CMP, i * NG * N_CMP)[0:HD], w1[:, i, k, :],
                                                 Zc[:, i, k].rearrange("p g n -> p (g n)"),
                                                 start=(k == 0), stop=(k == CMP_LEN // 2 - 1))
                        last.then_inc(first, 1)
                        pe.wait_ge(hid, 1)
                        for i in range(2):
                            for g in range(NG):
                                last = pe.matmul(self.bank(2, HD, (2 * i + g) * HD)[0:N_CMP],
                                                 H1[:, i, g, :], w2[:, i, :], start=True, stop=True)
                        last.then_inc(second, 1)

                    @block.scalar
                    def _(act):
                        ch = self.act_chain.on(act)
                        act.activation(gates[:, :, :], PR[:, :, A_GATE:A_GATE + 24], ACT.Sigmoid)
                        act.wait_ge(first, 1)
                        ch(act.activation(H1[:, :, :, :].rearrange("p i g n -> p (i g n)"),
                                          self.bank(0, 2 * NG * N_CMP)[0:HD], ACT.Gelu_apprx_tanh))
                        act.sem_inc(hid, 1)

                    @block.vector
                    def _(dve):
                        ch = self.dve_chain.on(dve)
                        for i in range(2):
                            for g in range(NG):
                                for s in range(2):
                                    r = slice(g * HD, (g + 1) * HD)
                                    z = zT[r, i, :].rearrange("p (n k s) -> p k s n", s=2, k=CMP_STRIDE // 2)[:, :, s, :]
                                    for a in range(CMP_LEN // CMP_STRIDE):
                                        k8 = slice(a * CMP_STRIDE // 2, (a + 1) * CMP_STRIDE // 2)
                                        pos = posT[r, i, a * CMP_STRIDE + s:(a + 1) * CMP_STRIDE:2].unsqueeze(2)
                                        last = dve.tensor_tensor(Zc[s * HD:(s + 1) * HD, i, k8, g, :], z[:, :, a:a + N_CMP],
                                                                 pos.to_broadcast([HD, CMP_STRIDE // 2, N_CMP]), ALU.add)
                        ch(last)
                        dve.sem_inc(windows, 1)
                        ch(dve.tensor_tensor(qn[:, :, :], q, q, ALU.mult))
                        for t in range(NT):
                            last = dve.tensor_tensor(ks[:, t], kv(t), kv(t), ALU.mult)
                        ch(last)
                        for t in range(NT):
                            dve.tensor_reduce(self.stat[:, 8 * t:8 * t + 8],
                                              qn[:, t, :].rearrange("p (h d) -> p h d", h=NH), AX.X, ALU.add)
                            last = dve.tensor_reduce(self.stat[:, 16 + 4 * t:20 + 4 * t],
                                                     ks[:, t].rearrange("p b g d -> p (b g) d"), AX.X, ALU.add)
                        ch(last)
                        dve.sem_inc(qk_ssq, 1)
                        dve.wait_ge(unflipped, 1)
                        ch(dve.tensor_copy(biasT[:, :, :].rearrange("p h t -> p (h t)"), self.psum[:, 4 * BANK:8 * BANK]))
                        dve.wait_ge(second, 1)
                        ps = self.bank(2, 4 * HD)[0:N_CMP].rearrange("p (i g d) -> p i g d", i=2, g=NG)
                        ch(dve.tensor_copy(vc[:, :, :], ps[:, 1]))
                        ch(dve.tensor_copy(kc[:, :, 0, :], ps[:, 0]))
                        ch(dve.tensor_tensor(sq[:, :, :], kc[:, :, 0, :], kc[:, :, 0, :], ALU.mult))
                        ch(dve.tensor_reduce(self.stat[0:N_CMP, 24:24 + NG], sq[:, :, :], AX.X, ALU.add))
                        dve.sem_inc(ssq, 1)
                        dve.wait_ge(qk_rsd, 1)
                        for t in range(NT):
                            dve.tensor_tensor(qn[:, t, :].rearrange("p (h d) -> p h d", h=NH),
                                              q[:, t, :].rearrange("p (h d) -> p h d", h=NH),
                                              self.rstd[:, 8 * t:8 * t + 8].unsqueeze(2).to_broadcast([P, NH, HD]), ALU.mult)
                            for b in range(2):
                                for dup in range(2):
                                    r = self.rstd[:, 16 + 4 * t + 2 * b:18 + 4 * t + 2 * b]
                                    dve.tensor_tensor(kn[:, t, b, :, dup, :], kv(t)[:, b],
                                                      r.unsqueeze(2).to_broadcast([P, NG, HD]), ALU.mult)
                        dve.wait_ge(rsd, 1)
                        rb = self.rstd[0:N_CMP, 24:24 + NG].unsqueeze(2).to_broadcast([N_CMP, NG, HD])
                        ch(dve.tensor_tensor(kc[:, :, 0, :], kc[:, :, 0, :], rb, ALU.mult))
                        ch(dve.tensor_copy(kc[:, :, 1, :], kc[:, :, 0, :]))

                    @block.gpsimd
                    def _(pool):
                        ch = self.pool_chain.on(pool)
                        ch(pool.memset(flip[:, :], 0.0))
                        ch(pool.affine_select(out=flip[:, :], in_=flip[:, :], pattern=[[1, P]], compare_op=ALU.not_equal,
                                              fill=1.0, base=1 - P, channel_multiplier=1))
                        pool.sem_inc(flip_made, 1)
                        pool.wait_ge(qk_ssq, 1)
                        self.rstd_on_pool(pool, HD, 24)
                        pool.sem_inc(qk_rsd, 1)
                        pool.wait_ge(ssq, 1)
                        st, rs = self.stat[0:N_CMP, 24:24 + NG], self.rstd[0:N_CMP, 24:24 + NG]
                        ch(pool.tensor_scalar(st, st, 1.0 / HD, 1e-6, ALU.mult, ALU.add))
                        ch(pool.tensor_tensor(out=rs, in0=st, in1=self.minus_half[0:N_CMP, 0:NG], op=ALU.pow))
                        pool.sem_inc(rsd, 1)
                jobs = [([kc[:, g].rearrange("p a d -> p (a d)")], kcT[:, g, :], [(N_CMP, self.gain(G_K))])
                        for g in range(NG)]
                for k in range(0, 4, 2):
                    jobs.append(([qn[:, t, kk * P:(kk + 1) * P] for kk in (k, k + 1) for t in range(NT)],
                                 qT[:, k:k + 2, :], [(2 * T, self.gain(G_Q))]))
                for b in range(2):
                    jobs.append(([kn[:, t, b, g].rearrange("p a d -> p (a d)") for g in range(NG) for t in range(NT)],
                                 kT[:, 2 * b:2 * b + 2, :], [(2 * T, self.gain(G_K))]))
                self.turn_stage(jobs)

            q = lambda h, t: qT[HD * (h % 2):HD * (h % 2) + HD, h // 2, t * P:(t + 1) * P]
            g = lambda h: h // (NH // NG)
            out = lambda t: PR[:, t, 0:512].rearrange("p (h d) -> p h d", h=NH)
            gate = lambda b: (lambda t: gates[:, t, b:3 * NH:3])
            with self.block() as block:
                @block.gpsimd
                def _(pool):
                    self.pool_chain.on(pool)(pool.affine_select(
                        out=gates[:, 0, 0:3 * NH:3], in_=gates[:, 0, 0:3 * NH:3], pattern=[[0, NH]],
                        compare_op=ALU.is_ge, fill=0.0, base=-(CMP_LEN - 1), channel_multiplier=1))
            first = P + CMP_LEN - 1
            cmp_bias = lambda t: (biasT[:, :, first:T:CMP_STRIDE] if t == 0 else biasT[:, :, CMP_LEN - 1:T:CMP_STRIDE])
            branches = [((N_CMP0, N_CMP), [(q, lambda h, n: kcT[HD * (h % 2):HD * (h % 2) + HD, g(h), 0:n])],
                         cmp_bias, lambda h, c, n: vc[0:n, g(h), :], gate(0))]
            all_bias = lambda t: biasT[:, :, P:T] if t == 0 else biasT[:, :, :]
            for b in range(2):
                off = A_KV + 384 + 256 * b
                branches.append(((P, T), [(q, lambda h, n, b=b: kT[HD * (h % 2):HD * (h % 2) + HD, 2 * b + g(h), 0:n])],
                                 all_bias,
                                 lambda h, c, n, off=off: PR[0:n, c, off + g(h) * HD:off + (g(h) + 1) * HD], gate(1 + b)))
            conv = self.conv(ctx, PR)

            def sync(sp):
                conv["sync"](sp)
                self.load_sgu(sp)
            self.attention("nsa", branches, HD, out, (S, PT, wtmp), {"gpsimd": conv["gpsimd"], "sync": sync})

    def ffn(self, streams, following):
        nc, ring = self.nc, self.ring
        up, down = streams
        rounds = up.rounds
        with ExitStack() as ctx:
            aT = ctx.enter_context(nc.sbuf_tensor("ffn_turned", [P, KF, T], F32))
            sg, pr = self.XN[:, :, 0:BANK], self.XN[:, :, BANK:2 * BANK]
            silu, prod, turned, kept = [self.sem("ffn_" + n) for n in ("silu", "product", "turned", "kept")]
            with ExitStack() as c2:
                hT = self.features(c2, KD)
                hi, lo = hT
                gains = self.gains_of(G_FFN, KD)
                x = lambda t: self.X[:, t, :]
                chunk = lambda t, k: self.X[:, t, k * P:(k + 1) * P]
                rstd = lambda t: self.rstd[:, t:t + 1]
                ring.parts(c2)
                with self.block() as block:
                    @block.sync
                    def _(sp):
                        ring.rest(sp, up, down)

                    @block.tensor
                    def _(pe):
                        def half_round(i, m, turned=True):
                            for q in range(4):
                                if not turned and q % 2 == 0:
                                    self.turn_split_wait(pe, gains, q // 2)
                                j, half = 2 * m + q // 2, q % 2
                                ring.wait(pe, i, j, half)
                                wh, wl = ring.piece(ring.hi, half, up), ring.piece(ring.lo, half, up)
                                for k in range(4):
                                    for t in range(NT):
                                        kk, tok = 4 * q + k, slice(t * P, (t + 1) * P)
                                        last = self.passes(pe, self.bank(2 * m + t), hi[:, kk, tok], lo[:, kk, tok],
                                                           wh[:, k, :], wl[:, k, :], kk == 0, kk == KD - 1)
                                last.then_inc(ring.used, 1)

                        def turn(i):
                            pe.wait_ge(prod, i)
                            pe.wait_ge(kept, i)
                            for k in range(4):
                                for t in range(NT):
                                    last = pe.transpose(self.bank(4 + k // 2, P, (k % 2) * T + t * P),
                                                        pr[:, t, k * P:(k + 1) * P], self.ident[:, :])
                            last.then_inc(turned, 1)

                        pe.sem_inc(turned, 1)
                        self.turn_split(chunk, hT, gains, pe, None, None)
                        half_round(0, 0, False)
                        half_round(0, 1)
                        with pe.Fori(1, rounds) as i:
                            pe.wait_ge(silu, i)
                            half_round(i, 0)
                            turn(i)
                            half_round(i, 1)
                        turn(rounds)

                    @block.scalar
                    def _(act):
                        def gate(i):
                            act.wait_ge(ring.used, ring.done(i, 4))
                            for t in range(NT):
                                last = act.activation(sg[:, t, :], self.bank(t), ACT.Silu, scale=rstd(t))
                            last.then_inc(silu, 1)

                        def keep(i):
                            act.wait_ge(turned, i + 1)
                            for b in range(2):
                                last = act.activation(aT[:, bass.ds((i - 1) * 4 + 2 * b, 2), :].rearrange("p k t -> p (k t)"),
                                                      self.bank(4 + b), ACT.Copy)
                            last.then_inc(kept, 1)

                        def split(i, pieces):
                            for q in pieces:
                                ring.split_hi(act, up, i, q // 2, q % 2)

                        act.sem_inc(kept, 1)
                        for half in range(2):
                            self.turn_split(chunk, hT, gains, None, act, None, half)
                            split(0, range(half, half + 1))
                        self.sum_squares(x, act, None)
                        split(0, range(2, 6))
                        self.rstd_wait(act)
                        gate(0)
                        split(0, range(6, 8))
                        with act.Fori(1, rounds) as i:
                            split(i, range(6))
                            act.wait_ge(prod, i)
                            gate(i)
                            keep(i)
                            split(i, range(6, 8))
                        keep(rounds)

                    @block.vector
                    def _(dve):
                        def product(i):
                            dve.wait_ge(silu, i)
                            dve.wait_ge(ring.used, ring.done(i - 1, 8))
                            dve.wait_ge(turned, i)
                            for t in range(NT):
                                last = dve.scalar_tensor_tensor(out=pr[:, t, :], in0=self.bank(2 + t), scalar=rstd(t),
                                                                in1=sg[:, t, :], op0=ALU.mult, op1=ALU.mult)
                            last.then_inc(prod, 1)

                        def split(i, pieces):
                            for q in pieces:
                                ring.split_lo(dve, up, i, q // 2, q % 2)

                        for half in range(2):
                            self.turn_split(chunk, hT, gains, None, None, dve, half)
                            split(0, range(half, half + 1))
                        self.sum_squares(x, None, dve)
                        split(0, range(2, 8))
                        self.rstd_wait(dve)
                        with dve.Fori(1, rounds) as i:
                            split(i, range(2))
                            product(i)
                            split(i, range(2, 8))
                        product(rounds)

                    @block.gpsimd
                    def _(pool):
                        self.rstd_of_tiles(pool, D)
            self.turn_split_close(gains)
            self.norm_close()
            ring.close(up)
            ring.parts(ctx)
            ahi, alo = [ctx.enter_context(nc.sbuf_tensor("ffn_turned_" + n, [P, 2, T], F32R)) for n in ("hi", "lo")]
            a_hi, applied = self.sem("ffn_hidden_hi"), self.sem("ffn_down_applied")
            pieces = [(n // 8, n % 8 // 2, n % 2) for n in range(KF)]
            skip = lambda n: 2 * (4 - down.last) if n == KF - 1 else 0
            with self.block() as block:
                @block.sync
                def _(sp):
                    ring.rest(sp, down, following)

                @block.scalar
                def _(act):
                    for n, (i, j, half) in enumerate(pieces):
                        ring.split_hi(act, down, i, j, half, skip(n))
                        act.activation(ahi[:, n % 2, :], aT[:, n, :], ACT.Copy).then_inc(a_hi, 1)

                @block.vector
                def _(dve):
                    for n, (i, j, half) in enumerate(pieces):
                        dve.wait_ge(a_hi, n + 1)
                        dve.tensor_tensor(alo[:, n % 2, :], aT[:, n, :], ahi[:, n % 2, :].bitcast(F32), ALU.subtract)
                        ring.split_lo(dve, down, i, j, half, skip(n))
                    for t in range(NT):
                        if t == 0:
                            dve.wait_ge(applied, 1)
                        else:
                            dve.wait_ge(ring.used, ring.done(down.rounds, 0))
                        self.dve_chain.on(dve)(dve.tensor_tensor(self.X[:, t, :], self.psum[:, 4 * t * BANK:4 * (t + 1) * BANK],
                                                                 self.X[:, t, :], ALU.add))

                @block.tensor
                def _(pe):
                    for n, (i, j, half) in enumerate(pieces):
                        ring.wait(pe, i, j, half)
                        wh, wl = ring.piece(ring.hi, half, down), ring.piece(ring.lo, half, down)
                        for t in range(NT):
                            tok = slice(t * P, (t + 1) * P)
                            for c in range(4):
                                col = slice(c * BANK, (c + 1) * BANK)
                                last = self.passes(pe, self.bank(4 * t + c), ahi[:, n % 2, tok], alo[:, n % 2, tok],
                                                   wh[:, 0, col], wl[:, 0, col], n == 0, n == KF - 1)
                            if n == KF - 1 and t == 0:
                                last.then_inc(applied, 1)
                        last.then_inc(ring.used, 1 + skip(n))
            ring.close(down)

    def pool_inputs(self, ctx):
        tmp = lambda n, s: ctx.enter_context(self.nc.sbuf_tensor(n, s, F32))
        band = tmp("pool_band", [P, 4, T + P])
        wp = tmp("pool_w", [P, 4, 2, T])
        loaded = self.sem("pool_loaded")

        def sync(sp):
            sp.dma_start(wp[:, :, :, :].rearrange("p g k d -> p (g k) d"),
                         self.a["w_pool_2"][0].rearrange("g (k p) d -> p (g k) d", p=P)).then_inc(loaded, 16)
            sp.wait_ge(loaded, 16)

        def gpsimd(pool):
            ch = self.pool_chain.on(pool)
            for g, w in enumerate(WINDOWS):
                last = pool.memset(band[:, g, :], 1.0 / w)
            ch(last)
            for g, w in enumerate(WINDOWS):
                for t in range(w - 1):
                    last = pool.memset(band[:, g, t:t + 1], 1.0 / (t + 1))
            ch(last)
            parts = [(g, w, lo, n) for g, w in enumerate(WINDOWS) for lo, n in ((0, T), (T, P))]
            for g, w, lo, n in parts:
                v = band[:, g, lo:lo + n]
                last = pool.affine_select(out=v, in_=v, pattern=[[1, n]], compare_op=ALU.is_ge, fill=0.0,
                                          base=0, channel_multiplier=-1)
            ch(last)
            for g, w, lo, n in parts:
                v = band[:, g, lo:lo + n]
                last = pool.affine_select(out=v, in_=v, pattern=[[-1, n]], compare_op=ALU.is_ge, fill=0.0,
                                          base=w - 1, channel_multiplier=1)
            ch(last)
            for g, w, lo, n in parts:
                pool.tensor_tensor(out=band[:, g, lo:lo + P], in0=band[:, g, lo:lo + P], in1=self.ident[:, :],
                                   op=ALU.subtract)

        self.pool_band, self.pool_w = band, wp
        return {"gpsimd": gpsimd, "sync": sync}

    def pool_mix(self, Z):
        nc, band, wp = self.nc, self.pool_band, self.pool_w
        with ExitStack() as ctx:
            dT = ctx.enter_context(nc.sbuf_tensor("pool_turned", [P, 4, 2, T], F32))
            diff, kept, done = [self.sem("pool_" + n) for n in ("means", "kept", "done")]
            with self.block() as block:
                @block.tensor
                def _(pe):
                    for g in range(4):
                        for c in range(2):
                            o = (2 * g + c) * T
                            col = slice(g * T + c * P, g * T + (c + 1) * P)
                            pe.matmul(self.psum[:, o:o + T], Z[:, 0, col], band[:, g, 0:T], start=True, stop=False)
                            last = pe.matmul(self.psum[:, o + P:o + T], Z[:, 1, col], band[:, g, T:T + P],
                                             start=False, stop=True)
                    last.then_inc(diff, 1)
                    pe.wait_ge(kept, 1)
                    for t in range(NT):
                        for g in range(4):
                            for c in range(2):
                                last = pe.matmul(self.bank(4 + 2 * t + g // 2, T, (g % 2) * T),
                                                 dT[:, g, c, t * P:(t + 1) * P], wp[:, g, c, :], start=(c == 0), stop=(c == 1))
                    last.then_inc(done, 1)

                @block.scalar
                def _(act):
                    act.wait_ge(diff, 1)
                    self.act_chain.on(act)(act.activation(dT[:, :, :, :].rearrange("p g c t -> p (g c t)"),
                                                          self.psum[:, 0:8 * T], ACT.Copy))
                    act.sem_inc(kept, 1)

                @block.vector
                def _(dve):
                    dve.wait_ge(done, 1)
                    for t in range(NT):
                        dve.tensor_copy(Z[:, t, 0:POOL_W], self.psum[:, (4 + 2 * t) * BANK:(6 + 2 * t) * BANK])

    def mla(self, Q, KV, Zr, M, beside):
        nc = self.nc
        with ExitStack() as ctx:
            tmp = lambda n, s: ctx.enter_context(nc.sbuf_tensor(n, s, F32))
            qT, kT = tmp("mla_q", [P, NH, T]), tmp("mla_k", [P, NH, T])
            qrT, krT = tmp("mla_q_rope", [P, 4, T]), tmp("mla_k_rope", [P, 4, T])
            mask = tmp("mla_mask", [P, T + P])
            S = self.XN[:, :, :].rearrange("p t c -> p (t c)")[:, 0:NH * 3 * P]
            PT = tmp("mla_weights_turned", [P, NH * 3 * P])
            q4 = Q.rearrange("p t (h d) -> p t h d", h=NH)
            kv4 = KV.rearrange("p t (h d) -> p t h d", h=NH)
            with ExitStack() as c2:
                tm2 = lambda n, s: c2.enter_context(nc.sbuf_tensor(n, s, F32))
                kg = tm2("rope_k", [P, NT, 64])
                kss = tm2("rope_k_squares", [P, NT])
                rot = tm2("rope_k_turned", [P, NT, 64])
                rr = tm2("rope_parts", [P, 2, NH, HALF])
                kr = tm2("rope_k_heads", [P, NT, NH, 64])
                qr = tm2("rope_q_heads", [P, NT, NH, 64])
                ssq, rsd, masked = self.sem("mla_squares"), self.sem("mla_rstd"), self.sem("mla_masked")

                def rope(dve, ch, dst, src, heads, t):
                    a1, a2 = src[:, :, 0:HALF], src[:, :, HALF:64]
                    cos = self.cosT[:, t:t + 1, :].to_broadcast([P, heads, HALF])
                    sin = self.sinT[:, t:t + 1, :].to_broadcast([P, heads, HALF])
                    r = rr[:, :, 0:heads, :]
                    ch(dve.tensor_tensor(r[:, 0], a2, sin, ALU.mult))
                    ch(dve.tensor_tensor(dst[:, :, 0:HALF], a1, cos, ALU.mult))
                    ch(dve.tensor_tensor(dst[:, :, 0:HALF], dst[:, :, 0:HALF], r[:, 0], ALU.subtract))
                    ch(dve.tensor_tensor(r[:, 1], a1, sin, ALU.mult))
                    ch(dve.tensor_tensor(dst[:, :, HALF:64], a2, cos, ALU.mult))
                    ch(dve.tensor_tensor(dst[:, :, HALF:64], dst[:, :, HALF:64], r[:, 1], ALU.add))

                angled = self.sem("sine_and_cosine")
                with self.block() as block:
                    @block.scalar
                    def _(act):
                        act.activation(self.sinT[:, :, :], self.angles[:, 0, :, :], ACT.Sin)
                        act.activation(self.cosT[:, :, :], self.angles[:, 1, :, :], ACT.Sin).then_inc(angled, 1)
                        for t in range(NT):
                            for h in range(NH):
                                o = (t * NH + h) * QKH
                                last = act.activation(self.psum[:, o:o + QKH], q4[:, t, h, :], ACT.Square,
                                                      accum_out=self.stat[:, 8 * t + h:8 * t + h + 1])
                        last.then_inc(ssq, 1)
                        for t in range(NT):
                            for h in range(NH):
                                act.activation(self.XN[:, t, h * P:(h + 1) * P], kv4[:, t, h, 0:P], ACT.Square,
                                               accum_out=self.stat[:, 16 + 8 * t + h:17 + 8 * t + h])
                            last = act.activation(self.psum[:, 7 * BANK + t * 64:7 * BANK + (t + 1) * 64], Zr[:, t, :],
                                                  ACT.Square, accum_out=kss[:, t:t + 1])
                        last.then_inc(ssq, 1)
                        act.wait_ge(rsd, 2)
                        for t in range(NT):
                            for h in range(NH):
                                k = kv4[:, t, h, 0:P]
                                act.activation(k, k, ACT.Copy, scale=self.rstd[:, 16 + 8 * t + h:17 + 8 * t + h])

                    @block.vector
                    def _(dve):
                        ch = self.dve_chain.on(dve)
                        ch(dve.tensor_tensor(kg[:, :, :], Zr, self.gbk[:, :].unsqueeze(1).to_broadcast([P, NT, 64]), ALU.mult))
                        dve.wait_ge(angled, 1)
                        for t in range(NT):
                            rope(dve, ch, rot[:, t:t + 1, :], kg[:, t:t + 1, :], 1, t)
                        dve.wait_ge(rsd, 1)
                        for t in range(NT):
                            rq = self.rstd[:, 8 * t:8 * t + 8].unsqueeze(2)
                            last = dve.tensor_tensor(q4[:, t], q4[:, t], rq.to_broadcast([P, NH, QKH]), ALU.mult)
                        ch(last)
                        for t in range(NT):
                            last = dve.tensor_tensor(q4[:, t, :, P:QKH], q4[:, t, :, P:QKH],
                                                     self.gbq[:, :].unsqueeze(1).to_broadcast([P, NH, 64]), ALU.mult)
                        ch(last)
                        for t in range(NT):
                            rope(dve, ch, qr[:, t], q4[:, t, :, P:QKH], NH, t)
                        dve.wait_ge(rsd, 2)
                        for t in range(NT):
                            rk = self.rstd[:, 16 + 8 * t:24 + 8 * t].unsqueeze(2)
                            dve.tensor_tensor(kr[:, t], rot[:, t:t + 1, :].to_broadcast([P, NH, 64]),
                                              rk.to_broadcast([P, NH, 64]), ALU.mult)

                    @block.gpsimd
                    def _(pool):
                        ch = self.pool_chain.on(pool)
                        ch(pool.memset(mask[:, :], 0.0))
                        pool.memset(mask[0:64, 64:P], NEG)
                        ch(pool.memset(mask[0:64, T + 64:T + P], NEG))
                        pool.wait_ge(ssq, 1)
                        self.rstd_on_pool(pool, QKH, 16, extra=QKH ** -0.5)
                        pool.sem_inc(rsd, 1)
                        pool.wait_ge(ssq, 2)
                        for t in range(NT):
                            k = self.stat[:, 16 + 8 * t:24 + 8 * t]
                            last = pool.tensor_scalar(k, k, kss[:, t:t + 1], 0.0, ALU.add, ALU.add)
                        ch(last)
                        self.rstd_on_pool(pool, QKH, 16, at=16)
                        pool.sem_inc(rsd, 1)
                jobs = []
                for h in range(0, NH, 2):
                    jobs.append(([q4[:, t, hh, 0:P] for hh in (h, h + 1) for t in range(NT)], qT[:, h:h + 2, :],
                                 [(2 * T, self.gain(G_QN))]))
                    jobs.append(([kv4[:, t, hh, 0:P] for hh in (h, h + 1) for t in range(NT)], kT[:, h:h + 2, :],
                                 [(2 * T, self.gain(G_KN))]))
                for k in range(0, 4, 2):
                    for src, dst in ((qr, qrT), (kr, krT)):
                        jobs.append(([src[:, t, 2 * kk:2 * kk + 2, :].rearrange("p a d -> p (a d)")
                                      for kk in (k, k + 1) for t in range(NT)], dst[:, k:k + 2, :], None))
                self.turn_stage(jobs)
            r = lambda h: slice(HD * (h % 2), HD * (h % 2) + HD)
            tok = lambda t: slice(t * P, (t + 1) * P)
            branch = ((P, T),
                      [(lambda h, t: qT[:, h, tok(t)], lambda h, n: kT[:, h, 0:n]),
                       (lambda h, t: qrT[r(h), h // 2, tok(t)], lambda h, n: krT[r(h), h // 2, 0:n])],
                      lambda t: (mask[:, 0:P] if t == 0 else mask[:, P:P + T]).unsqueeze(1).to_broadcast([P, NH, (P, T)[t]]),
                      lambda h, c, n: KV[0:n, c, h * T + P:(h + 1) * T], None)
            self.attention("mla", [branch], P, lambda t: M[:, t, POOL_W:D].rearrange("p (h d) -> p h d", h=NH),
                           (S, PT, None), beside)

    def peer(self, following, w_pq):
        nc, a = self.nc, self.a
        J = 2 * NH
        PARTS = J * P // BANK
        with ExitStack() as ctx:
            tmp = lambda n, s, d=F32: ctx.enter_context(nc.sbuf_tensor(n, s, d))
            eidx = tmp("expert_index", [P, NT, SLOTS], U32)
            gts = tmp("expert_gates", [P, NT, NH, TOPK])
            wts = tmp("expert_weights", [P, NT, SLOTS])
            HP = NH // PARTS
            JP = 2 * HP
            v, vi = tmp("top_values", [P, JP, TOPK]), tmp("top_index", [P, JP, TOPK], U32)
            vif = tmp("top_index_f", [P, JP, TOPK])
            cv, ci = tmp("pair_values", [P, HP, TOPK]), tmp("pair_index", [P, HP, TOPK], U32)
            cab, cf = tmp("pair_parts", [P, 2, HP, TOPK], U32), tmp("pair_parts_f", [P, 2, HP, TOPK])
            io, iof = tmp("count", [P, TOPK], I32), tmp("count_f", [P, TOPK])
            e12 = tmp("pair_experts", [P, 2, HP * TOPK])
            sm = tmp("gate_sums", [P, HP])
            scored, counted, chosen, ex, exped = [self.sem(n) for n in (
                "peer_scored", "counted", "experts_chosen", "peer_shifted", "peer_exponentials")]
            LOW = -3.0e38
            heads = lambda part: slice(part * HP, (part + 1) * HP)

            def retrieval(dve, ch, t, part):
                bank = self.bank(4 * t + part)
                gates = gts[:, t, heads(part)]

                def top16(rows):
                    def step(op):
                        def run():
                            for row in rows:
                                last = op(*row)
                            ch(last)
                        return run
                    return [step(lambda s, val, ind: dve.max(val[:, 0:8], s)),
                            step(lambda s, val, ind: dve.max_index(ind[:, 0:8], val[:, 0:8], s)),
                            step(lambda s, val, ind: dve.match_replace(s, val[:, 0:8], s, LOW)),
                            step(lambda s, val, ind: dve.max(val[:, 8:16], s)),
                            step(lambda s, val, ind: dve.max_index(ind[:, 8:16], val[:, 8:16], s))]

                def pairs():
                    ch(dve.tensor_copy(vif[:, :, :], vi[:, :, :]))
                    ch(dve.tensor_tensor(bank.rearrange("p (h a b) -> p h a b", h=HP, a=TOPK),
                                         v[:, 0:JP:2, :].unsqueeze(3).to_broadcast([P, HP, TOPK, TOPK]),
                                         v[:, 1:JP:2, :].unsqueeze(2).to_broadcast([P, HP, TOPK, TOPK]), ALU.add))

                def parts():
                    dve.tensor_scalar(cab[:, 0], ci[:, :, :], 4, None, ALU.logical_shift_right)
                    ch(dve.tensor_scalar(cab[:, 1], ci[:, :, :], TOPK - 1, None, ALU.bitwise_and))
                    ch(dve.tensor_copy(cf[:, :].rearrange("p a h k -> p (a h k)"), cab[:, :].rearrange("p a h k -> p (a h k)")))

                def index(half):
                    def run():
                        m = bank.rearrange("p (h k a) -> p h k a", h=HP, k=TOPK)
                        m3 = bank.rearrange("p (hk a) -> p hk a", a=TOPK)
                        ch(dve.tensor_tensor(m3, cf[:, half].rearrange("p h k -> p (h k)").unsqueeze(2)
                                             .to_broadcast([P, HP * TOPK, TOPK]),
                                             iof[:, :].unsqueeze(1).to_broadcast([P, HP * TOPK, TOPK]), ALU.is_equal))
                        ch(dve.tensor_tensor(m, m, vif[:, half:JP:2, :].unsqueeze(2)
                                             .to_broadcast([P, HP, TOPK, TOPK]), ALU.mult))
                        ch(dve.tensor_reduce(e12[:, half], m3, AX.X, ALU.add))
                    return run

                def choose():
                    ch(dve.scalar_tensor_tensor(out=eidx[:, t, part * HP * TOPK:(part + 1) * HP * TOPK], in0=e12[:, 0],
                                                scalar=float(NKEYS), in1=e12[:, 1], op0=ALU.mult, op1=ALU.add))
                    dve.sem_inc(chosen, 1)
                    ch(dve.tensor_tensor(gates, cv[:, :, :], cv[:, :, 0:1].to_broadcast([P, HP, TOPK]), ALU.subtract))
                    dve.sem_inc(ex, 1)
                    dve.wait_ge(exped, t * PARTS + part + 1)
                    ch(dve.tensor_reduce(sm[:, :], gates, AX.X, ALU.add))
                    ch(dve.reciprocal(sm[:, :], sm[:, :]))
                    ch(dve.tensor_tensor(gates, gates, sm[:, :].unsqueeze(2).to_broadcast([P, HP, TOPK]), ALU.mult))

                return (top16([(bank[:, j * P:(j + 1) * P], v[:, j, :], vi[:, j, :]) for j in range(JP)]) + [pairs]
                        + top16([(bank[:, h * 256:(h + 1) * 256], cv[:, h, :], ci[:, h, :]) for h in range(HP)])
                        + [parts, index(0), index(1), choose])

            def exponentials(act, t, part):
                act.wait_ge(ex, t * PARTS + part + 1)
                g = gts[:, t, heads(part)]
                self.act_chain.on(act)(act.activation(g, g, ACT.Exp))
                act.sem_inc(exped, 1)

            with ExitStack() as c2:
                tm2 = lambda n, s, d=F32: c2.enter_context(nc.sbuf_tensor(n, s, d))
                sk = tm2("sub_keys", [P, J, P])
                loaded = self.sem("sub_keys_loaded")
                with self.block() as block:
                    @block.scalar
                    def _(act):
                        for h, name in enumerate(("sub_k1_2", "sub_k2_2")):
                            act.dma_start(sk[:, h:J:2, :], a[name][0].rearrange("h n d -> n h d")).then_inc(loaded, 16)
                qp = tm2("peer_q", [P, NT, D])
                with ExitStack() as c3:
                    hT = self.features(c3, KD)
                    self.linear(w_pq, following, hT, lambda t, k: self.X[:, t, k * P:(k + 1) * P], self.gains_of(G_FFN2, KD),
                                BANK, self.scaled_to(qp, BANK), ("act", "dve"), lambda t: self.X[:, t, :])
                skT = tm2("sub_keys_turned", [P, J, P])
                qpT = tm2("peer_q_turned", [P, J, T])
                with self.block() as block:
                    @block.tensor
                    def _(pe):
                        pe.wait_ge(loaded, 32)
                self.turn_stage(self.feature_jobs(lambda t: qp[:, t, :], qpT[:, :, :], KD)
                                + [([sk[:, j + i, :] for i in range(4)], skT[:, j:j + 4, :], None) for j in range(0, J, 4)])
                with self.block() as block:
                    @block.tensor
                    def _(pe):
                        for t in range(NT):
                            for j in range(J):
                                last = pe.matmul(self.bank(4 * t + j // 4, P, j % 4 * P), qpT[:, j, t * P:(t + 1) * P],
                                                 skT[:, j, :], start=True, stop=True)
                                if t == 0 and j == 3:
                                    last.then_inc(scored, 1)

                    @block.gpsimd
                    def _(pool):
                        self.pool_chain.on(pool)(pool.iota(io[:, :], pattern=[[1, TOPK]], base=0, channel_multiplier=0))
                        pool.sem_inc(counted, 1)

                    @block.vector
                    def _(dve):
                        ch = self.dve_chain.on(dve)
                        dve.wait_ge(counted, 1)
                        ch(dve.tensor_copy(iof[:, :], io[:, :]))
                        dve.wait_ge(scored, 1)
                        for step in retrieval(dve, ch, 0, 0):
                            step()

                    @block.scalar
                    def _(act):
                        exponentials(act, 0, 0)

            proj = tmp("ple_projection", [P, NT, D])
            with ExitStack() as c4:
                tmp4 = lambda n, s, d=F32: c4.enter_context(nc.sbuf_tensor(n, s, d))
                NB = 8
                rows = tmp4("expert_rows", [P, NB, D])
                cur = tmp4("gather_index", [P, NB], U32)
                gb = tmp4("ffn_gain", [P, D])
                dots = tmp4("expert_products", [P, NB])
                gathered = [self.sem(f"expert_row_gathered{b}") for b in range(NB)]
                used, gained, xready, acted = [self.sem("expert_" + n) for n in ("row_used", "gain_loaded", "input", "activated")]
                pin, pT, wp = tmp4("ple_in", [P, NT, T]), tmp4("ple_in_turned", [P, 2, T]), tmp4("ple_proj", [P, 2, 2, BANK])
                wploaded = [self.sem(f"ple_weight_loaded{b}") for b in range(2)]
                ploaded, pturned, pkept, projected = [self.sem("ple_" + n) for n in ("loaded", "turned", "kept", "projected")]
                kept, started = self.sem("expert_products_kept"), self.sem("gathers_started")
                loops = SLOTS // NB
                with self.block() as block:
                    @block.sync
                    def _(sp):
                        sp.dma_start(gb[:, :], a["ffn_norm_gain_2"].to_broadcast([P, D])).then_inc(gained, 16)
                        sp.dma_start(pin[:, :, :], a["p_2"][0, 0].rearrange("(t p) c -> p t c", p=P)).then_inc(ploaded, 16)
                        for c in range(4):
                            if c >= 2:
                                sp.wait_ge(projected, c - 1)
                            sp.dma_start(wp[:, c % 2], a["w_ple_proj_2"][0][:, c * BANK:(c + 1) * BANK]
                                         .rearrange("(k p) n -> p k n", p=P)).then_inc(wploaded[c % 2], 16)

                    @block.tensor
                    def _(pe):
                        pe.wait_ge(ploaded, 16)
                        pe.wait_ge(ex, PARTS)
                        for k in range(2):
                            for t in range(NT):
                                last = pe.transpose(self.bank(0, P, k * T + t * P), pin[:, t, k * P:(k + 1) * P],
                                                    self.ident[:, :])
                        last.then_inc(pturned, 1)
                        for c in range(4):
                            pe.wait_ge(wploaded[c % 2], 16 * (c // 2 + 1))
                            pe.wait_ge(pkept, max(c, 1))
                            for t in range(NT):
                                for k in range(2):
                                    last = pe.matmul(self.bank(c % 2 * 2 + t), pT[:, k, t * P:(t + 1) * P],
                                                     wp[:, c % 2, k, :], start=(k == 0), stop=(k == 1))
                            last.then_inc(projected, 1)

                    @block.gpsimd
                    def _(pool):
                        ch_n = self.pool_chain
                        phase = 0
                        pool.sem_inc(used, NB)
                        for t in range(NT):
                            for table in ("expert_u_2", "expert_v_2"):
                                for part in range(PARTS):
                                    if table == "expert_u_2":
                                        pool.wait_ge(chosen, t * PARTS + part + 1)
                                    with pool.Fori(part * loops // PARTS, (part + 1) * loops // PARTS) as i:
                                        for b in range(NB):
                                            pool.wait_ge(used, i * NB + (phase * SLOTS + b + 1))
                                            pool.tensor_copy(cur[:, b:b + 1], eidx[:, t, bass.ds(i * NB + b, 1)])\
                                                .then_inc(ch_n.sem, 1)
                                            pool.wait_ge(ch_n.sem, i * NB + (ch_n.n + b + 1))
                                            pool.sem_inc(started, 1)
                                            pool.indirect_dma_start(
                                                out=rows[:, b, :], out_offset=None, in_=a[table][0],
                                                in_offset=bass.IndirectOffsetOnAxis(ap=cur[:, b:b + 1], axis=0))\
                                                .then_inc(gathered[b], 16)
                                ch_n.n += SLOTS
                                phase += 1

                    @block.vector
                    def _(dve):
                        ch = self.dve_chain.on(dve)
                        phase = 0
                        dve.sem_inc(kept, 1)
                        dve.wait_ge(gained, 16)
                        for t in range(NT):
                            ch(dve.scalar_tensor_tensor(out=self.XN[:, t, :], in0=self.X[:, t, :], scalar=self.rstd[:, t:t + 1],
                                                        in1=gb[:, :], op0=ALU.mult, op1=ALU.mult))

                        def products(t, phase, lo, hi):
                            with dve.Fori(lo, hi) as i:
                                for b in range(NB):
                                    dve.wait_ge(gathered[b], i * 16 + 16 * (phase * loops + 1))
                                    if b == 0:
                                        dve.wait_ge(kept, i + (t * loops + 1))
                                    dve.tensor_tensor_reduce(rows[:, b, :], rows[:, b, :], self.XN[:, t, :], 1.0, 0.0,
                                                             ALU.mult, ALU.add, dots[:, b:b + 1]).then_inc(used, 1)
                                dve.wait_ge(used, i * NB + (phase * SLOTS + 2 * NB))
                                dve.tensor_copy(wts[:, t, bass.ds(i * NB, NB)], dots[:, :]).then_inc(kept, 1)

                        def added(t, phase, lo, hi):
                            with dve.Fori(lo, hi) as i:
                                for b in range(NB):
                                    dve.wait_ge(gathered[b], i * 16 + 16 * (phase * loops + 1))
                                    dve.wait_ge(used, i * NB + (phase * SLOTS + NB + b))
                                    dve.scalar_tensor_tensor(out=self.X[:, t, :], in0=rows[:, b, :],
                                                             scalar=wts[:, t, bass.ds(i * NB + b, 1)],
                                                             in1=self.X[:, t, :], op0=ALU.mult, op1=ALU.add).then_inc(used, 1)

                        part_loops = loops // PARTS
                        for t in range(NT):
                            if t == 0:
                                for part in range(PARTS):
                                    lo = part * part_loops
                                    products(t, phase, lo, lo + part_loops // 2)
                                    if part + 1 < PARTS:
                                        for step in retrieval(dve, ch, 0, part + 1):
                                            step()
                                    products(t, phase, lo + part_loops // 2, lo + part_loops)
                            else:
                                products(t, phase, 0, loops)
                            phase += 1
                            dve.sem_inc(xready, 1)
                            dve.wait_ge(acted, t + 1)
                            ch(dve.tensor_tensor(wts[:, t, :], wts[:, t, :], gts[:, t].rearrange("p h k -> p (h k)"), ALU.mult))
                            if t == 0:
                                for part in range(PARTS):
                                    steps = retrieval(dve, ch, 1, part)
                                    for half in range(2):
                                        lo = part * part_loops + half * part_loops // 2
                                        added(t, phase, lo, lo + part_loops // 2)
                                        for step in steps[half * len(steps) // 2:(half + 1) * len(steps) // 2]:
                                            step()
                            else:
                                added(t, phase, 0, loops)
                            phase += 1

                    @block.scalar
                    def _(act):
                        def gelu(t):
                            act.wait_ge(xready, t + 1)
                            act.wait_ge(kept, loops * (t + 1) + 1)
                            self.act_chain.on(act)(act.activation(wts[:, t, :], wts[:, t, :], ACT.Gelu_apprx_tanh))
                            act.sem_inc(acted, 1)

                        for part in range(1, PARTS):
                            exponentials(act, 0, part)
                        ch = self.act_chain.on(act)
                        act.wait_ge(pturned, 1)
                        ch(act.activation(pT[:, :, :].rearrange("p k t -> p (k t)"), self.bank(0), ACT.Copy))
                        act.sem_inc(pkept, 1)
                        for c in range(4):
                            act.wait_ge(projected, c + 1)
                            for t in range(NT):
                                last = act.activation(proj[:, t, c * BANK:(c + 1) * BANK], self.bank(c % 2 * 2 + t), ACT.Copy)
                            ch(last)
                            act.sem_inc(pkept, 1)
                        gelu(0)
                        for part in range(PARTS):
                            exponentials(act, 1, part)
                        gelu(1)
            self.ple(following, proj)

    def scaled_to(self, dst, width):
        def evac(eng, t, c, ps):
            to, scale = dst[:, t, bass.ds(c * width, width)], self.rstd[:, t:t + 1]
            if eng is self.nc.scalar:
                return eng.activation(to, ps, ACT.Copy, scale=scale)
            return eng.tensor_scalar(to, ps, scale, None, ALU.mult)
        return evac

    def add_out(self, eng, t, c, ps):
        x = self.X[:, t, bass.ds(c * BANK, BANK)]
        return eng.tensor_tensor(x, ps, x, ALU.add)

    def ple(self, w_gate, proj):
        with ExitStack() as ctx:
            gate = ctx.enter_context(self.nc.sbuf_tensor("ple_gate", [P, NT, D], F32))
            gated, stored = self.sem("ple_gated"), self.sem("output_stored")
            with ExitStack() as c2:
                hT = self.features(c2, KD)
                self.linear(w_gate, None, hT, lambda t, k: self.X[:, t, k * P:(k + 1) * P], self.gains_of(G_PLE, KD), BANK,
                            lambda eng, t, c, ps: eng.activation(gate[:, t, bass.ds(c * BANK, BANK)], ps, ACT.Sigmoid,
                                                                 scale=self.rstd[:, t:t + 1]),
                            ("act", "act"), lambda t: self.X[:, t, :])
            halves = [(t, slice(h * D // 2, (h + 1) * D // 2)) for t in range(NT) for h in range(2)]
            with self.block() as block:
                @block.vector
                def _(dve):
                    ch = self.dve_chain.on(dve)
                    for t, col in halves:
                        ch(dve.tensor_tensor(gate[:, t, col], proj[:, t, col], gate[:, t, col], ALU.mult))
                        dve.tensor_tensor(self.X[:, t, col], self.X[:, t, col], gate[:, t, col], ALU.add)\
                            .then_inc(gated, 1)

                @block.sync
                def _(sp):
                    o = self.out[0].rearrange("(t p) c -> p t c", p=P)
                    for n, (t, col) in enumerate(halves):
                        sp.wait_ge(gated, n + 1)
                        sp.dma_start(o[:, t, col], self.X[:, t, col]).then_inc(stored, 16)
                    sp.wait_ge(stored, 16 * len(halves))

    def run(self):
        nc, a = self.nc, self.a
        w = lambda name: a[name][0]
        kview = lambda name: w(name).rearrange("(k p) n -> p k n", p=P)
        gate, up, down = kview("w_ffn_gate"), kview("w_ffn_up"), kview("w_ffn_down")
        uq, ukv = kview("w_uq_2"), kview("w_ukv_2")
        WI, WI2, WQ = 450, 352, 384
        s_in = Stream(wide(w("w_in"), WI), (8, WI), W_IN_COLS // (2 * WI))
        s_out = Stream(wide(w("w_out"), BANK), (8, BANK), 2)
        s_up = Stream(lambda i, j: (gate if j < 2 else up)[:, 8 * (j % 2):8 * (j % 2) + 8, bass.ds(i * BANK, BANK)],
                      (8, BANK), D_FF // BANK)
        s_down = Stream(lambda i, j: down[:, bass.ds(i * 8 + 2 * j, 2), :], (2, D), 6, last=2)
        s_in2 = Stream(wide(w("w_in_2"), WI2), (8, WI2), IN2_COLS // (2 * WI2))
        s_uq = Stream(lambda i, j: uq[:, :, j * WQ:(j + 1) * WQ], (4, WQ), 1)
        s_ukv = Stream(lambda i, j: ukv[:, :, j * BANK:(j + 1) * BANK], (4, BANK), 1)
        s_out2 = Stream(wide(w("w_out_2"), BANK), (8, BANK), 2)
        s_pq = Stream(wide(w("w_pq_2"), BANK), (8, BANK), 2)
        s_ple = Stream(wide(w("w_ple_gate_2"), BANK), (8, BANK), 2)
        X, to = self.X, self.scaled_to
        x = lambda t: X[:, t, :]
        chunk = lambda y: (lambda t, k: y[:, t, k * P:(k + 1) * P])

        self.setup(s_in)
        with ExitStack() as ctx:
            PR = ctx.enter_context(nc.sbuf_tensor("projections", [P, NT, W_IN_COLS], F32))
            self.cmp_w2 = ctx.enter_context(nc.sbuf_tensor("cmp_w2", [HD, 2, HD], F32))
            self.cmp_pos = ctx.enter_context(nc.sbuf_tensor("cmp_pos", [2 * CMP_LEN, 2, HD], F32))
            with ExitStack() as c2:
                hT = self.features(c2, KD)
                self.linear(s_in, s_out, hT, chunk(X), self.gains_of(G_MIX, KD), WI, to(PR, WI), ("act", "dve"), x,
                            self.nsa_inputs)
            with ExitStack() as c2:
                self.sgu_w = c2.enter_context(nc.sbuf_tensor("sgu_w", [P, NH, P], F32))
                self.nsa(PR)
                self.sticks_sgu(PR)
            hT = self.features(ctx, KD)
            offs = (0, B_OFF, C_OFF, D_OFF)
            self.norm_groups(lambda t, g: PR[:, t, offs[g]:offs[g] + BANK], 4, BANK)
            self.linear(s_out, s_up, hT, chunk(self.XN), self.gains_of(G_GROUP, KD), BANK, self.add_out, ("dve", "dve"))
        self.ffn((s_up, s_down), s_in2)
        with ExitStack() as ctx:
            Z = ctx.enter_context(nc.sbuf_tensor("projections2", [P, NT, IN2_COLS], F32))
            rope_inputs = self.rope_inputs(ctx)
            with ExitStack() as c2:
                hT = self.features(c2, KD)
                self.linear(s_in2, s_uq, hT, chunk(X), self.gains_of(G_MIX2, KD), WI2, to(Z, WI2), ("act", "dve"), x,
                            rope_inputs)
            pctx = ctx.enter_context(ExitStack())
            beside = self.pool_inputs(pctx)
            with ExitStack() as c2:
                Q = c2.enter_context(nc.sbuf_tensor("queries", [P, NT, NH * QKH], F32))
                KV = c2.enter_context(nc.sbuf_tensor("keys_values", [P, NT, D], F32))
                with ExitStack() as c3:
                    hT = self.features(c3, 4)
                    lat = Z[:, :, Q_OFF:KV_OFF]
                    self.linear(s_uq, s_ukv, hT, chunk(lat), self.gains_of(G_QLAT, 4), WQ, to(Q, WQ), ("act", "dve"),
                                lambda t: Z[:, t, Q_OFF:KV_OFF])
                    lat = Z[:, :, KV_OFF:ROPE_OFF]
                    self.linear(s_ukv, s_out2, hT, chunk(lat), self.gains_of(G_KVLAT, 4), BANK, to(KV, BANK), ("act", "dve"),
                                lambda t: Z[:, t, KV_OFF:ROPE_OFF])
                self.mla(Q[:, :, :], KV[:, :, :], Z[:, :, ROPE_OFF:IN2_COLS], Z, beside)
            self.pool_mix(Z)
            pctx.close()
            hT = self.features(ctx, KD)
            self.linear(s_out2, s_pq, hT, chunk(Z), self.gains_of(G_POOL, 8) + self.gains_of(None, 8), BANK,
                        self.add_out, ("dve", "dve"))
        self.peer(s_ple, s_pq)


_INS = ["x", "w_in", "w_out", "norm_mix", "norm_ffn", "q_gain", "k_gain", "cmp_pos", "cmp_w1", "cmp_w2", "rel_table",
        "conv_w", "sgu_w", "sgu_b", "group_gain", "w_ffn_gate", "w_ffn_up", "w_ffn_down", "p_2", "positions_2",
        "mix_norm_gain_2", "w_in_2", "w_pool_2", "pool_scale_2", "q_lat_gain_2", "kv_lat_gain_2", "w_uq_2", "w_ukv_2",
        "q_norm_gain_2", "k_norm_gain_2", "w_out_2", "ffn_norm_gain_2", "w_pq_2", "sub_k1_2", "sub_k2_2",
        "expert_u_2", "expert_v_2", "ple_norm_gain_2", "w_ple_gate_2", "w_ple_proj_2"]


def kernel(**inputs):
    import concourse.bacc as bacc
    from concourse.bass_utils import run_bass_kernel_spmd

    nc = bacc.Bacc("TRN2", target_bir_lowering=False, num_devices=1)
    arrays, args = {}, {}
    for name in _INS:
        v = np.ascontiguousarray(inputs[name])
        arrays["in_" + name] = v
        args[name] = nc.dram_tensor("in_" + name, v.shape, mybir.dt.from_np(v.dtype), kind="ExternalInput").ap()
    out = nc.dram_tensor("out", (1, T, D), F32, kind="ExternalOutput").ap()
    Kernel(nc, args, out).run()
    return run_bass_kernel_spmd(nc, [arrays], core_ids=[0]).results[0]["out"]
```
